# Optimizing a Trainium2 kernel written in Bass

```python
import math
import jax, jax.numpy as jnp
from jax import lax
import numpy as np

D_MODEL = 1024
BATCH = 1
SEQ = 512
DEPTH = 1
DEC_BATCH = 8
DEC_SEQ = 4
PAST_LEN = 2048
PAGE_SIZE = 128

DN_HEADS = 8
DN_HEAD_DIM = 128
DN_WIDTH = DN_HEADS * DN_HEAD_DIM
CONV_W = 4
DN_CONV_CH = 3 * DN_WIDTH
DN_CHUNK = 64
NSA_HEADS = 16
NSA_KV_HEADS = 2
NSA_GROUP = NSA_HEADS // NSA_KV_HEADS
NSA_HEAD_DIM = 64
NSA_WIDTH = NSA_HEADS * NSA_HEAD_DIM
NSA_KV_WIDTH = NSA_KV_HEADS * NSA_HEAD_DIM
CMP_BLOCK = 32
CMP_STRIDE = 16
CMP_RATIO = CMP_BLOCK // CMP_STRIDE
SLC_BLOCK = 64
N_SELECT = 16
WINDOW = 512
Q_BLOCK = 64
N_EXPERTS = 64
TOP_K = 6
N_GROUPS = 8
TOPK_GROUPS = 4
D_EXPERT = 256
D_SHARED = 256
ROUTED_SCALE = 2.5
MOE_BLOCK = 128
D_IN_PROJ = 4 * DN_WIDTH + 2 * DN_HEADS + NSA_WIDTH + 6 * NSA_KV_WIDTH + 3 * NSA_HEADS + 2 * D_MODEL
DEEPNORM_ALPHA = (2.0 * DEPTH) ** 0.25
DEEPNORM_BETA = (8.0 * DEPTH) ** -0.25
LN_EPS = 1e-5
RMS_EPS = 1e-6
NEG = -1e30
FORCE_BONUS = 1e6
F32 = jnp.float32

kernel_name = 'hybrid_gdn_nsa_moe_deepnorm_step'

def _layer_norm(x, g, b):
    xf = x.astype(F32)
    xc = xf - jnp.mean(xf, -1, keepdims=True)
    var = jnp.mean(xc * xc, -1, keepdims=True)
    return (xc * lax.rsqrt(var + LN_EPS) * g.astype(F32) + b.astype(F32)).astype(x.dtype)

def _l2norm(x):
    return x * lax.rsqrt(jnp.sum(x * x, -1, keepdims=True) + 1e-6)

def _masked_softmax(s, valid, axis):
    s = jnp.where(valid, s, NEG)
    m = jnp.max(s, axis=axis, keepdims=True)
    p = jnp.where(valid, jnp.exp(s - m), 0.0)
    return p / jnp.maximum(jnp.sum(p, axis=axis, keepdims=True), 1e-30)

def _alibi_slopes():
    return 2.0 ** (-8.0 * jnp.arange(1, NSA_HEADS + 1, dtype=F32) / NSA_HEADS)

def _split_proj(p):
    sizes = (3 * DN_WIDTH, DN_WIDTH, DN_HEADS, DN_HEADS, NSA_WIDTH,
             2 * NSA_KV_WIDTH, 2 * NSA_KV_WIDTH, 2 * NSA_KV_WIDTH, 3 * NSA_HEADS, 2 * D_MODEL)
    return jnp.split(p, np.cumsum(sizes)[:-1].tolist(), axis=-1)

def _to_kv(t):
    return t.reshape(t.shape[:2] + (2, NSA_KV_HEADS, NSA_HEAD_DIM))

def _causal_conv(x, buf, w):
    T = x.shape[1]
    xp = jnp.concatenate([buf.astype(x.dtype), x], axis=1)
    y = xp[:, 0:T] * w[0]
    for j in range(1, CONV_W):
        y = y + xp[:, j:j + T] * w[j]
    return jax.nn.silu(y), xp[:, -(CONV_W - 1):]

def _gated_delta_chunked(q, k, v, g, beta, S0):
    Bsz, T, H, _ = q.shape
    dv = v.shape[-1]
    C = DN_CHUNK
    n = -(-T // C)
    pad = n * C - T

    def prep(x):
        x = jnp.pad(x, [(0, 0), (0, pad)] + [(0, 0)] * (x.ndim - 2))
        x = x.reshape((Bsz, n, C) + x.shape[2:])
        return jnp.moveaxis(jnp.moveaxis(x, 1, 0), 2, 3)

    qc, kc, vc, gc, bc = prep(q), prep(k), prep(v), prep(g), prep(beta)
    gcum = jnp.cumsum(gc, axis=-1)
    idx = jnp.arange(C)
    incl = idx[:, None] >= idx[None, :]
    strict = idx[:, None] > idx[None, :]
    diff = gcum[..., :, None] - gcum[..., None, :]
    decay = jnp.where(incl, jnp.exp(jnp.where(incl, diff, 0.0)), 0.0)
    kb = kc * bc[..., None]
    vb = vc * bc[..., None]
    Lm = jnp.where(strict, jnp.einsum('nbhid,nbhjd->nbhij', kb, kc) * decay, 0.0)
    eye = jnp.broadcast_to(jnp.eye(C, dtype=F32), Lm.shape)
    Tm = lax.linalg.triangular_solve(Lm, eye, left_side=True, lower=True, unit_diagonal=True)
    u = jnp.einsum('nbhij,nbhjd->nbhid', Tm, vb)
    w = jnp.einsum('nbhij,nbhjd->nbhid', Tm, kb * jnp.exp(gcum)[..., None])
    A = jnp.where(incl, jnp.einsum('nbhid,nbhjd->nbhij', qc, kc) * decay, 0.0)

    def step(S, xs):
        q_i, k_i, u_i, w_i, A_i, g_i = xs
        v_new = u_i - jnp.einsum('bhcd,bhde->bhce', w_i, S)
        o_i = (jnp.einsum('bhcd,bhde->bhce', q_i * jnp.exp(g_i)[..., None], S)
               + jnp.einsum('bhij,bhje->bhie', A_i, v_new))
        g_last = g_i[..., -1]
        S = (S * jnp.exp(g_last)[..., None, None]
             + jnp.einsum('bhcd,bhce->bhde', k_i * jnp.exp(g_last[..., None] - g_i)[..., None], v_new))
        return S, o_i

    S_final, o = lax.scan(step, S0, (qc, kc, u, w, A, gcum))
    o = jnp.swapaxes(jnp.moveaxis(o, 0, 1), 2, 3).reshape(Bsz, n * C, H, dv)[:, :T]
    return o, S_final

def _deltanet_mixer(qkv_raw, z, a, b, conv_buf, S0, conv_w, A_log, dt_bias, norm_w):
    Bsz, T, _ = qkv_raw.shape
    qkv, conv_new = _causal_conv(qkv_raw, conv_buf, conv_w)
    qkv = qkv.astype(F32).reshape(Bsz, T, 3, DN_HEADS, DN_HEAD_DIM)
    q = _l2norm(qkv[:, :, 0]) * DN_HEAD_DIM ** -0.5
    k = _l2norm(qkv[:, :, 1])
    v = qkv[:, :, 2]
    beta = jax.nn.sigmoid(b.astype(F32))
    g = -jnp.exp(A_log.astype(F32)) * jax.nn.softplus(a.astype(F32) + dt_bias.astype(F32))
    o, S_new = _gated_delta_chunked(q, k, v, g, beta, S0.astype(F32))
    o = o * lax.rsqrt(jnp.mean(o * o, -1, keepdims=True) + RMS_EPS) * norm_w.astype(F32)
    o = o * jax.nn.silu(z.astype(F32).reshape(Bsz, T, DN_HEADS, DN_HEAD_DIM))
    return o.reshape(Bsz, T, DN_WIDTH), S_new.astype(S0.dtype), conv_new

def _nsa_compress(kv, w1, pos, w2):
    Bsz, L = kv.shape[:2]
    n_sub = L // CMP_STRIDE
    nc = n_sub - CMP_RATIO + 1
    sub = kv[:, :n_sub * CMP_STRIDE].reshape(Bsz, n_sub, CMP_STRIDE, 2, NSA_KV_HEADS, NSA_HEAD_DIM)
    w1r = w1.reshape(2, CMP_RATIO, CMP_STRIDE, NSA_HEAD_DIM, NSA_HEAD_DIM)
    proj = jnp.einsum('bnpshd,srpde->bnshre', sub.astype(F32), w1r.astype(F32))
    bias = jnp.einsum('sf,sfe->se', pos.reshape(2, -1).astype(F32), w1.astype(F32))
    h = bias[None, None, :, None, :]
    for r in range(CMP_RATIO):
        h = h + proj[:, r:r + nc, :, :, r]
    out = jnp.einsum('bnshe,sef->bnshf', jax.nn.gelu(h), w2.astype(F32))
    return out[:, :, 0], out[:, :, 1]

def _nsa_core(q, q_pos, k_c, v_c, gather_slc, n_slc, k_w, v_w, w_pos, gates):
    Bsz, Tq = q.shape[:2]
    qf = q.astype(F32).reshape(Bsz, Tq, NSA_KV_HEADS, NSA_GROUP, NSA_HEAD_DIM) * NSA_HEAD_DIM ** -0.5
    slopes = _alibi_slopes().reshape(NSA_KV_HEADS, NSA_GROUP)[None, :, :, None, None]
    tq = q_pos.astype(F32)
    n_cmp = k_c.shape[1]
    c_start = jnp.arange(n_cmp) * CMP_STRIDE
    c_end = c_start + CMP_BLOCK - 1
    s_c = jnp.einsum('bqhgd,bchd->bhgqc', qf, k_c) - slopes * (tq[:, None] - c_end.astype(F32)[None, :])
    p_c = _masked_softmax(s_c, c_end[None, :] <= q_pos[:, None], -1)
    o_c = jnp.einsum('bhgqc,bchd->bqhgd', p_c, v_c)
    s_start = jnp.arange(n_slc) * SLC_BLOCK
    cover = ((c_start[:, None] < s_start[None, :] + SLC_BLOCK) & (c_end[:, None] >= s_start[None, :])).astype(F32)
    imp = jnp.einsum('bhgqc,cs->bhqs', p_c, cover)
    cur = q_pos // SLC_BLOCK
    blk = jnp.arange(n_slc)
    forced = (blk[None, :] == 0) | (blk[None, :] == cur[:, None]) | (blk[None, :] == cur[:, None] - 1)
    score = jnp.where(s_start[None, :] <= q_pos[:, None], imp + jnp.where(forced, FORCE_BONUS, 0.0), NEG)
    _, sel = lax.top_k(score, min(N_SELECT, n_slc))
    kv_s = gather_slc(sel).astype(F32)
    pos_s = sel[..., None] * SLC_BLOCK + jnp.arange(SLC_BLOCK)
    dist_s = (tq[None, None, :, None, None] - pos_s.astype(F32))[:, :, None]
    s_s = jnp.einsum('bqhgd,bhqnkd->bhgqnk', qf, kv_s[..., 0, :]) - slopes[..., None] * dist_s
    p_s = _masked_softmax(s_s, dist_s >= 0, (-2, -1))
    o_s = jnp.einsum('bhgqnk,bhqnkd->bqhgd', p_s, kv_s[..., 1, :])
    dist_w = q_pos[:, None] - w_pos[None, :]
    valid_w = (dist_w >= 0) & (dist_w < WINDOW) & (w_pos[None, :] >= 0)
    s_w = jnp.einsum('bqhgd,bwhd->bhgqw', qf, k_w.astype(F32)) - slopes * dist_w.astype(F32)
    p_w = _masked_softmax(s_w, valid_w, -1)
    o_w = jnp.einsum('bhgqw,bwhd->bqhgd', p_w, v_w.astype(F32))
    gt = jax.nn.sigmoid(gates.astype(F32)).reshape(Bsz, Tq, NSA_KV_HEADS, NSA_GROUP, 3)
    o = gt[..., 0:1] * o_c + gt[..., 1:2] * o_s + gt[..., 2:3] * o_w
    return o.reshape(Bsz, Tq, NSA_WIDTH)

def _merge_branches(o_dn, o_nsa, mg):
    g_dn, g_nsa = jnp.split(jax.nn.sigmoid(mg.astype(F32)), 2, axis=-1)
    return (g_dn * o_dn.astype(F32) + g_nsa * o_nsa.astype(F32)).astype(mg.dtype)

def _mixer_prompt(x, w_in, conv_w, A_log, dt_bias, norm_w, cmp_w1, cmp_pos, cmp_w2):
    Bsz, T, _ = x.shape
    qkv, z, a, b, nq, kvc, kvs, kvw, ng, mg = _split_proj(x @ w_in)
    conv0 = jnp.zeros((Bsz, CONV_W - 1, DN_CONV_CH), x.dtype)
    S0 = jnp.zeros((Bsz, DN_HEADS, DN_HEAD_DIM, DN_HEAD_DIM), F32)
    o_dn, S_new, conv_new = _deltanet_mixer(qkv, z, a, b, conv0, S0, conv_w, A_log, dt_bias, norm_w)
    kvc, kvs, kvw = _to_kv(kvc), _to_kv(kvs), _to_kv(kvw)
    k_c, v_c = _nsa_compress(kvc, cmp_w1, cmp_pos, cmp_w2)
    n_slc = -(-T // SLC_BLOCK)
    blocks = jnp.pad(kvs, ((0, 0), (0, n_slc * SLC_BLOCK - T), (0, 0), (0, 0), (0, 0)))
    blocks = blocks.reshape(Bsz, n_slc, SLC_BLOCK, 2, NSA_KV_HEADS, NSA_HEAD_DIM)
    bi = jnp.arange(Bsz)[:, None, None, None]
    hi = jnp.arange(NSA_KV_HEADS)[None, :, None, None]

    def gather_slc(sel):
        return blocks[bi, sel, :, :, hi]

    kvw_pad = jnp.pad(kvw, ((0, 0), (WINDOW, 0), (0, 0), (0, 0), (0, 0)))
    q = nq.reshape(Bsz, T, NSA_HEADS, NSA_HEAD_DIM)
    gates = ng.reshape(Bsz, T, NSA_HEADS, 3)

    def one_block(j):
        q0 = j * Q_BLOCK
        qb = lax.dynamic_slice_in_dim(q, q0, Q_BLOCK, axis=1)
        gb = lax.dynamic_slice_in_dim(gates, q0, Q_BLOCK, axis=1)
        wb = lax.dynamic_slice_in_dim(kvw_pad, q0, WINDOW + Q_BLOCK, axis=1)
        q_pos = q0 + jnp.arange(Q_BLOCK)
        w_pos = q0 - WINDOW + jnp.arange(WINDOW + Q_BLOCK)
        return _nsa_core(qb, q_pos, k_c, v_c, gather_slc, n_slc, wb[:, :, 0], wb[:, :, 1], w_pos, gb)

    o_nsa = lax.map(one_block, jnp.arange(T // Q_BLOCK))
    o_nsa = jnp.moveaxis(o_nsa, 0, 1).reshape(Bsz, T, NSA_WIDTH)
    h = _merge_branches(o_dn, o_nsa, mg)
    return h, (kvc, kvs, kvw[:, -min(WINDOW, T):], S_new, conv_new)

def _paged_block_gather(cache_slc_kv, l, page_table, kv_new):
    Bsz, T = kv_new.shape[:2]
    bpp = PAGE_SIZE // SLC_BLOCK
    n_past_blocks = page_table.shape[1] * bpp
    pool = cache_slc_kv.reshape(cache_slc_kv.shape[:2] + (bpp, SLC_BLOCK) + cache_slc_kv.shape[3:])
    n_tail = -(-T // SLC_BLOCK)
    tail = jnp.pad(kv_new, ((0, 0), (0, n_tail * SLC_BLOCK - T), (0, 0), (0, 0), (0, 0)))
    tail = tail.reshape(Bsz, n_tail, SLC_BLOCK, 2, NSA_KV_HEADS, NSA_HEAD_DIM)
    bi = jnp.arange(Bsz)[:, None, None, None]
    hi = jnp.arange(NSA_KV_HEADS)[None, :, None, None]

    def gather(sel):
        jp = jnp.minimum(sel, n_past_blocks - 1)
        phys = page_table[bi, jp // bpp]
        from_pool = pool[l, phys, jp % bpp, :, :, hi]
        jt = jnp.clip(sel - n_past_blocks, 0, n_tail - 1)
        from_tail = tail[bi, jt, :, :, hi]
        return jnp.where((sel < n_past_blocks)[..., None, None, None], from_pool, from_tail)

    return gather, n_past_blocks + n_tail

def _mixer_sample(x, l, cache_cmp_kv, cache_slc_kv, win_buf, S0, conv_buf, page_table,
                  w_in, conv_w, A_log, dt_bias, norm_w, cmp_w1, cmp_pos, cmp_w2):
    Bsz, T, _ = x.shape
    past = page_table.shape[1] * PAGE_SIZE
    qkv, z, a, b, nq, kvc, kvs, kvw, ng, mg = _split_proj(x @ w_in)
    o_dn, S_new, conv_new = _deltanet_mixer(qkv, z, a, b, conv_buf, S0, conv_w, A_log, dt_bias, norm_w)
    kvc, kvs, kvw = _to_kv(kvc), _to_kv(kvs), _to_kv(kvw)
    cmp_past = cache_cmp_kv[l, page_table].reshape((Bsz, past) + kvc.shape[2:])
    k_c, v_c = _nsa_compress(jnp.concatenate([cmp_past.astype(kvc.dtype), kvc], axis=1), cmp_w1, cmp_pos, cmp_w2)
    gather_slc, n_slc = _paged_block_gather(cache_slc_kv, l, page_table, kvs)
    kvw_all = jnp.concatenate([win_buf.astype(kvw.dtype), kvw], axis=1)
    w_pos = past - win_buf.shape[1] + jnp.arange(kvw_all.shape[1])
    q_pos = past + jnp.arange(T)
    o_nsa = _nsa_core(nq.reshape(Bsz, T, NSA_HEADS, NSA_HEAD_DIM), q_pos, k_c, v_c, gather_slc, n_slc,
                      kvw_all[:, :, 0], kvw_all[:, :, 1], w_pos, ng.reshape(Bsz, T, NSA_HEADS, 3))
    h = _merge_branches(o_dn, o_nsa, mg)
    return h, (kvc, kvs, kvw_all[:, -min(WINDOW, past + T):], S_new, conv_new)

def _moe_ffn(x, w_router, b_router, w_gate, w_up, w_down, ws_gate, ws_up, ws_down):
    shp = x.shape
    xt = x.reshape(-1, D_MODEL)
    T = xt.shape[0]
    scores = jax.nn.sigmoid(jnp.einsum('td,de->te', xt.astype(F32), w_router.astype(F32)))
    sel = scores + b_router.astype(F32)
    grp_score = jnp.sum(lax.top_k(sel.reshape(T, N_GROUPS, N_EXPERTS // N_GROUPS), 2)[0], -1)
    _, top_g = lax.top_k(grp_score, TOPK_GROUPS)
    gmask = jnp.any(top_g[..., None] == jnp.arange(N_GROUPS), axis=1)
    sel = jnp.where(jnp.repeat(gmask, N_EXPERTS // N_GROUPS, axis=1), sel, NEG)
    _, idx = lax.top_k(sel, TOP_K)
    wts = jnp.take_along_axis(scores, idx, axis=1)
    wts = wts / jnp.sum(wts, -1, keepdims=True) * ROUTED_SCALE
    flat_e = idx.reshape(-1)
    order = jnp.argsort(flat_e)
    e_sorted = flat_e[order]
    counts = jnp.bincount(flat_e, length=N_EXPERTS)
    padded = (counts + MOE_BLOCK - 1) // MOE_BLOCK * MOE_BLOCK
    pad_end = jnp.cumsum(padded)
    pad_start = pad_end - padded
    start = jnp.cumsum(counts) - counts
    slot = pad_start[e_sorted] + jnp.arange(T * TOP_K) - start[e_sorted]
    n_blocks = -(-(T * TOP_K) // MOE_BLOCK) + N_EXPERTS
    slot_tok = jnp.full((n_blocks * MOE_BLOCK,), T, jnp.int32).at[slot].set((order // TOP_K).astype(jnp.int32))
    slot_w = jnp.zeros((n_blocks * MOE_BLOCK,), F32).at[slot].set(wts.reshape(-1)[order])
    blk_exp = jnp.minimum(jnp.sum(pad_end[None, :] <= (jnp.arange(n_blocks) * MOE_BLOCK)[:, None], axis=1),
                          N_EXPERTS - 1)
    x_pad = jnp.concatenate([xt, jnp.zeros((1, D_MODEL), xt.dtype)], axis=0)

    def expert_block(args):
        tok, e = args
        xb = x_pad[tok]
        hb = jax.nn.silu(xb @ w_gate[e]) * (xb @ w_up[e])
        return hb @ w_down[e]

    y_slots = lax.map(expert_block, (slot_tok.reshape(n_blocks, MOE_BLOCK), blk_exp)).reshape(-1, D_MODEL)
    routed = jax.ops.segment_sum(y_slots.astype(F32) * slot_w[:, None], slot_tok, num_segments=T + 1)[:T]
    shared = ((jax.nn.silu(xt @ ws_gate) * (xt @ ws_up)) @ ws_down).astype(F32)
    return (routed + shared).astype(x.dtype).reshape(shp)

def setup_inputs(seed: int = 0) -> dict:
    key = jax.random.key(seed)
    ks = jax.random.split(key, 32)
    n_pages = PAST_LEN // PAGE_SIZE
    n_pool = (5 * DEC_BATCH * n_pages + 3) // 4
    win_buf = min(WINDOW, PAST_LEN)
    kvs = (2, NSA_KV_HEADS, NSA_HEAD_DIM)

    def nrm(k, shape, scale):
        return scale * jax.random.normal(k, shape, F32)

    page_table = jax.random.permutation(ks[7], n_pool)[:DEC_BATCH * n_pages]
    page_table = page_table.reshape(DEC_BATCH, n_pages).astype(jnp.int32)
    dt = jnp.exp(jax.random.uniform(ks[10], (DEPTH, DN_HEADS), F32, math.log(1e-3), math.log(1e-1)))
    return {
        'x_prompt': nrm(ks[0], (BATCH, SEQ, D_MODEL), 1.0),
        'x_sample': nrm(ks[1], (DEC_BATCH, DEC_SEQ, D_MODEL), 1.0),
        'cache_cmp_kv': nrm(ks[2], (DEPTH, n_pool, PAGE_SIZE) + kvs, 1.0),
        'cache_slc_kv': nrm(ks[3], (DEPTH, n_pool, PAGE_SIZE) + kvs, 1.0),
        'cache_win_kv': nrm(ks[4], (DEPTH, DEC_BATCH, win_buf) + kvs, 1.0),
        'state_delta_S': nrm(ks[5], (DEPTH, DEC_BATCH, DN_HEADS, DN_HEAD_DIM, DN_HEAD_DIM), DN_HEAD_DIM ** -0.5),
        'state_delta_conv': nrm(ks[6], (DEPTH, DEC_BATCH, CONV_W - 1, DN_CONV_CH), 1.0),
        'page_table': page_table,
        'w_in': nrm(ks[8], (DEPTH, D_MODEL, D_IN_PROJ), D_MODEL ** -0.5),
        'dn_conv_w': nrm(ks[9], (DEPTH, CONV_W, DN_CONV_CH), CONV_W ** -0.5),
        'dn_A_log': jnp.log(jax.random.uniform(ks[11], (DEPTH, DN_HEADS), F32, 1.0, 16.0)),
        'dn_dt_bias': dt + jnp.log(-jnp.expm1(-dt)),
        'dn_norm_w': 1.0 + nrm(ks[12], (DEPTH, DN_HEAD_DIM), 0.1),
        'nsa_cmp_w1': nrm(ks[13], (DEPTH, 2, CMP_BLOCK * NSA_HEAD_DIM, NSA_HEAD_DIM), (CMP_BLOCK * NSA_HEAD_DIM) ** -0.5),
        'nsa_cmp_pos': nrm(ks[14], (DEPTH, 2, CMP_BLOCK, NSA_HEAD_DIM), 0.1),
        'nsa_cmp_w2': nrm(ks[15], (DEPTH, 2, NSA_HEAD_DIM, NSA_HEAD_DIM), NSA_HEAD_DIM ** -0.5),
        'w_out': nrm(ks[16], (DEPTH, D_MODEL, D_MODEL), D_MODEL ** -0.5 * DEEPNORM_BETA),
        'ln1_g': 1.0 + nrm(ks[17], (DEPTH, D_MODEL), 0.1),
        'ln1_b': nrm(ks[18], (DEPTH, D_MODEL), 0.02),
        'w_router': nrm(ks[19], (DEPTH, D_MODEL, N_EXPERTS), D_MODEL ** -0.5),
        'b_router': nrm(ks[20], (DEPTH, N_EXPERTS), 0.01),
        'w_exp_gate': nrm(ks[21], (DEPTH, N_EXPERTS, D_MODEL, D_EXPERT), D_MODEL ** -0.5),
        'w_exp_up': nrm(ks[22], (DEPTH, N_EXPERTS, D_MODEL, D_EXPERT), D_MODEL ** -0.5),
        'w_exp_down': nrm(ks[23], (DEPTH, N_EXPERTS, D_EXPERT, D_MODEL), D_EXPERT ** -0.5 * DEEPNORM_BETA),
        'w_sh_gate': nrm(ks[24], (DEPTH, D_MODEL, D_SHARED), D_MODEL ** -0.5),
        'w_sh_up': nrm(ks[25], (DEPTH, D_MODEL, D_SHARED), D_MODEL ** -0.5),
        'w_sh_down': nrm(ks[26], (DEPTH, D_SHARED, D_MODEL), D_SHARED ** -0.5 * DEEPNORM_BETA),
        'ln2_g': 1.0 + nrm(ks[27], (DEPTH, D_MODEL), 0.1),
        'ln2_b': nrm(ks[28], (DEPTH, D_MODEL), 0.02),
    }

def reference(x_prompt, x_sample, cache_cmp_kv, cache_slc_kv, cache_win_kv, state_delta_S, state_delta_conv,
              page_table, w_in, dn_conv_w, dn_A_log, dn_dt_bias, dn_norm_w, nsa_cmp_w1, nsa_cmp_pos, nsa_cmp_w2,
              w_out, ln1_g, ln1_b, w_router, b_router, w_exp_gate, w_exp_up, w_exp_down,
              w_sh_gate, w_sh_up, w_sh_down, ln2_g, ln2_b):
    xp, xs = x_prompt, x_sample
    st_p = ([], [], [], [], [])
    st_s = ([], [], [], [], [])
    for l in range(DEPTH):
        mix_w = (w_in[l], dn_conv_w[l], dn_A_log[l], dn_dt_bias[l], dn_norm_w[l],
                 nsa_cmp_w1[l], nsa_cmp_pos[l], nsa_cmp_w2[l])
        moe_w = (w_router[l], b_router[l], w_exp_gate[l], w_exp_up[l], w_exp_down[l],
                 w_sh_gate[l], w_sh_up[l], w_sh_down[l])
        hp, new_p = _mixer_prompt(xp, *mix_w)
        hs, new_s = _mixer_sample(xs, l, cache_cmp_kv, cache_slc_kv, cache_win_kv[l], state_delta_S[l],
                                  state_delta_conv[l], page_table, *mix_w)
        xp = _layer_norm(DEEPNORM_ALPHA * xp + hp @ w_out[l], ln1_g[l], ln1_b[l])
        xs = _layer_norm(DEEPNORM_ALPHA * xs + hs @ w_out[l], ln1_g[l], ln1_b[l])
        xp = _layer_norm(DEEPNORM_ALPHA * xp + _moe_ffn(xp, *moe_w), ln2_g[l], ln2_b[l])
        xs = _layer_norm(DEEPNORM_ALPHA * xs + _moe_ffn(xs, *moe_w), ln2_g[l], ln2_b[l])
        for acc, t in zip(st_p, new_p):
            acc.append(t)
        for acc, t in zip(st_s, new_s):
            acc.append(t)
    cmp_kv_p, slc_kv_p, win_kv_p, delta_S_p, delta_conv_p = [jnp.stack(a) for a in st_p]
    cmp_kv_s, slc_kv_s, win_kv_s, delta_S_s, delta_conv_s = [jnp.stack(a) for a in st_s]
    return (xp, xs, cmp_kv_p, slc_kv_p, win_kv_p, delta_S_p, delta_conv_p,
            cmp_kv_s, slc_kv_s, win_kv_s, delta_S_s, delta_conv_s)


_drawn_inputs = setup_inputs


def setup_inputs(seed=0):
    import zlib

    import numpy as np

    out = dict(_drawn_inputs(seed))
    spreads = {}
    factors = {'ln2_b': 2.749}
    for name, (base, spread) in spreads.items():
        noise = np.random.default_rng([zlib.crc32(name.encode()), seed]).standard_normal(out[name].shape)
        drawn = base * np.exp(spread * noise) if base else spread * noise
        out[name] = __import__('jax').numpy.asarray(drawn.astype(out[name].dtype))
    for name, factor in factors.items():
        out[name] = (out[name] * factor).astype(out[name].dtype)
    return out
```

```python
from contextlib import ExitStack

import numpy as np
import concourse.bass as bass
from concourse import mybir

D = 1024
NP_TOK = 512
NB, NT = 8, 4
NS_TOK = NB * NT
NTOK = NP_TOK + NS_TOK
PAST, PAGE, NPOOL = 2048, 128, 160
NPG = PAST // PAGE
H, DH = 8, 128
CH = 3 * H * DH
QH, KVH, G, HD = 16, 2, 8, 64
WIN = 512
NE, DE = 64, 256
ALPHA = 2.0 ** 0.25
NEG = -1e30
P = 128
KD = D // P
NTILE = 5
HALF = NTOK // 2
C = 128
NCH = NP_TOK // C
LEVELS = 7
RAWW = 3 + NP_TOK + NB * 7
SROW = 3 + NP_TOK
NCMP_P = 31
NCMP_S = 127
NBLK = 33
TOP_K = 6
ROUTED_SCALE = 2.5
ARENA = 37400
RING = 6
COL_QKV, COL_Z, COL_AB, COL_NQ, COL_KV, COL_NG, COL_MG = 0, 3072, 4096, 4112, 5136, 5904, 5952
KVW = COL_MG - COL_KV


def shape_constants():
    f = np.float32
    i = np.arange(P)
    c = {}
    c["ident"] = np.eye(P, dtype=f)
    c["tri"] = (i[:, None] <= i[None, :]).astype(f)
    s = np.arange(NS_TOK)
    same = (s[:, None] // NT) == (s[None, :] // NT)
    c["tri_s"] = (same & (s[:, None] <= s[None, :])).astype(f)
    c["same_s"] = same.astype(f)
    c["causal_t"] = np.where(i[:, None] <= i[None, :], 0, NEG).astype(f)
    c["causal_ts"] = np.where(same & (s[:, None] <= s[None, :]), 0, NEG).astype(f)
    lev = []
    for n in range(LEVELS):
        w = 1 << n
        m = (i[:, None] // (2 * w) == i[None, :] // (2 * w)) & (i[:, None] % (2 * w) >= w) & (i[None, :] % (2 * w) < w)
        lev.append(m.T.astype(f))
    c["levels"] = np.stack(lev, 1).reshape(P, LEVELS * P)
    c["rows_s"] = (s[:, None] // NT == np.arange(NB)[None, :]).astype(f)
    slope = (2.0 ** (-8.0 * np.arange(1, QH + 1, dtype=f) / QH)).astype(f)
    m = np.arange(NP_TOK)
    dist = i[:, None] - (m[None, :] - 384)
    c["dist"] = np.where(dist >= 0, dist, 1e32).astype(f)
    tq = np.arange(NP_TOK).reshape(4, P)
    c_end = np.arange(NCMP_S) * 16 + 31
    ok = c_end[None, None, :NCMP_P] <= tq[:, :, None]
    bias = -slope[None, None, :, None] * (tq[:, :, None, None] - c_end[None, None, None, :NCMP_P]).astype(f)
    bias = np.where(ok[:, :, None, :], bias, NEG)
    c["cmp_bias"] = bias.transpose(1, 0, 2, 3).reshape(P, 4 * QH * NCMP_P).astype(f)
    c["cmp_any"] = ok.any(-1).T.astype(f)
    row = np.arange(P)
    rb, rh, rt, rg = row // 64, row // 32 % 2, row // 8 % 4, row % 8
    rs, rq = slope[rh * 8 + rg][:, None], (PAST + rt)[:, None]
    c["cmp_bias_s"] = (-rs * (rq - c_end[None, :]).astype(f)).astype(f)
    key = np.arange(PAST)
    c["slc_bias_s"] = (-rs * (rq - key[None, :]).astype(f)).astype(f)
    wk = PAST - WIN + np.arange(WIN)
    c["win_bias_s"] = np.where(rq - wk[None, :] < WIN, -rs * (rq - wk[None, :]).astype(f), NEG).astype(f)
    nk = np.arange(NS_TOK)
    new = []
    for pair in range(4):
        mine = (nk[None, :] // NT == 2 * pair + rb[:, None]) & (nk[None, :] % NT <= rt[:, None])
        new.append(np.where(mine, -rs * (rt[:, None] - nk[None, :] % NT).astype(f), NEG))
    c["new_bias_s"] = np.stack(new, 1).reshape(P, 4 * NS_TOK).astype(f)
    blk = np.arange(NBLK)
    c["cover"] = ((c_end[:, None] - 31 < blk[None, :] * 64 + 64) & (c_end[:, None] >= blk[None, :] * 64)).astype(f)
    c["forced"] = np.broadcast_to(np.where((blk == 0) | (blk >= NBLK - 2), 1e6, 0.0), (P, NBLK)).astype(f)
    c["group"] = (row[:, None] // 8 == row[None, :] // 8).astype(f)
    c["kv_rows"] = np.stack([rh == 0, rh == 1], 1).astype(f)
    gi = np.arange(8)
    c["before8"] = np.broadcast_to((gi[None, :] < gi[:, None]).reshape(1, 64), (P, 64)).astype(f)
    return c


SLOPES = [2.0 ** (-(j + 1) / 2.0) for j in range(QH)]


def build(nc, io):
    fp32 = mybir.dt.float32
    ALU = mybir.AluOpType
    ACT = mybir.ActivationFunctionType
    AX = mybir.AxisListType
    ctx = ExitStack()
    with ctx:
        def sb(name, shape, dt=fp32):
            return ctx.enter_context(nc.sbuf_tensor(name, shape, dt))

        def sem(name):
            taken.append(nc.alloc_semaphore(name=f"{name}_{stage[0]}"))
            return taken[-1]

        taken, stage = [], [0]

        def end_block():
            nc.clear_and_free_semaphores(list(taken))
            nc.all_engine_barrier()
            taken.clear()
            stage[0] += 1

        def width(shape):
            n = 1
            for k in shape:
                n *= k
            return n

        def shaped(ap, shape):
            if len(shape) == 2:
                return ap.rearrange("p (a b) -> p a b", a=shape[0])
            if len(shape) == 3:
                return ap.rearrange("p (a b c) -> p a b c", a=shape[0], b=shape[1])
            return ap

        xT = sb("xT", [P, KD, NTOK])
        hT = sb("hT", [P, KD, NTOK])
        kvt = sb("kvt", [P, NTILE, KVW])
        ident = sb("ident", [P, P])
        ones = sb("ones", [P, P])
        tri = sb("tri", [P, P])
        tri_s = sb("tri_s", [NS_TOK, NS_TOK])
        same_s = sb("same_s", [NS_TOK, NS_TOK])
        causal_t = sb("causal_t", [P, P])
        causal_ts = sb("causal_ts", [NS_TOK, NS_TOK])
        rows_s = sb("rows_s", [NS_TOK, NB])
        ab = sb("ab", [P, NTILE, 16])
        eps = sb("eps", [P, 2])
        arena = sb("arena", [P, ARENA])
        banks = [ctx.enter_context(nc.psum_tensor(f"bank{i}", [P, 512], fp32)) for i in range(8)]

        class Carve:
            def __init__(self):
                self.at = 0

            def __call__(self, *shape):
                n = width(shape)
                ap = arena[:, self.at:self.at + n]
                self.at += n
                assert self.at <= ARENA, self.at
                return shaped(ap, shape)

        a = Carve()
        xrow = a(NTILE, D)
        wkv = a(KD, KVW + 16)
        b = Carve()
        b.at = ARENA - RING * D
        wh = [b(KD, P) for _ in range(RING)]
        b.at = 0
        levels = b(LEVELS, P)
        raw = [b(3, RAWW), b(3, RAWW)]
        zm = [b(2, NTOK), b(2, NTOK)]
        convw = b(96)
        conv_rows = [b(3, P), b(3, P)]
        conv_out = [b(3, P), b(3, P)]
        normw = b(1)
        y = b(3, RAWW - 3)
        ey = b(3, RAWW - 3)
        act = b(3, NTOK)
        sq = b(2, NTOK)
        rn = b(2, NTOK)
        gb = b(2, NTILE, P)
        kbT = b(NTOK)
        eg = b(NTOK)
        qgT = b(NTOK)
        dec = b(NTILE, P)
        kbg = b(NTILE, P)
        kdec = b(NTILE, P)
        kdec8 = b(NB, P)
        vb = b(NTILE, P)
        LT = b(NTILE, P)
        AT = b(NTILE, P)
        MT = b(NCH, P)
        T = b(NTILE, P)
        U = b(NTILE, P)
        Y = b(NTILE, P)
        nwT = b(NCH, P)
        nw8 = b(NB * 36)
        vn = b(NTILE, P)
        S = [b(P), b(P)]
        Sb = b(NB, P)
        Sn = b(NB, P)
        oT = b(NTOK)
        sgz = b(2, NTOK)
        cg = b(3, 27)
        assert b.at <= ARENA - RING * D, b.at
        q = Carve()
        qT = q(8, NTOK)
        mgB = q(8, NTOK)
        otok = q(NTILE, D)
        gt = q(NTILE, QH * 3)
        kcT_s = q(NB, NCMP_S)
        vc_s = q(NB, P)
        kcT_p = q(2, 32)
        vc_p = q(P)
        knT = q(2, NS_TOK)
        QD = q(NB, 64)
        small = q(64)
        keep = q.at
        W1 = q(2, 32, P)
        pages = q(8, 256)
        kvT = q(2, 2 * PAST)
        kvT_p = kvT[:, :, 0:NP_TOK]
        posT = q(2, 32)
        pos_rows = q(2, P)
        W2k = q(P)
        W2v = q(P)
        W2kd = q(2, P)
        gk = q(2 * NCMP_S)
        gv = q(2 * NCMP_S)
        cbias = q(2)
        assert q.at <= ARENA
        q.at = keep
        dupK = q(4, 4, P)
        KT = q(4, NP_TOK)
        dist = q(NP_TOK)
        hbias = q(2, NP_TOK)
        sc_p = [q(2, NP_TOK), q(2, NP_TOK)]
        PT = [q(2, 4, P), q(2, 4, P)]
        cmp_bias = q(4, QH, NCMP_P)
        cmp_any = q(4)
        sc_c = q(QH, 32)
        PcT = q(4, P)
        qd_rows = q(D)
        cst = [q(QH), q(QH)]
        ast = [q(8), q(8)]
        assert q.at <= ARENA
        q.at = keep
        slc_raw = q(32, 256)
        KTs = q(2, PAST)
        Ss = q(PAST + NS_TOK)
        PTs = q(17, P)
        slc_bias_s = q(PAST)
        win_bias_s = q(WIN)
        new_bias_s = q(4, NS_TOK)
        cmp_bias_s = q(NCMP_S)
        cover = q(NBLK)
        forced = q(NBLK)
        group = q(P)
        kv_rows = q(2)
        sel = q(3, NBLK)
        sst = q(32)
        orow = q(HD)
        imp = q(NBLK)
        assert q.at <= ARENA, q.at
        odec = slc_raw[:, 0:12, :].rearrange("p a b -> p (a b)")

        d = Carve()
        x1 = d(NTILE, D)
        lnw = d(4, D)
        GT = d(NTOK)
        G_ = d(NTILE, NE)
        bnst = d(2, 6)
        lnst = d(4)
        keep_d = d.at
        wout = d(KD, D)
        wr = d(KD, NE)
        brow = d(NE)
        before8 = d(G, G)
        rt = [d(NTILE, NE) for _ in range(6)]
        m8 = d(NTILE, G, 8)
        gs = d(NTILE, G)
        gr = [d(NTILE, G, G) for _ in range(2)]
        v8 = d(NTILE, 8)
        cnt = d(NTILE)
        assert d.at <= ARENA
        d.at = keep_d
        wge = [d(KD, DE), d(KD, DE)]
        wue = [d(KD, DE), d(KD, DE)]
        wde = [d(2, D), d(2, D)]
        hid = d(2, NTOK)
        sg = d(2, NTOK)
        gsel = d(NTOK)
        grow = d(NTOK)
        assert d.at <= ARENA

        tk = {n: sb(n, [P, NTILE, H]) for n in ("beta", "gg", "gcum", "bg", "kd", "glast", "hbeta", "tmpa", "tmpb", "tmpc")}
        hb = sb("hb", [P, 2, H])

        page_ids = sb("page_ids", [1, NB * NPG], mybir.dt.int32)
        o_scratch = nc.dram_tensor("o_scratch", (3, NB, 2, NT, G * HD), fp32).ap()

        class Steps:
            def __init__(self, eng, own):
                self.eng, self.own, self.n = eng, own, {}

            def __call__(self, ins, signal=None):
                s = signal if signal is not None else self.own
                k = id(s)
                self.n[k] = self.n.get(k, 0) + 1
                ins.then_inc(s, 1)
                self.eng.wait_ge(s, self.n[k])

        def tok(t):
            return (t * P, P if t < 4 else NS_TOK)

        consts_in = sem("consts_in")
        x_in = sem("x_in")
        wkv_in = sem("wkv_in")
        misc_in = sem("misc_in")
        b_in = sem("b_in")
        dve_step = sem("dve_step")
        act_step = sem("act_step")
        zeroed = sem("zeroed")
        xt_banked = sem("xt_banked")
        xt_ready = sem("xt_ready")
        kv_banked = sem("kv_banked")
        kv_ready = sem("kv_ready")
        kv_out = sem("kv_out")
        g_ready = sem("g_ready")
        gcum_banked = sem("gcum_banked")
        tk_ready = sem("tk_ready")
        cw_banked = sem("cw_banked")
        cw_ready = sem("cw_ready")
        wh_in = [sem(f"wh_in{i}") for i in range(RING)]
        rows_in = [sem("rows_in0"), sem("rows_in1")]
        sb_in = sem("sb_in")
        pr_banked = sem("pr_banked")
        pr_saved = sem("pr_saved")
        conv_done = sem("conv_done")
        zm_done = sem("zm_done")
        cg_ready = sem("cg_ready")
        cg_banked = sem("cg_banked")
        cg_saved = sem("cg_saved")
        ey_ready = sem("ey_ready")
        rn_ready = sem("rn_ready")
        y_ready = sem("y_ready")
        act_ready = sem("act_ready")
        sq_ready = sem("sq_ready")
        ss_banked = sem("ss_banked")
        qk_ready = sem("qk_ready")
        gb_ready = sem("gb_ready")
        bc_banked = sem("bc_banked")
        eg_ready = sem("eg_ready")
        diff_ready = sem("diff_ready")
        dec_ready = sem("dec_ready")
        kb_ready = sem("kb_ready")
        tok_banked = sem("tok_banked")
        tok_ready = sem("tok_ready")
        prod_banked = sem("prod_banked")
        lt_ready = sem("lt_ready")
        u_ready = sem("u_ready")
        t_banked = sem("t_banked")
        t_ready = sem("t_ready")
        mt_ready = sem("mt_ready")
        y_banked = sem("y_banked")
        y_saved = sem("y_saved")
        tu_banked = sem("tu_banked")
        tu_ready = sem("tu_ready")
        w_banked = sem("w_banked")
        w_ready = sem("w_ready")
        vn_banked = sem("vn_banked")
        vn_ready = sem("vn_ready")
        s_banked = sem("s_banked")
        s_ready = sem("s_ready")
        vns_banked = sem("vns_banked")
        vns_ready = sem("vns_ready")
        ss_new_banked = sem("ss_new_banked")
        sn_final = sem("sn_final")
        s_out = sem("s_out")
        sn_out = sem("sn_out")
        o_banked = sem("o_banked")
        o_saved = sem("o_saved")
        osq_ready = sem("osq_ready")
        oss_banked = sem("oss_banked")
        ez_ready = sem("ez_ready")
        h_ready = sem("h_ready")
        conv_sent = [sem("conv_sent0"), sem("conv_sent1")]
        block_ctx = ExitStack()
        block = block_ctx.enter_context(nc.Block())

        @block.sync
        def _(sp):
            for t, (name, dst) in enumerate((("ident", ident[:, :]), ("tri", tri[:, :]), ("tri_s", tri_s[:, :]),
                                             ("same_s", same_s[:, :]), ("causal_t", causal_t[:, :]),
                                             ("causal_ts", causal_ts[:, :]), ("rows_s", rows_s[:, :]))):
                sp.dma_start(dst, io[name]).then_inc(consts_in, 16)
            sp.dma_start(xrow[:, 0:4, :], io["x_prompt"][0].rearrange("(t p) d -> p t d", p=P)).then_inc(x_in, 16)
            sp.dma_start(xrow[0:NS_TOK, 4, :], io["x_sample"].rearrange("b t d -> (b t) d")).then_inc(x_in, 16)
            w = io["w_in"][0].rearrange("(k p) n -> p k n", p=P)
            sp.dma_start(wkv[:, :, 0:KVW], w[:, :, COL_KV:COL_MG]).then_inc(wkv_in, 16)
            sp.dma_start(wkv[:, :, KVW:KVW + 16], w[:, :, COL_AB:COL_AB + 16]).then_inc(wkv_in, 16)
            sp.dma_start(hb[:, 0, :], io["dn_dt_bias"][0:1, :].to_broadcast([P, H])).then_inc(misc_in, 16)
            sp.dma_start(hb[:, 1, :], io["dn_A_log"][0:1, :].to_broadcast([P, H])).then_inc(misc_in, 16)
            sp.wait_ge(kv_ready, 2 * NTILE)
            for n in range(3):
                cols = slice(n * 256, n * 256 + 256)
                dst = io[("out2", "out3", "out4")[n]][0, 0].rearrange("(t p) s h d -> p t (s h d)", p=P)
                sp.dma_start(dst, kvt[:, 0:4, cols]).then_inc(kv_out, 16)
                rows = kvt[0:NS_TOK, 4, cols]
                if n < 2:
                    dst = io[("out7", "out8")[n]][0].rearrange("b t s h d -> (b t) (s h d)")
                    sp.dma_start(dst, rows).then_inc(kv_out, 16)
                else:
                    for bb in range(NB):
                        sp.dma_start(io["out9"][0, bb, WIN - NT:WIN].rearrange("t s h d -> t (s h d)"),
                                     kvt[bb * NT:bb * NT + NT, 4, cols]).then_inc(kv_out, 16)
            for bb in range(NB):
                sp.dma_start(io["out9"][0, bb, 0:WIN - NT].rearrange("t s h d -> t (s h d)"),
                             io["cache_win_kv"][0, bb, NT:WIN].rearrange("t s h d -> t (s h d)")).then_inc(kv_out, 16)
            sp.wait_ge(xt_ready, 2 * NTILE)
            sp.dma_start(levels, io["levels"].rearrange("p (l i) -> p l i", l=LEVELS)).then_inc(b_in, 16)
            sp.dma_start(normw, io["dn_norm_w"][0].rearrange("(p o) -> p o", o=1)).then_inc(b_in, 16)
            sp.dma_start(y[0:96, 0, 0:P], io["dn_conv_w"][0].rearrange("j (c p) -> (j c) p", p=P)).then_inc(b_in, 16)
            blocks = [COL_QKV, COL_QKV + D, COL_QKV + 2 * D, COL_Z, COL_MG]

            def load_head(h):
                for n, c0 in enumerate(blocks):
                    i = 5 * h + n
                    if i >= RING:
                        sp.wait_ge(pr_banked, (i - RING) // 5 * 6 + (i - RING) % 5 + 1)
                    sp.dma_start(wh[i % RING], w[:, :, c0 + h * P:c0 + h * P + P]).then_inc(wh_in[i % RING], 16)
                if h >= 2:
                    sp.wait_ge(pr_banked, 6 * (h - 1))
                sp.dma_start(conv_rows[h % 2][0:24],
                             io["state_delta_conv"][0].rearrange("b r (n c) -> (b r) n c", n=3)[:, :, h * P:h * P + P]
                             ).then_inc(rows_in[h % 2], 16)

            load_head(0)
            for h in range(H):
                if h >= 1:
                    sp.wait_ge(sn_final, h)
                sp.dma_start(Sb, io["state_delta_S"][0, :, h].rearrange("b d e -> d b e")).then_inc(sb_in, 16)
                if h + 1 < H:
                    load_head(h + 1)
                sp.wait_ge(cg_saved, h + 1)
                co = conv_out[h % 2]
                hs = slice(h * P, h * P + P)
                sp.dma_start(io["out6"][0, 0].rearrange("r (n c) -> r n c", n=3)[:, :, hs], co[0:3]).then_inc(conv_sent[h % 2], 16)
                sp.dma_start(io["out11"][0].rearrange("b r (n c) -> (b r) n c", n=3)[:, :, hs], co[3:27]).then_inc(conv_sent[h % 2], 16)
                sp.wait_ge(s_ready, (h + 1) * (NCH + 1))
                sp.dma_start(io["out5"][0, 0, h], S[NCH % 2]).then_inc(s_out, 16)
                sp.wait_ge(sn_final, h + 1)
                sp.dma_start(io["out10"][0, :, h].rearrange("b d e -> d b e"), Sn).then_inc(sn_out, 16)
            sp.wait_ge(conv_sent[0], 16 * H)
            sp.wait_ge(conv_sent[1], 16 * H)
            sp.wait_ge(s_out, 16 * H)
            sp.wait_ge(sn_out, 16 * H)
            sp.wait_ge(kv_out, 16 * (5 + 2 * NB))

        @block.tensor
        def _(pe):
            mm, tr = nc.tensor.matmul, nc.tensor.transpose
            pe.wait_ge(consts_in, 16 * 7)
            pe.wait_ge(x_in, 32)
            for t in range(NTILE):
                _, n = tok(t)
                for half in range(2):
                    i = 2 * t + half
                    if i >= 2:
                        pe.wait_ge(xt_ready, i - 1)
                    for k in range(4):
                        last = tr(banks[i % 2][:, k * P:k * P + n], xrow[0:n, t, (4 * half + k) * P:(4 * half + k + 1) * P],
                                  ident[0:n, 0:n])
                    last.then_inc(xt_banked, 1)
            pe.wait_ge(xt_ready, 2 * NTILE)
            pe.wait_ge(wkv_in, 32)
            for t in range(NTILE):
                t0, n = tok(t)
                for half, (c0, c1) in enumerate(((0, 512), (512, KVW + 16))):
                    i = 2 * t + half
                    if i >= 2:
                        pe.wait_ge(kv_ready, i - 1)
                    for k in range(KD):
                        last = mm(banks[2 + i % 2][0:n, 0:c1 - c0], xT[:, k, t0:t0 + n], wkv[:, k, c0:c1],
                                  start=(k == 0), stop=(k == KD - 1))
                    last.then_inc(kv_banked, 1)
            pe.wait_ge(zeroed, 1)
            pe.wait_ge(g_ready, 1)
            gview = tk["gg"]
            mm(banks[4][:, 0:32], tri[:, :], gview[:, 0:4, :], start=True, stop=True)
            mm(banks[4][:, 32:64], ones[:, :], gview[:, 0:4, :], start=True, stop=True)
            mm(banks[4][0:NS_TOK, 64:72], tri_s[:, :], gview[0:NS_TOK, 4, :], start=True, stop=True)
            mm(banks[4][0:NS_TOK, 72:80], same_s[:, :], gview[0:NS_TOK, 4, :], start=True, stop=True).then_inc(gcum_banked, 1)
            pe.wait_ge(b_in, 16 * 3)
            tr(banks[5][:, 0:96], y[0:96, 0, 0:P], ident[0:96, 0:96]).then_inc(cw_banked, 1)

            def project(h):
                for n in range(5):
                    i = 6 * h + n
                    pr = i % 2
                    blk = 5 * h + n
                    pe.wait_ge(wh_in[blk % RING], 16 * (blk // RING + 1))
                    if i >= 2:
                        pe.wait_ge(pr_saved, i - 1)
                    for half in range(2):
                        for k in range(KD):
                            last = mm(banks[2 * pr + half][:, 0:HALF], wh[blk % RING][:, k, :],
                                      xT[:, k, half * HALF:(half + 1) * HALF], start=(k == 0), stop=(k == KD - 1))
                    last.then_inc(pr_banked, 1)
                pe.wait_ge(pr_saved, 6 * h + 5)
                pe.wait_ge(rows_in[h % 2], 16 * (h // 2 + 1))
                for n in range(3):
                    last = tr(banks[2][:, n * 24:(n + 1) * 24], conv_rows[h % 2][0:24, n],
                              ident[0:24, 0:24])
                last.then_inc(pr_banked, 1)

            def delta(h):
                b4, b5, b6, b7 = banks[4], banks[5], banks[6], banks[7]
                S0 = NP_TOK
                pe.wait_ge(cg_ready, h + 1)
                for n in range(3):
                    last = tr(b7[0:27, n * P:(n + 1) * P], cg[:, n, :], ident[:, :])
                last.then_inc(cg_banked, 1)
                pe.wait_ge(sq_ready, h + 1)
                mm(b4[:, :], ones[:, :], sq[:, 0, 0:S0], start=True, stop=True)
                mm(b5[:, :], ones[:, :], sq[:, 1, 0:S0], start=True, stop=True)
                mm(b6[:, 0:32], ones[:, :], sq[:, 0, S0:], start=True, stop=True)
                mm(b6[:, 32:64], ones[:, :], sq[:, 1, S0:], start=True, stop=True).then_inc(ss_banked, 1)
                pe.wait_ge(gb_ready, h + 1)
                pe.wait_ge(qk_ready, h + 1)
                for c in range(NCH):
                    mm(b4[:, c * P:(c + 1) * P], gb[:, 0, c], ident[:, :], start=True, stop=True)
                for c in range(NCH):
                    mm(b5[:, c * P:(c + 1) * P], gb[:, 1, c], tri[:, :], start=True, stop=True)
                mm(b6[:, 0:32], gb[0:32, 0, 4], ident[0:32, 0:32], start=True, stop=True)
                mm(b6[:, 32:64], gb[0:32, 1, 4], tri_s[:, :], start=True, stop=True).then_inc(bc_banked, 1)
                pe.wait_ge(cg_saved, h + 1)
                for c in range(NCH):
                    tr(b7[:, c * P:(c + 1) * P], act[:, 1, c * P:(c + 1) * P], ident[:, :])
                pe.wait_ge(kb_ready, h + 1)
                pe.wait_ge(diff_ready, h + 1)
                pe.wait_ge(eg_ready, h + 1)
                for c in range(NCH):
                    tr(b4[:, c * P:(c + 1) * P], act[:, 2, c * P:(c + 1) * P], ident[:, :])
                tr(b6[0:32, 0:P], act[:, 1, S0:], ident[:, :])
                tr(b6[0:32, P:2 * P], act[:, 2, S0:], ident[:, :]).then_inc(tok_banked, 1)
                for c in range(NCH):
                    cs = slice(c * P, (c + 1) * P)
                    mm(b5[:, cs], act[:, 1, cs], kbT[:, cs], start=True, stop=True)
                pe.wait_ge(tok_ready, h + 1)
                for c in range(NCH):
                    cs = slice(c * P, (c + 1) * P)
                    mm(b7[:, cs], act[:, 1, cs], act[:, 0, cs], start=True, stop=True)
                mm(b6[0:32, 256:288], act[:, 1, S0:], kbT[:, S0:], start=True, stop=True)
                mm(b6[0:32, 288:320], act[:, 1, S0:], act[:, 0, S0:], start=True, stop=True).then_inc(prod_banked, 1)
                pe.wait_ge(u_ready, h + 1)
                for c in range(NCH):
                    tr(b4[:, c * P:(c + 1) * P], U[:, c], ident[:, :])
                tr(b6[0:32, 0:32], U[0:32, 4, 0:32], ident[0:32, 0:32]).then_inc(t_banked, 1)
                pe.wait_ge(t_ready, h + 1)
                for lv in range(1, LEVELS):
                    n = h * (LEVELS - 1) + lv
                    pe.wait_ge(mt_ready, n)
                    if lv >= 2:
                        pe.wait_ge(tu_ready, n - 1)
                    for c in range(NCH):
                        last = mm(b4[:, c * P:(c + 1) * P], MT[:, c], T[:, c], start=True, stop=True)
                    if lv == 1:
                        last = mm(b6[0:32, 0:32], vn[0:32, 4, 0:32], T[0:32, 4, 0:32], start=True, stop=True)
                    last.then_inc(y_banked, 1)
                    pe.wait_ge(y_saved, n)
                    for c in range(NCH):
                        last = mm(b5[:, c * P:(c + 1) * P], Y[:, c], U[:, c], start=True, stop=True)
                    if lv == 1:
                        last = mm(b6[0:32, 32:64], Y[0:32, 4, 0:32], U[0:32, 4, 0:32], start=True, stop=True)
                    if lv < LEVELS - 1:
                        for c in range(NCH):
                            last = mm(b7[:, c * P:(c + 1) * P], U[:, c], Y[:, c], start=True, stop=True)
                    last.then_inc(tu_banked, 1)
                pe.wait_ge(tu_ready, (h + 1) * (LEVELS - 1))
                for c in range(NCH):
                    mm(b4[:, c * P:(c + 1) * P], kbg[:, c], U[:, c], start=True, stop=True)
                mm(b6[:, 0:32], kbg[0:32, 4], U[0:32, 4, 0:32], start=True, stop=True).then_inc(w_banked, 1)
                pe.wait_ge(w_ready, h + 1)
                for c in range(NCH):
                    n = h * NCH + c
                    cs = slice(c * P, (c + 1) * P)
                    pe.wait_ge(s_ready, h * (NCH + 1) + c + 1)
                    mm(b5[:, cs], U[:, c], vb[:, c], start=True, stop=False)
                    mm(b5[:, cs], nwT[:, c], S[c % 2], start=False, stop=True).then_inc(vn_banked, 1)
                    pe.wait_ge(vn_ready, n + 1)
                    mm(b4[:, cs], kdec[:, c], vn[:, c], start=True, stop=True).then_inc(s_banked, 1)
                    mm(b7[:, cs], S[c % 2], qgT[:, cs], start=True, stop=False)
                    mm(b7[:, cs], vn[:, c], AT[:, c], start=False, stop=True).then_inc(o_banked, 1)
                pe.wait_ge(sb_in, 16 * (h + 1))
                mm(b6[0:32, 128:256], U[0:32, 4, 0:32], vb[0:32, 4], start=True, stop=False)
                for bb in range(NB):
                    last = mm(b6[0:32, 128:256], nw8[:, bb * 32:bb * 32 + 32], Sb[:, bb], start=False, stop=(bb == NB - 1))
                last.then_inc(vns_banked, 1)
                pe.wait_ge(vns_ready, h + 1)
                mm(b6[:, 0:32], vn[0:32, 4], AT[0:32, 4, 0:32], start=True, stop=False)
                for bb in range(NB):
                    last = mm(b6[:, bb * NT:bb * NT + NT], Sb[:, bb], qgT[:, S0 + bb * NT:S0 + bb * NT + NT],
                              start=False, stop=(bb == NB - 1))
                last.then_inc(o_banked, 1)
                pe.wait_ge(s_ready, (h + 1) * (NCH + 1))
                for bb in range(NB):
                    last = mm((b4, b5)[bb // 4][:, (bb % 4) * P:(bb % 4 + 1) * P], kdec8[0:32, bb], vn[0:32, 4],
                              start=True, stop=True)
                last.then_inc(ss_new_banked, 1)
                pe.wait_ge(osq_ready, h + 1)
                mm(b7[:, :], ones[:, :], sq[:, 0, 0:S0], start=True, stop=True)
                mm(b6[:, 0:32], ones[:, :], sq[:, 0, S0:], start=True, stop=True).then_inc(oss_banked, 1)

            project(0)
            for h in range(H):
                if h + 1 < H:
                    project(h + 1)
                if h >= 1:
                    pe.wait_ge(h_ready, h)
                delta(h)

        @block.scalar
        def _(sc):
            actv = nc.scalar.activation
            step = Steps(sc, act_step)
            for t in range(NTILE):
                t0, n = tok(t)
                for half in range(2):
                    i = 2 * t + half
                    sc.wait_ge(xt_banked, i + 1)
                    actv(xT[:, 4 * half:4 * half + 4, t0:t0 + n],
                         banks[i % 2][:, :].rearrange("p (k n) -> p k n", k=4)[:, :, 0:n], ACT.Copy).then_inc(xt_ready, 1)
            sc.wait_ge(zeroed, 2)
            for t in range(NTILE):
                _, n = tok(t)
                sc.wait_ge(kv_banked, 2 * t + 1)
                actv(kvt[0:n, t, 0:512], banks[2][0:n, :], ACT.Copy).then_inc(kv_ready, 1)
                sc.wait_ge(kv_banked, 2 * t + 2)
                actv(ab[0:n, t, :], banks[3][0:n, 304:320], ACT.Copy)
                actv(kvt[0:n, t, 512:KVW], banks[3][0:n, 0:304], ACT.Copy).then_inc(kv_ready, 1)
            sc.wait_ge(misc_in, 32)
            sc.wait_ge(y_ready, 1)
            step(actv(tk["tmpb"][:, :, :], tk["tmpa"][:, :, :], ACT.Abs))
            step(actv(tk["tmpb"][:, :, :], tk["tmpb"][:, :, :], ACT.Exp, scale=-1.0))
            actv(tk["beta"][:, :, :], ab[:, :, 8:16], ACT.Exp, scale=-1.0)
            actv(hb[:, 1, :], hb[:, 1, :], ACT.Exp)
            actv(tk["tmpb"][:, :, :], tk["tmpb"][:, :, :], ACT.Ln, bias=1.0).then_inc(ey_ready, 1)
            sc.wait_ge(y_ready, 2)
            actv(tk["kd"][:, :, :], tk["kd"][:, :, :], ACT.Exp)
            actv(tk["bg"][:, :, :], tk["gcum"][:, :, :], ACT.Exp).then_inc(ey_ready, 1)
            sc.wait_ge(cw_banked, 1)
            actv(convw[:, :], banks[5][:, 0:96], ACT.Copy).then_inc(cw_ready, 1)

            def save_projection(h):
                if h >= 2:
                    sc.wait_ge(conv_done, h - 1)
                    sc.wait_ge(cg_ready, h - 1)
                    sc.wait_ge(zm_done, h - 1)
                for n in range(5):
                    i = 6 * h + n
                    pr = i % 2
                    sc.wait_ge(pr_banked, i + 1)
                    b0, b1 = banks[2 * pr], banks[2 * pr + 1]
                    m = NP_TOK - HALF
                    if n < 3:
                        r = raw[h % 2]
                        actv(r[:, n, 3:3 + HALF], b0[:, 0:HALF], ACT.Copy)
                        actv(r[:, n, 3 + HALF:SROW], b1[:, 0:m], ACT.Copy)
                        actv(r[:, n, SROW:].rearrange("p (b s) -> p b s", s=7)[:, :, 3:7],
                             b1[:, m:HALF].rearrange("p (b s) -> p b s", s=4), ACT.Copy).then_inc(pr_saved, 1)
                    else:
                        actv(zm[h % 2][:, n - 3, 0:HALF], b0[:, 0:HALF], ACT.Copy)
                        actv(zm[h % 2][:, n - 3, HALF:], b1[:, 0:HALF], ACT.Copy).then_inc(pr_saved, 1)
                sc.wait_ge(pr_banked, 6 * h + 6)
                for n in range(3):
                    last = actv(raw[h % 2][:, n, SROW:].rearrange("p (b s) -> p b s", s=7)[:, :, 0:3],
                                banks[2][:, n * 24:(n + 1) * 24].rearrange("p (b s) -> p b s", s=3), ACT.Copy)
                last.then_inc(pr_saved, 1)

            def conv_exp(h):
                sc.wait_ge(conv_done, h + 1)
                sc.wait_ge(pr_saved, 6 * (h + 1))
                actv(ey, y, ACT.Tanh, scale=0.5).then_inc(ey_ready, 1)
                actv(sgz, zm[h % 2], ACT.Tanh, scale=0.5).then_inc(ez_ready, 1)
                sc.wait_ge(act_ready, h + 1)
                actv(sq, act[:, 0:2, :], ACT.Square, scale=0.5).then_inc(sq_ready, 1)

            def delta(h):
                b4, b5, b6, b7 = banks[4], banks[5], banks[6], banks[7]
                S0 = NP_TOK
                sc.wait_ge(cg_banked, h + 1)
                if h >= 2:
                    sc.wait_ge(conv_sent[h % 2], 32 * (h // 2))
                actv(conv_out[h % 2][0:27],
                     b7[0:27, 0:384].rearrange("r (n c) -> r n c", n=3), ACT.Copy).then_inc(cg_saved, 1)
                sc.wait_ge(ss_banked, h + 1)
                actv(rn[:, 0, 0:S0], b4[:, :], ACT.Ln, bias=eps[:, 0:1])
                actv(rn[:, 1, 0:S0], b5[:, :], ACT.Ln, bias=eps[:, 0:1])
                step(actv(rn[:, :, S0:], b6[:, 0:64].rearrange("p (a b) -> p a b", a=2), ACT.Ln, bias=eps[:, 0:1]))
                actv(rn, rn, ACT.Exp, scale=-0.5).then_inc(rn_ready, 1)
                sc.wait_ge(bc_banked, h + 1)
                actv(eg[:, 0:S0], b5[:, :], ACT.Exp)
                actv(eg[:, S0:], b6[:, 32:64], ACT.Exp).then_inc(eg_ready, 1)
                sc.wait_ge(diff_ready, h + 1)
                actv(dec[:, 0:4], dec[:, 0:4], ACT.Exp)
                actv(dec[0:32, 4, 0:32], dec[0:32, 4, 0:32], ACT.Exp).then_inc(dec_ready, 1)
                sc.wait_ge(t_banked, h + 1)
                actv(T[:, 0:4], b4[:, :].rearrange("p (c i) -> p c i", c=4), ACT.Copy)
                actv(T[0:32, 4, 0:32], b6[0:32, 0:32], ACT.Copy).then_inc(t_ready, 1)
                for lv in range(1, LEVELS):
                    sc.wait_ge(y_banked, h * (LEVELS - 1) + lv)
                    last = actv(Y[:, 0:4], b4[:, :].rearrange("p (c i) -> p c i", c=4), ACT.Copy)
                    if lv == 1:
                        last = actv(Y[0:32, 4, 0:32], b6[0:32, 0:32], ACT.Copy)
                    last.then_inc(y_saved, 1)
                sc.wait_ge(w_banked, h + 1)
                actv(nwT, b4[:, :].rearrange("p (c i) -> p c i", c=4), ACT.Copy, scale=-1.0)
                actv(nw8.rearrange("p (b s) -> p b s", s=36)[:, :, 0:NT],
                     b6[:, 0:32].rearrange("p (b s) -> p b s", s=NT), ACT.Copy, scale=-1.0).then_inc(w_ready, 1)
                for c in range(NCH):
                    n = h * NCH + c
                    sc.wait_ge(vn_banked, n + 1)
                    actv(vn[:, c], b5[:, c * P:(c + 1) * P], ACT.Copy).then_inc(vn_ready, 1)
                sc.wait_ge(vns_banked, h + 1)
                actv(vn[0:32, 4], b6[0:32, 128:256], ACT.Copy).then_inc(vns_ready, 1)
                sc.wait_ge(o_banked, (h + 1) * (NCH + 1))
                if h >= 1:
                    sc.wait_ge(h_ready, h)
                actv(oT[:, 0:S0], b7[:, :], ACT.Copy)
                step(actv(oT[:, S0:], b6[:, 0:32], ACT.Copy), o_saved)
                actv(sq[:, 0, :], oT, ACT.Square).then_inc(osq_ready, 1)
                sc.wait_ge(oss_banked, h + 1)
                actv(rn[:, 1, 0:S0], b7[:, :], ACT.Ln, scale=1.0 / DH, bias=eps[:, 0:1])
                step(actv(rn[:, 1, S0:], b6[:, 0:32], ACT.Ln, scale=1.0 / DH, bias=eps[:, 0:1]))
                actv(rn[:, 1], rn[:, 1], ACT.Exp, scale=-0.5).then_inc(rn_ready, 1)

            save_projection(0)
            for h in range(H):
                conv_exp(h)
                if h + 1 < H:
                    save_projection(h + 1)
                delta(h)

        @block.gpsimd
        def _(pool):
            nc.gpsimd.memset(eps[:, 0:1], 1e-6)
            nc.gpsimd.memset(eps[:, 1:2], 1e-5)
            nc.gpsimd.memset(ones[:, :], 1.0).then_inc(zeroed, 1)
            nc.gpsimd.memset(ab[:, 4, :], 0.0).then_inc(zeroed, 1)
            pool.wait_ge(tk_ready, 1)
            pool.wait_ge(kv_ready, 2 * NTILE)
            for r in raw:
                for n in range(3):
                    nc.gpsimd.memset(r[:, n, 0:3], 0.0)
            nc.gpsimd.memset(nw8, 0.0).then_inc(zeroed, 1)
            for h in range(H):
                if h >= 1:
                    pool.wait_ge(bc_banked, h)
                for n, src in enumerate((tk["beta"], tk["gg"])):
                    last = nc.gpsimd.tensor_copy(gb[:, n], src[:, :, h:h + 1].to_broadcast([P, NTILE, P]))
                last.then_inc(gb_ready, 1)
                pool.wait_ge(pr_saved, 6 * (h + 1))
                if h >= 1:
                    pool.wait_ge(cg_banked, h)
                nc.gpsimd.tensor_copy(cg[:, :, 0:3], raw[h % 2][:, :, NP_TOK:NP_TOK + 3])
                for n in range(3):
                    last = nc.gpsimd.tensor_copy(cg[:, n, 3:27].rearrange("p (b s) -> p b s", s=3),
                                                 raw[h % 2][:, n, SROW:].rearrange("p (b s) -> p b s", s=7)[:, :, 4:7])
                last.then_inc(cg_ready, 1)
                pool.wait_ge(lt_ready, h + 1)
                for lv in range(1, LEVELS):
                    n = h * (LEVELS - 1) + lv
                    if n >= 2:
                        pool.wait_ge(y_banked, n - 1)
                    last = nc.gpsimd.tensor_tensor(MT, LT[:, 0:4], levels[:, lv:lv + 1, :].to_broadcast([P, 4, P]), ALU.mult)
                    if lv == 1:
                        last = nc.gpsimd.tensor_tensor(vn[0:32, 4, 0:32], LT[0:32, 4, 0:32], levels[0:32, lv, 0:32], ALU.mult)
                    last.then_inc(mt_ready, 1)

        @block.vector
        def _(dve):
            step = Steps(dve, dve_step)
            V = nc.vector
            beta, gg, gcum, bg, kd, glast, hbeta = (tk[n] for n in ("beta", "gg", "gcum", "bg", "kd", "glast", "hbeta"))
            dve.wait_ge(zeroed, 2)
            step(V.memset(gcum[:, 4, :], 0.0))
            step(V.memset(glast[:, 4, :], 0.0))
            dve.wait_ge(kv_ready, 2 * NTILE)
            dve.wait_ge(misc_in, 32)
            step(V.tensor_tensor(tk["tmpa"][:, :, :], ab[:, :, 0:8], hb[:, 0:1, :].to_broadcast([P, NTILE, H]), ALU.add), y_ready)
            dve.wait_ge(ey_ready, 1)
            step(V.tensor_scalar(tk["tmpc"][:, :, :], tk["tmpa"][:, :, :], 0.0, None, ALU.max))
            step(V.tensor_tensor(tk["tmpc"][:, :, :], tk["tmpc"][:, :, :], tk["tmpb"][:, :, :], ALU.add))
            step(V.scalar_tensor_tensor(gg[:, :, :], tk["tmpc"][:, :, :], -1.0, hb[:, 1:2, :].to_broadcast([P, NTILE, H]),
                                        ALU.mult, ALU.mult), g_ready)
            step(V.tensor_scalar(beta[:, :, :], beta[:, :, :], 1.0, None, ALU.add))
            step(V.reciprocal(beta[:, :, :], beta[:, :, :]))
            step(V.tensor_scalar(hbeta[:, :, :], beta[:, :, :], 0.5, None, ALU.mult))
            dve.wait_ge(gcum_banked, 1)
            step(V.tensor_copy(gcum[:, 0:4, :], banks[4][:, 0:32].rearrange("p (c h) -> p c h", c=4)))
            step(V.tensor_copy(glast[:, 0:4, :], banks[4][:, 32:64].rearrange("p (c h) -> p c h", c=4)))
            step(V.tensor_copy(gcum[0:32, 4, :], banks[4][0:32, 64:72]))
            step(V.tensor_copy(glast[0:32, 4, :], banks[4][0:32, 72:80]))
            step(V.tensor_tensor(kd[:, :, :], glast[:, :, :], gcum[:, :, :], ALU.subtract), y_ready)
            dve.wait_ge(ey_ready, 2)
            step(V.tensor_tensor(bg[:, :, :], bg[:, :, :], beta[:, :, :], ALU.mult), tk_ready)
            dve.wait_ge(zeroed, 3)
            dve.wait_ge(cw_ready, 1)
            dve.wait_ge(b_in, 16 * 3)
            step(V.tensor_scalar(normw, normw, 0.25, None, ALU.mult))

            def conv(h):
                dve.wait_ge(pr_saved, 6 * (h + 1))
                r = raw[h % 2]
                n = RAWW - 3
                for i in range(3):
                    w = [convw[:, j * 24 + i * 8 + h:j * 24 + i * 8 + h + 1] for j in range(4)]
                    step(V.tensor_scalar(y[:, i], r[:, i, 0:n], w[0], None, ALU.mult))
                    for j in range(1, 3):
                        step(V.scalar_tensor_tensor(y[:, i], r[:, i, j:j + n], w[j], y[:, i], ALU.mult, ALU.add))
                    ins = V.scalar_tensor_tensor(y[:, i], r[:, i, 3:3 + n], w[3], y[:, i], ALU.mult, ALU.add)
                    step(ins, conv_done if i == 2 else None)
                dve.wait_ge(ey_ready, 2 + h + 1)
                for i in range(3):
                    step(V.scalar_tensor_tensor(act[:, i, 0:NP_TOK], ey[:, i, 0:NP_TOK], 1.0, y[:, i, 0:NP_TOK], ALU.add, ALU.mult))
                    ev, yv = (v[:, i, SROW:SROW + 49].rearrange("p (b s) -> p b s", s=7)[:, :, 0:4] for v in (ey, y))
                    step(V.scalar_tensor_tensor(act[:, i, NP_TOK:NP_TOK + 28].rearrange("p (b s) -> p b s", s=4), ev, 1.0, yv,
                                                ALU.add, ALU.mult))
                end = slice(SROW + 49, SROW + 53)
                step(V.scalar_tensor_tensor(act[:, :, NP_TOK + 28:], ey[:, :, end], 1.0, y[:, :, end], ALU.add, ALU.mult), act_ready)

            def delta(h):
                b4, b5, b6, b7 = banks[4], banks[5], banks[6], banks[7]
                S0 = NP_TOK
                chunks = lambda ap: ap.rearrange("p (c i) -> p c i", c=4)
                dve.wait_ge(rn_ready, 2 * h + 1)
                step(V.scalar_tensor_tensor(act[:, 0], act[:, 0], 0.5 * float(DH) ** -0.5, rn[:, 0], ALU.mult, ALU.mult))
                step(V.scalar_tensor_tensor(act[:, 1], act[:, 1], 0.5, rn[:, 1], ALU.mult, ALU.mult), qk_ready)
                dve.wait_ge(bc_banked, h + 1)
                step(V.tensor_tensor(kbT[:, 0:S0], act[:, 1, 0:S0], b4[:, :], ALU.mult))
                dve.wait_ge(eg_ready, h + 1)
                step(V.tensor_tensor(kbT[:, S0:], act[:, 1, S0:], b6[:, 0:32], ALU.mult), kb_ready)
                step(V.tensor_tensor(dec[:, 0:4], chunks(b5[:, :]), gcum[:, 0:4, h:h + 1].to_broadcast([P, 4, P]), ALU.subtract))
                step(V.scalar_tensor_tensor(dec[:, 0:4], dec[:, 0:4], 0.0, causal_t[:, :].rearrange("p (o i) -> p o i", o=1).to_broadcast([P, 4, P]),
                                            ALU.min, ALU.add))
                step(V.tensor_scalar(dec[0:32, 4, 0:32], b6[0:32, 32:64], gcum[0:32, 4, h:h + 1], 0.0, ALU.subtract, ALU.min))
                step(V.tensor_tensor(dec[0:32, 4, 0:32], dec[0:32, 4, 0:32], causal_ts[:, :], ALU.add), diff_ready)
                step(V.tensor_tensor(qgT, act[:, 0], eg, ALU.mult))
                dve.wait_ge(tok_banked, h + 1)
                if h >= 1:
                    dve.wait_ge(ss_new_banked, h)
                for dst, src, ssrc, s in ((kbg, b7[:, :], b6[0:32, 0:P], bg), (kdec, b7[:, :], b6[0:32, 0:P], kd),
                                          (vb, b4[:, :], b6[0:32, P:2 * P], hbeta)):
                    step(V.tensor_tensor(dst[:, 0:4], chunks(src), s[:, 0:4, h:h + 1].to_broadcast([P, 4, P]), ALU.mult))
                    last = V.tensor_scalar(dst[0:32, 4], ssrc, s[0:32, 4, h:h + 1], None, ALU.mult)
                    step(last, tok_ready if s is hbeta else None)
                step(V.tensor_tensor(kdec8[0:32], kdec[0:32, 4:5, :].to_broadcast([32, NB, P]),
                                     rows_s[:, :].rearrange("p (b o) -> p b o", o=1).to_broadcast([32, NB, P]), ALU.mult))
                dve.wait_ge(prod_banked, h + 1)
                dve.wait_ge(dec_ready, h + 1)
                step(V.tensor_tensor(LT[:, 0:4], chunks(b5[:, :]), dec[:, 0:4], ALU.mult))
                step(V.tensor_tensor(LT[0:32, 4, 0:32], b6[0:32, 256:288], dec[0:32, 4, 0:32], ALU.mult), lt_ready)
                step(V.tensor_tensor(AT[:, 0:4], chunks(b7[:, :]), dec[:, 0:4], ALU.mult))
                step(V.tensor_tensor(AT[0:32, 4, 0:32], b6[0:32, 288:320], dec[0:32, 4, 0:32], ALU.mult))
                step(V.scalar_tensor_tensor(U[:, 0:4], LT[:, 0:4], -1.0, levels[:, 0:1, :].to_broadcast([P, 4, P]), ALU.mult, ALU.mult))
                step(V.scalar_tensor_tensor(U[0:32, 4, 0:32], LT[0:32, 4, 0:32], -1.0, levels[0:32, 0, 0:32], ALU.mult, ALU.mult))
                step(V.tensor_tensor(U[:, 0:4], U[:, 0:4], ident[:, :].rearrange("p (o i) -> p o i", o=1).to_broadcast([P, 4, P]), ALU.add))
                step(V.tensor_tensor(U[0:32, 4, 0:32], U[0:32, 4, 0:32], ident[0:32, 0:32], ALU.add), u_ready)
                dve.wait_ge(t_ready, h + 1)
                for lv in range(1, LEVELS):
                    dve.wait_ge(tu_banked, h * (LEVELS - 1) + lv)
                    if lv == 1:
                        step(V.tensor_tensor(U[0:32, 4, 0:32], U[0:32, 4, 0:32], b6[0:32, 32:64], ALU.subtract))
                    if lv < LEVELS - 1:
                        step(V.tensor_tensor(T[:, 0:4], T[:, 0:4], chunks(b7[:, :]), ALU.subtract))
                    step(V.tensor_tensor(U[:, 0:4], U[:, 0:4], chunks(b5[:, :]), ALU.subtract), tu_ready)
                if h >= 1:
                    dve.wait_ge(s_out, 16 * h)
                step(V.memset(S[0], 0.0), s_ready)
                for c in range(NCH):
                    dve.wait_ge(s_banked, h * NCH + c + 1)
                    last = (V.scalar_tensor_tensor(S[(c + 1) % 2], S[c % 2], eg[:, (c + 1) * P - 1:(c + 1) * P],
                                                     b4[:, c * P:(c + 1) * P], ALU.mult, ALU.add))
                    step(last, s_ready)
                if h >= 1:
                    dve.wait_ge(sn_out, 16 * h)
                dve.wait_ge(ss_new_banked, h + 1)
                egl = eg[:, S0:].rearrange("p (b s) -> p b s", s=NT)[:, :, NT - 1:NT].to_broadcast([P, NB, P])
                step(V.tensor_tensor(Sn, Sb, egl, ALU.mult))
                step(V.tensor_tensor(Sn[:, 0:4], Sn[:, 0:4], chunks(b4[:, :]), ALU.add))
                step(V.tensor_tensor(Sn[:, 4:8], Sn[:, 4:8], chunks(b5[:, :]), ALU.add), sn_final)
                dve.wait_ge(rn_ready, 2 * h + 2)
                step(V.scalar_tensor_tensor(oT, oT, normw, rn[:, 1], ALU.mult, ALU.mult))
                dve.wait_ge(ez_ready, h + 1)
                step(V.scalar_tensor_tensor(sgz[:, 0], sgz[:, 0], 1.0, zm[h % 2][:, 0], ALU.add, ALU.mult), zm_done)
                step(V.scalar_tensor_tensor(sgz[:, 0], sgz[:, 1], 1.0, sgz[:, 0], ALU.add, ALU.mult))
                step(V.tensor_tensor(hT[:, h], oT, sgz[:, 0], ALU.mult), h_ready)

            for h in range(H):
                conv(h)
                delta(h)

        block_ctx.close()
        end_block()

        dve_step = sem("dve_step")
        act_step = sem("act_step")
        wh_in = [sem(f"wh_in{i}") for i in range(RING)]
        ids_in = sem("ids_in")
        w1_in = sem("w1_in")
        c2_in = sem("c2_in")
        att_in = sem("att_in")
        dec_in = sem("dec_in")
        pool_step = sem("pool_step")
        prj_banked = sem("prj_banked")
        prj_saved = sem("prj_saved")
        q_zeroed = sem("q_zeroed")
        kvp_banked = sem("kvp_banked")
        kvp_saved = sem("kvp_saved")
        posr_banked = sem("posr_banked")
        posr_saved = sem("posr_saved")
        pg_banked = sem("pg_banked")
        pg_saved = [sem("pg_saved_even"), sem("pg_saved_odd")]
        hid_banked = sem("hid_banked")
        gelu_done = sem("gelu_done")
        cmpo_banked = sem("cmpo_banked")
        cmpo_saved = sem("cmpo_saved")
        gt_tanh = sem("gt_tanh")
        gt_ready = sem("gt_ready")
        dup_ready = sem("dup_ready")
        kt_banked = sem("kt_banked")
        kt_saved = sem("kt_saved")
        cs_banked = sem("cs_banked")
        cs_max = sem("cs_max")
        cs_exp = sem("cs_exp")
        cs_ready = sem("cs_ready")
        pct_banked = sem("pct_banked")
        pct_saved = sem("pct_saved")
        co_banked = sem("co_banked")
        co_saved = sem("co_saved")
        hb_ready = sem("hb_ready")
        at_banked = sem("at_banked")
        at_max = sem("at_max")
        at_raw = sem("at_raw")
        at_exp = sem("at_exp")
        at_tr_banked = sem("at_tr_banked")
        at_tr_a = sem("at_tr_a")
        at_tr_v = sem("at_tr_v")
        at_o_banked = sem("at_o_banked")
        at_done = sem("at_done")
        qr_banked = sem("qr_banked")
        qr_saved = sem("qr_saved")
        qd_banked = sem("qd_banked")
        qd_ready = sem("qd_ready")
        slc_in = sem("slc_in")
        win_in = sem("win_in")
        ks_banked = sem("ks_banked")
        ks_saved = sem("ks_saved")
        kn_saved = sem("kn_saved")
        sd_banked = sem("sd_banked")
        sd_max = sem("sd_max")
        sd_exp = sem("sd_exp")
        sd_sum = sem("sd_sum")
        ptd_banked = sem("ptd_banked")
        ptd_saved = sem("ptd_saved")
        od_banked = sem("od_banked")
        od_saved = sem("od_saved")
        imp_banked = sem("imp_banked")
        imp_saved = sem("imp_saved")
        grp_banked = sem("grp_banked")
        sel_ready = sem("sel_ready")
        od_out = sem("od_out")
        odec_in = sem("odec_in")
        odec_ready = sem("odec_ready")
        of_banked = sem("of_banked")
        of_ready = sem("of_ready")
        page_in = [sem(f"page_in{i}") for i in range(8)]
        block_ctx = ExitStack()
        block = block_ctx.enter_context(nc.Block())

        @block.sync
        def _(sp):
            w = io["w_in"][0].rearrange("(k p) n -> p k n", p=P)
            for n in range(16):
                if n >= RING:
                    sp.wait_ge(prj_banked, n - RING + 1)
                c0 = COL_NQ + n * P if n < 8 else COL_MG + D + (n - 8) * P
                sp.dma_start(wh[n % RING], w[:, :, c0:c0 + P]).then_inc(wh_in[n % RING], 16)
            w1 = io["nsa_cmp_w1"][0].rearrange("s (r d) e -> d s r e", d=HD)
            for s in range(2):
                for kv in range(2):
                    half = slice(kv * 64, kv * 64 + 64)
                    sp.dma_start(W1[half, s, :, half], w1[:, s]).then_inc(w1_in, 16)
            sp.dma_start(page_ids[0:1, :], io["page_table"].rearrange("(o b) p -> o (b p)", o=1)).then_inc(ids_in, 16)
            sp.wait_ge(prj_banked, 16)
            pos = io["nsa_cmp_pos"][0].rearrange("s r d -> r s d")
            w2 = io["nsa_cmp_w2"][0]
            for kv in range(2):
                half = slice(kv * 64, kv * 64 + 64)
                sp.dma_start(pos_rows[0:32, :, half], pos).then_inc(c2_in, 16)
                sp.wait_ge(q_zeroed, 1)
                sp.dma_start(W2k[half, half], w2[0]).then_inc(c2_in, 16)
                sp.dma_start(W2v[half, half], w2[1]).then_inc(c2_in, 16)
                for dup in range(2):
                    sp.dma_start(W2kd[half, kv, dup * 64:dup * 64 + 64], w2[0]).then_inc(c2_in, 16)
            sp.wait_ge(ids_in, 16)
            cmp_pool = io["cache_cmp_kv"][0].rearrange("n p s h d -> n p (s h d)")
            slc_pool = io["cache_slc_kv"][0].rearrange("n p s h d -> n p (s h d)")
            for j in range(8):
                page = sp.value_load(page_ids[0:1, j:j + 1], min_val=0, max_val=NPOOL - 1)
                sp.dma_start(pages[:, j, :], cmp_pool[bass.ds(page, 1)]).then_inc(page_in[j], 16)
            with sp.Fori(1, NB * NPG // 8) as it:
                for j in range(8):
                    page = sp.value_load(page_ids[0:1, bass.ds(it * 8 + j, 1)], min_val=0, max_val=NPOOL - 1)
                    sp.wait_ge(pg_banked, it * 4 + (j // 2 - 3))
                    sp.dma_start(pages[:, j, :], cmp_pool[bass.ds(page, 1)]).then_inc(page_in[j], 16)
            sp.wait_ge(cmpo_saved, 2 + 8)
            sp.dma_start(dist, io["dist"]).then_inc(att_in, 16)
            sp.dma_start(cmp_bias, io["cmp_bias"].rearrange("p (t h c) -> p t h c", t=4, h=QH)).then_inc(att_in, 16)
            sp.dma_start(cmp_any, io["cmp_any"]).then_inc(att_in, 16)
            sp.wait_ge(at_done, 64)
            sp.wait_ge(qd_ready, 1)
            for dst, name in ((slc_bias_s, "slc_bias_s"), (win_bias_s, "win_bias_s"), (cmp_bias_s, "cmp_bias_s"),
                              (cover[0:NCMP_S], "cover"), (forced, "forced"), (group, "group"), (kv_rows, "kv_rows")):
                sp.dma_start(dst, io[name]).then_inc(dec_in, 16)
            sp.dma_start(new_bias_s, io["new_bias_s"].rearrange("p (a k) -> p a k", a=4)).then_inc(dec_in, 16)
            win_pool = io["cache_win_kv"][0].rearrange("b (t p) s h d -> b p t (s h d)", p=P)
            for pair in range(4):
                if pair >= 1:
                    sp.wait_ge(od_saved, 3 * pair)
                with sp.Fori(0, 32) as i:
                    page = sp.value_load(page_ids[0:1, bass.ds(i + 32 * pair, 1)], min_val=0, max_val=NPOOL - 1)
                    sp.dma_start(slc_raw[:, bass.ds(i, 1), :], slc_pool[bass.ds(page, 1)].rearrange("o p c -> p o c")).then_inc(slc_in, 16)
                for br in range(2):
                    sp.wait_ge(od_saved, 3 * pair + br + 1)
                    sp.dma_start(o_scratch[br, 2 * pair:2 * pair + 2].rearrange("b h t (g d) -> (b h t g) d", g=G),
                                 orow).then_inc(od_out, 16)
                for b2 in range(2):
                    sp.dma_start(slc_raw[:, 4 * b2:4 * b2 + 4, :], win_pool[2 * pair + b2]).then_inc(win_in, 16)
                sp.wait_ge(od_saved, 3 * pair + 3)
                sp.dma_start(o_scratch[2, 2 * pair:2 * pair + 2].rearrange("b h t (g d) -> (b h t g) d", g=G),
                             orow).then_inc(od_out, 16)
            sp.wait_ge(od_out, 16 * 12)
            for br in range(3):
                for bb in range(NB):
                    sp.dma_start(odec[bb * NT:bb * NT + NT, br * D:(br + 1) * D].rearrange("t (h x) -> t h x", h=2),
                                 o_scratch[br, bb].rearrange("h t x -> t h x")).then_inc(odec_in, 16)

        @block.tensor
        def _(pe):
            mm, tr = nc.tensor.matmul, nc.tensor.transpose
            for n in range(16):
                blk = n
                pe.wait_ge(wh_in[blk % RING], 16 * (blk // RING + 1))
                if n >= 2:
                    pe.wait_ge(prj_saved, n - 1)
                for half in range(2):
                    for k in range(KD):
                        last = mm(banks[2 * (n % 2) + half][:, 0:HALF], wh[blk % RING][:, k, :],
                                  xT[:, k, half * HALF:(half + 1) * HALF], start=(k == 0), stop=(k == KD - 1))
                last.then_inc(prj_banked, 1)
            pe.wait_ge(prj_saved, 16)
            for g in range(2):
                for s in range(2):
                    for j in range(2):
                        last = tr(banks[g][:, s * 256 + j * P:s * 256 + j * P + P], kvt[:, 2 * g + j, s * P:s * P + P], ident[:, :])
                last.then_inc(kvp_banked, 1)
            pe.wait_ge(c2_in, 16 * 10)
            for s in range(2):
                last = tr(banks[2][:, s * 32:s * 32 + 32], pos_rows[0:32, s, :], ident[0:32, 0:32])
            last.then_inc(posr_banked, 1)
            pe.wait_ge(posr_saved, 1)
            pe.wait_ge(w1_in, 16 * 4)
            for s in range(2):
                for rp in range(32):
                    last = mm(banks[3][:, s:s + 1], W1[:, s, rp, :], posT[:, s, rp:rp + 1], start=(rp == 0), stop=(rp == 31))
            last.then_inc(posr_banked, 1)

            def compress(src, width):
                for s in range(2):
                    for rp in range(32):
                        last = mm(banks[4 + s][:, 0:width], W1[:, s, rp, :], src(s, rp // 16, rp % 16), start=(rp == 0), stop=(rp == 31))
                last.then_inc(hid_banked, 1)

            pe.wait_ge(kvp_saved, 2)
            compress(lambda s, a, b: kvT_p[:, s].rearrange("p (n q) -> p n q", q=16)[:, a:a + NCMP_P, b], NCMP_P)
            pe.wait_ge(gelu_done, 1)
            for kv in range(2):
                mm(banks[6][:, kv * 32:kv * 32 + NCMP_P], W2kd[:, kv], gk[:, 0:NCMP_P], start=True, stop=True)
            mm(banks[7][:, 0:P], gv[:, 0:P], W2v, start=True, stop=True).then_inc(cmpo_banked, 1)
            for pair in range(4):
                for g in range(16):
                    i = 16 * pair + g
                    for j in range(2):
                        n = 2 * i + j
                        pe.wait_ge(page_in[n % 8], 16 * (n // 8 + 1))
                    if i >= 2:
                        pe.wait_ge(pg_saved[i % 2], i // 2)
                    if i == 0:
                        pe.wait_ge(kvp_saved, 2)
                    for s in range(2):
                        for j in range(2):
                            last = tr(banks[i % 2][:, s * 256 + j * P:s * 256 + j * P + P],
                                      pages[:, (2 * i + j) % 8, s * P:s * P + P], ident[:, :])
                    last.then_inc(pg_banked, 1)
                pe.wait_ge(pg_saved[0], 8 * (pair + 1))
                pe.wait_ge(pg_saved[1], 8 * (pair + 1))
                pe.wait_ge(gelu_done, pair + 1)
                compress(lambda s, a, b: kvT[:, s].rearrange("p (c n q) -> p c n q", c=2, q=16)[:, :, a:a + NCMP_S, b], 2 * NCMP_S)
                pe.wait_ge(gelu_done, pair + 2)
                pe.wait_ge(cmpo_saved, 2 * pair + 2)
                mm(banks[6][:, 0:2 * NCMP_S], W2k, gk, start=True, stop=True)
                for b2 in range(2):
                    last = mm(banks[7][0:NCMP_S, b2 * P:(b2 + 1) * P], gv[:, b2 * NCMP_S:(b2 + 1) * NCMP_S], W2v, start=True, stop=True)
                last.then_inc(cmpo_banked, 1)

            pe.wait_ge(dup_ready, 1)
            for n in range(4):
                if n >= 2:
                    pe.wait_ge(kt_saved, n - 1)
                for t in range(4):
                    last = tr(banks[n % 2][:, t * P:t * P + P], dupK[:, n, t], ident[:, :])
                last.then_inc(kt_banked, 1)
            pe.wait_ge(kt_saved, 4)
            for t in range(4):
                if t >= 1:
                    pe.wait_ge(co_saved, t)
                for hd in range(QH):
                    half = slice(hd % 2 * 64, hd % 2 * 64 + 64)
                    last = mm(banks[4 * (hd % 2)][:, hd // 2 * 32:hd // 2 * 32 + NCMP_P], qT[half, hd // 2, t * P:t * P + P],
                              kcT_p[half, hd // 8, 0:NCMP_P], start=True, stop=True)
                last.then_inc(cs_banked, 1)
                pe.wait_ge(cs_ready, t + 1)
                for j in range(4):
                    last = tr(banks[1][:, j * P:j * P + P], sc_c[:, 4 * j:4 * j + 4, :].rearrange("p a b -> p (a b)"), ident[:, :])
                last.then_inc(pct_banked, 1)
                pe.wait_ge(pct_saved, t + 1)
                for hd in range(QH):
                    rows = slice(hd % 4 * 32, hd % 4 * 32 + 32)
                    kv = hd // 8
                    last = mm(banks[(2, 3, 5, 6)[hd % 4]][:, hd // 4 * 64:hd // 4 * 64 + 64], PcT[rows, hd // 4], vc_p[rows, kv * 64:kv * 64 + 64],
                              start=True, stop=True)
                last.then_inc(co_banked, 1)
            pe.wait_ge(co_saved, 4)

            def scores(i):
                hd, t = divmod(i, 4)
                if i >= 2:
                    pe.wait_ge(at_max, i - 1)
                half = slice(hd % 2 * 64, hd % 2 * 64 + 64)
                for br in range(2):
                    last = mm(banks[2 * (i % 2) + br][:, 0:(t + 1) * P], qT[half, hd // 2, t * P:t * P + P],
                              KT[half, 2 * br + hd // 8, 0:(t + 1) * P], start=True, stop=True)
                last.then_inc(at_banked, 1)

            def values(i):
                hd, t = divmod(i, 4)
                pe.wait_ge(at_tr_a, i + 1)
                pe.wait_ge(at_tr_v, i + 1)
                if i >= 1:
                    pe.wait_ge(at_done, i)
                for br in range(2):
                    c0 = (br + 1) * 256 + P + hd // 8 * 64
                    for k in range(t + 1):
                        last = mm(banks[6][:, br * 64:br * 64 + 64], PT[i % 2][:, br, k], kvt[:, k, c0:c0 + 64],
                                  start=(k == 0), stop=(k == t))
                last.then_inc(at_o_banked, 1)

            scores(0)
            for i in range(64):
                if i + 1 < 64:
                    scores(i + 1)
                if i >= 1:
                    values(i - 1)
                pe.wait_ge(at_exp, i + 1)
                for br in range(2):
                    for k in range(i % 4 + 1):
                        last = tr(banks[4 + br][:, k * P:k * P + P], sc_p[i % 2][:, br, k * P:k * P + P], ident[:, :])
                last.then_inc(at_tr_banked, 1)
            values(63)

            pe.wait_ge(at_done, 64)
            for m in range(8):
                last = tr(banks[m // 4][0:NS_TOK, m % 4 * P:m % 4 * P + P], qT[:, m, NP_TOK:], ident[:, :])
            last.then_inc(qr_banked, 1)
            pe.wait_ge(qr_saved, 1)
            for g in range(G):
                last = tr(banks[2][:, g * NS_TOK:(g + 1) * NS_TOK], dupK[0:NS_TOK, g // 4, g % 4], ident[0:NS_TOK, 0:NS_TOK])
            for br in range(2):
                last = tr(banks[3][:, br * NS_TOK:(br + 1) * NS_TOK], kvt[0:NS_TOK, 4, (br + 1) * 256:(br + 1) * 256 + P],
                          ident[0:NS_TOK, 0:NS_TOK])
            last.then_inc(qd_banked, 1)
            pe.wait_ge(qd_ready, 1)
            pe.wait_ge(kn_saved, 1)
            pe.wait_ge(dec_in, 16 * 8)
            ktg = 0
            for pair in range(4):
                if pair >= 1:
                    pe.wait_ge(od_saved, 3 * pair)
                for b2 in range(2):
                    half = slice(64 * b2, 64 * b2 + 64)
                    last = mm(banks[0][half, 0:NCMP_S], QD[:, 2 * pair + b2], kcT_s[:, 2 * pair + b2], start=True, stop=True)
                last.then_inc(sd_banked, 1)
                pe.wait_ge(sd_exp, 3 * pair + 1)
                tr(banks[1][0:NCMP_S, 0:P], Ss[:, 0:NCMP_S], ident[:, :]).then_inc(ptd_banked, 1)
                pe.wait_ge(ptd_saved, 6 * pair + 1)
                for b2 in range(2):
                    half = slice(64 * b2, 64 * b2 + 64)
                    last = mm(banks[6][half, 0:P], PTs[0:NCMP_S, 0, half], vc_s[0:NCMP_S, 2 * pair + b2], start=True, stop=True)
                last.then_inc(od_banked, 1)
                mm(banks[2][:, 0:NBLK], PTs[0:NCMP_S, 0], cover[0:NCMP_S], start=True, stop=True).then_inc(imp_banked, 1)
                pe.wait_ge(imp_saved, pair + 1)
                mm(banks[3][:, 0:NBLK], group, imp, start=True, stop=True).then_inc(grp_banked, 1)
                for br in range(2):
                    ntile = (16, 4)[br]
                    nk = ntile * P
                    if br == 0:
                        pe.wait_ge(slc_in, 512 * (pair + 1))
                    else:
                        pe.wait_ge(win_in, 32 * (pair + 1))
                    pe.wait_ge(od_saved, 3 * pair + br + 1)
                    for g in range(2 * ntile // 4):
                        if ktg >= 2:
                            pe.wait_ge(ks_saved, ktg - 1)
                        for j in range(4):
                            last = tr(banks[4 + ktg % 2][:, j * P:j * P + P], slc_raw[:, 4 * g + j, 0:P], ident[:, :])
                        last.then_inc(ks_banked, 1)
                        ktg += 1
                    pe.wait_ge(ks_saved, ktg)
                    pe.wait_ge(sel_ready, pair + 1)
                    for c in range(ntile // 4 + 1):
                        for b2 in range(2):
                            half = slice(64 * b2, 64 * b2 + 64)
                            bb = 2 * pair + b2
                            if c < ntile // 4:
                                last = mm(banks[c % 4][half, :], QD[:, bb], KTs[:, b2, c * 512:c * 512 + 512], start=True, stop=True)
                            else:
                                last = mm(banks[7][half, 0:NS_TOK], QD[:, bb], knT[:, br], start=True, stop=True)
                    last.then_inc(sd_banked, 1)
                    pe.wait_ge(sd_exp, 3 * pair + br + 2)
                    for g in range(ntile // 4):
                        if g >= 2:
                            pe.wait_ge(ptd_saved, 6 * pair + 1 + 4 * br + g - 1)
                        for j in range(4):
                            last = tr(banks[4 + g % 2][:, j * P:j * P + P], Ss[:, (4 * g + j) * P:(4 * g + j + 1) * P], ident[:, :])
                        if g == ntile // 4 - 1:
                            last = tr(banks[7][0:NS_TOK, 0:P], Ss[:, nk:nk + NS_TOK], ident[:, :])
                        last.then_inc(ptd_banked, 1)
                    pe.wait_ge(ptd_saved, 6 * pair + (5, 6)[br])
                    for b2 in range(2):
                        half = slice(64 * b2, 64 * b2 + 64)
                        for j in range(ntile):
                            mm(banks[6][half, 0:P], PTs[:, j, half], slc_raw[:, b2 * ntile + j, P:256], start=(j == 0), stop=False)
                        last = mm(banks[6][half, 0:P], PTs[0:NS_TOK, 16, half], kvt[0:NS_TOK, 4, (br + 1) * 256 + P:(br + 2) * 256],
                                  start=False, stop=True)
                    last.then_inc(od_banked, 1)
            pe.wait_ge(odec_ready, 1)
            for t in range(NTILE):
                _, n = tok(t)
                for half in range(2):
                    i = 2 * t + half
                    if i >= 2:
                        pe.wait_ge(of_ready, i - 1)
                    for k in range(4):
                        last = tr(banks[i % 2][:, k * P:k * P + n], otok[0:n, t, (4 * half + k) * P:(4 * half + k + 1) * P],
                                  ident[0:n, 0:n])
                    last.then_inc(of_banked, 1)

        @block.scalar
        def _(sc):
            actv = nc.scalar.activation
            step = Steps(sc, act_step)
            for n in range(16):
                sc.wait_ge(prj_banked, n + 1)
                dst = qT[:, n] if n < 8 else mgB[:, n - 8]
                for half in range(2):
                    last = actv(dst[:, half * HALF:(half + 1) * HALF], banks[2 * (n % 2) + half][:, 0:HALF], ACT.Copy)
                last.then_inc(prj_saved, 1)
            sc.wait_ge(prj_saved, 16)
            actv(mgB, mgB, ACT.Tanh, scale=0.5)
            actv(gt[:, 0:4], kvt[:, 0:4, 768:816], ACT.Tanh, scale=0.5)
            actv(gt[0:NS_TOK, 4], kvt[0:NS_TOK, 4, 768:816], ACT.Tanh, scale=0.5).then_inc(gt_tanh, 1)
            for g in range(2):
                sc.wait_ge(kvp_banked, g + 1)
                actv(kvT_p[:, :, g * 256:(g + 1) * 256], banks[g][:, :].rearrange("p (s n) -> p s n", s=2), ACT.Copy).then_inc(kvp_saved, 1)
            sc.wait_ge(posr_banked, 1)
            step(actv(posT, banks[2][:, 0:64].rearrange("p (s n) -> p s n", s=2), ACT.Copy), posr_saved)
            sc.wait_ge(posr_banked, 2)
            step(actv(cbias, banks[3][:, 0:2], ACT.Copy), posr_saved)
            sc.wait_ge(q_zeroed, 2)
            sc.wait_ge(hid_banked, 1)
            actv(gk[:, 0:NCMP_P], banks[4][:, 0:NCMP_P], ACT.Gelu_apprx_tanh, bias=cbias[:, 0:1])
            for j in range(4):
                last = actv(gv[:, 32 * j:32 * j + NCMP_P], banks[5][:, 0:NCMP_P], ACT.Gelu_apprx_tanh, bias=cbias[:, 1:2])
            last.then_inc(gelu_done, 1)
            sc.wait_ge(cmpo_banked, 1)
            actv(kcT_p[:, :, 0:NCMP_P], banks[6][:, 0:64].rearrange("p (k n) -> p k n", k=2)[:, :, 0:NCMP_P], ACT.Copy).then_inc(cmpo_saved, 1)
            actv(vc_p, banks[7][:, 0:P], ACT.Copy).then_inc(cmpo_saved, 1)
            for pair in range(4):
                for g in range(0, 16, 2):
                    i = 16 * pair + g
                    sc.wait_ge(pg_banked, i + 1)
                    if g == 0:
                        sc.wait_ge(hid_banked, pair + 1)
                    c0 = g * 256
                    actv(kvT[:, :, c0:c0 + 256], banks[i % 2][:, :].rearrange("p (s n) -> p s n", s=2), ACT.Copy).then_inc(pg_saved[0], 1)
                sc.wait_ge(hid_banked, pair + 2)
                actv(gk, banks[4][:, 0:2 * NCMP_S], ACT.Gelu_apprx_tanh, bias=cbias[:, 0:1])
                actv(gv, banks[5][:, 0:2 * NCMP_S], ACT.Gelu_apprx_tanh, bias=cbias[:, 1:2]).then_inc(gelu_done, 1)
                sc.wait_ge(cmpo_banked, pair + 2)
                actv(kcT_s[:, 2 * pair:2 * pair + 2], banks[6][:, 0:2 * NCMP_S].rearrange("p (b n) -> p b n", b=2), ACT.Copy).then_inc(cmpo_saved, 1)
                actv(vc_s[0:NCMP_S, 2 * pair:2 * pair + 2], banks[7][0:NCMP_S, 0:2 * P].rearrange("p (b n) -> p b n", b=2), ACT.Copy).then_inc(cmpo_saved, 1)
            for n in range(4):
                sc.wait_ge(kt_banked, n + 1)
                actv(KT[:, n], banks[n % 2][:, :], ACT.Copy).then_inc(kt_saved, 1)
            for t in range(4):
                sc.wait_ge(cs_max, t + 1)
                actv(sc_c[:, :, 0:NCMP_P], sc_c[:, :, 0:NCMP_P], ACT.Exp).then_inc(cs_exp, 1)
                sc.wait_ge(pct_banked, t + 1)
                actv(PcT, banks[1][:, :].rearrange("p (j n) -> p j n", j=4), ACT.Copy).then_inc(pct_saved, 1)
                sc.wait_ge(co_banked, t + 1)
                for j in range(4):
                    last = actv(otok[:, t].rearrange("p (a j d) -> p j a d", j=4, d=HD)[:, j],
                                banks[(2, 3, 5, 6)[j]][:, 0:256].rearrange("p (a d) -> p a d", d=HD), ACT.Copy)
                last.then_inc(co_saved, 1)

            def exps(i):
                n = (i % 4 + 1) * P
                sc.wait_ge(at_max, i + 1)
                for br in range(2):
                    last = actv(sc_p[i % 2][:, br, 0:n], sc_p[i % 2][:, br, 0:n], ACT.Exp, bias=ast[i % 2][:, 2 + br:3 + br],
                                accum_out=ast[i % 2][:, 4 + br:5 + br])
                last.then_inc(at_exp, 1)

            exps(0)
            for i in range(64):
                if i + 1 < 64:
                    exps(i + 1)
                sc.wait_ge(at_tr_banked, i + 1)
                if i >= 2:
                    sc.wait_ge(at_o_banked, i - 1)
                n = i % 4 + 1
                actv(PT[i % 2][:, 0, 0:n], banks[4][:, 0:n * P].rearrange("p (k n) -> p k n", n=P), ACT.Copy).then_inc(at_tr_a, 1)

            sc.wait_ge(qr_banked, 1)
            for half in range(2):
                src = banks[half][0:NS_TOK, :].rearrange("p (g d) -> p g d", g=G)
                last = actv(dupK[0:NS_TOK, 0:2].rearrange("p a b c -> p (a b) c")[:, :, half * 64:half * 64 + 64], src, ACT.Copy)
            last.then_inc(qr_saved, 1)
            sc.wait_ge(qd_banked, 1)
            actv(knT, banks[3][:, 0:2 * NS_TOK].rearrange("p (b n) -> p b n", b=2), ACT.Copy).then_inc(kn_saved, 1)
            sc.wait_ge(dec_in, 16 * 8)
            ktg = 0
            for pair in range(4):
                for br in range(-1, 2):
                    job = 3 * pair + br + 1
                    nk = (NCMP_S, PAST + NS_TOK, WIN + NS_TOK)[br + 1]
                    if br >= 0:
                        ntile = (16, 4)[br]
                        for g in range(2 * ntile // 4):
                            sc.wait_ge(ks_banked, ktg + 1)
                            b2, c0 = divmod(4 * g, ntile)
                            actv(KTs[:, b2, c0 * P:c0 * P + 512], banks[4 + ktg % 2][:, :], ACT.Copy).then_inc(ks_saved, 1)
                            ktg += 1
                    sc.wait_ge(sd_max, job + 1)
                    actv(Ss[:, 0:nk], Ss[:, 0:nk], ACT.Exp, bias=sst[:, 1:2], accum_out=sst[:, 2:3]).then_inc(sd_sum, 1)
                    if br < 0:
                        sc.wait_ge(ptd_banked, 6 * pair + 1)
                        actv(PTs[0:NCMP_S, 0], banks[1][0:NCMP_S, 0:P], ACT.Copy).then_inc(ptd_saved, 1)
                        sc.wait_ge(imp_banked, pair + 1)
                        actv(imp, banks[2][:, 0:NBLK], ACT.Copy).then_inc(imp_saved, 1)
                    else:
                        for g in range(ntile // 4):
                            sc.wait_ge(ptd_banked, 6 * pair + 1 + 4 * br + g + 1)
                            last = actv(PTs[:, 4 * g:4 * g + 4], banks[4 + g % 2][:, :].rearrange("p (k n) -> p k n", n=P), ACT.Copy)
                            if g == ntile // 4 - 1:
                                last = actv(PTs[0:NS_TOK, 16], banks[7][0:NS_TOK, 0:P], ACT.Copy)
                            last.then_inc(ptd_saved, 1)

        @block.gpsimd
        def _(pool):
            step = Steps(pool, pool_step)
            for kv in range(2):
                step(nc.gpsimd.memset(W1[kv * 64:kv * 64 + 64, :, :, 64 - kv * 64:128 - kv * 64], 0.0))
            pool.wait_ge(prj_banked, 16)
            for kv in range(2):
                step(nc.gpsimd.memset(W2kd[kv * 64:kv * 64 + 64, 1 - kv], 0.0))
                for wt in (W2k, W2v):
                    step(nc.gpsimd.memset(wt[kv * 64:kv * 64 + 64, 64 - kv * 64:128 - kv * 64], 0.0))
            step(nc.gpsimd.memset(QD, 0.0), q_zeroed)
            step(nc.gpsimd.memset(gv[:, 0:P], 0.0), q_zeroed)
            pool.wait_ge(cmpo_saved, 2 + 8)
            for br in range(2):
                for kv in range(2):
                    c0 = (br + 1) * 256 + kv * 64
                    for half in range(2):
                        step(nc.gpsimd.tensor_copy(dupK[:, 2 * br + kv, :, half * 64:half * 64 + 64], kvt[:, 0:4, c0:c0 + 64]))
            step(nc.gpsimd.memset(sc_c, 0.0), dup_ready)
            pool.wait_ge(att_in, 16 * 3)
            for hd in range(QH):
                if hd >= 2:
                    pool.wait_ge(at_max, 4 * (hd - 1))
                step(nc.gpsimd.tensor_scalar(hbias[:, hd % 2], dist, -8.0 * SLOPES[hd], None, ALU.mult), hb_ready)

        @block.vector
        def _(dve):
            step = Steps(dve, dve_step)
            V = nc.vector
            dve.wait_ge(gt_tanh, 1)
            step(V.tensor_scalar(mgB, mgB, 1.0, 0.5, ALU.add, ALU.mult))
            step(V.tensor_scalar(gt[:, 0:4], gt[:, 0:4], 1.0, 0.5, ALU.add, ALU.mult))
            step(V.tensor_scalar(gt[0:NS_TOK, 4], gt[0:NS_TOK, 4], 1.0, 0.5, ALU.add, ALU.mult), gt_ready)
            for pair in range(4):
                for g in range(1, 16, 2):
                    i = 16 * pair + g
                    dve.wait_ge(pg_banked, i + 1)
                    dve.wait_ge(hid_banked, pair + 1)
                    V.tensor_copy(kvT[:, :, g * 256:g * 256 + 256], banks[i % 2][:, :].rearrange("p (s n) -> p s n", s=2)).then_inc(pg_saved[1], 1)
            dve.wait_ge(dup_ready, 1)
            dve.wait_ge(att_in, 16 * 3)
            g4 = gt.rearrange("p t (h b) -> p t h b", b=3)
            for t in range(4):
                live = sc_c[:, :, 0:NCMP_P]
                wide = lambda v: v.rearrange("p (h o) -> p h o", o=1).to_broadcast([P, QH, NCMP_P])
                dve.wait_ge(cs_banked, t + 1)
                if t >= 1:
                    dve.wait_ge(pct_banked, t)
                for odd in range(2):
                    step(V.scalar_tensor_tensor(live.rearrange("p (h o) c -> p o h c", o=2)[:, odd],
                                                banks[4 * odd][:, 0:256].rearrange("p (h c) -> p h c", c=32)[:, :, 0:NCMP_P], 0.125,
                                                cmp_bias[:, t].rearrange("p (h o) c -> p o h c", o=2)[:, odd], ALU.mult, ALU.add))
                step(V.tensor_reduce(cst[0], live, AX.X, ALU.max))
                step(V.tensor_tensor(live, live, wide(cst[0]), ALU.subtract), cs_max)
                dve.wait_ge(cs_exp, t + 1)
                step(V.tensor_reduce(cst[0], live, AX.X, ALU.add))
                step(V.reciprocal(cst[0], cst[0]))
                step(V.tensor_scalar(cst[0], cst[0], cmp_any[:, t:t + 1], None, ALU.mult))
                step(V.tensor_tensor(cst[0], cst[0], g4[:, t, :, 0], ALU.mult))
                step(V.tensor_tensor(live, live, wide(cst[0]), ALU.mult), cs_ready)
            dve.wait_ge(co_saved, 4)

            def maxima(i):
                hd, t = divmod(i, 4)
                n = (t + 1) * P
                dve.wait_ge(at_banked, i + 1)
                dve.wait_ge(hb_ready, hd + 1)
                for br in range(2):
                    V.tensor_tensor_reduce(out=sc_p[i % 2][:, br, 0:n], in0=banks[2 * (i % 2) + br][:, 0:n],
                                           in1=hbias[:, hd % 2, NP_TOK - n:], scale=0.125, scalar=-3e38, op0=ALU.add, op1=ALU.max,
                                           accum_out=ast[i % 2][:, br:br + 1]).then_inc(at_raw, 1)
                dve.wait_ge(at_raw, 2 * i + 2)
                step(V.tensor_scalar(ast[i % 2][:, 2:4], ast[i % 2][:, 0:2], -1.0, None, ALU.mult), at_max)

            def combine(i):
                hd, t = divmod(i, 4)
                a = ast[i % 2]
                dst = otok[:, t, hd * 64:hd * 64 + 64]
                dve.wait_ge(at_o_banked, i + 1)
                step(V.reciprocal(a[:, 6:8], a[:, 4:6]))
                step(V.tensor_tensor(a[:, 6:8], a[:, 6:8], g4[:, t, hd, 1:3], ALU.mult))
                step(V.scalar_tensor_tensor(dst, banks[6][:, 0:64], a[:, 6:7], dst, ALU.mult, ALU.add))
                step(V.scalar_tensor_tensor(dst, banks[6][:, 64:128], a[:, 7:8], dst, ALU.mult, ALU.add), at_done)

            maxima(0)
            for i in range(64):
                if i >= 1:
                    combine(i - 1)
                if i + 1 < 64:
                    maxima(i + 1)
                dve.wait_ge(at_tr_banked, i + 1)
                if i >= 2:
                    dve.wait_ge(at_o_banked, i - 1)
                n = i % 4 + 1
                step(V.tensor_copy(PT[i % 2][:, 1, 0:n], banks[5][:, 0:n * P].rearrange("p (k n) -> p k n", n=P)), at_tr_v)
            combine(63)

            dve.wait_ge(qd_banked, 1)
            dve.wait_ge(q_zeroed, 2)
            for kv in range(2):
                half = slice(kv * 64, kv * 64 + 64)
                last = V.tensor_copy(QD[half, :, kv * 32:kv * 32 + 32].rearrange("p b (t g) -> p b t g", g=G),
                                     banks[2][half, 0:256].rearrange("p (g b t) -> p b t g", g=G, t=NT))
            step(last, qd_ready)
            dve.wait_ge(dec_in, 16 * 8)
            for pair in range(4):
                for br in range(-1, 2):
                    job = 3 * pair + br + 1
                    nk = (NCMP_S, PAST + NS_TOK, WIN + NS_TOK)[br + 1]
                    dve.wait_ge(sd_banked, job + 1)
                    if br < 0:
                        step(V.scalar_tensor_tensor(Ss[:, 0:NCMP_S], banks[0][:, 0:NCMP_S], 0.125, cmp_bias_s, ALU.mult, ALU.add))
                    else:
                        bias = (slc_bias_s, win_bias_s)[br]
                        for c in range((4, 1)[br]):
                            cs = slice(c * 512, c * 512 + 512)
                            step(V.scalar_tensor_tensor(Ss[:, cs], banks[c][:, :], 0.125, bias[:, cs], ALU.mult, ALU.add))
                        step(V.scalar_tensor_tensor(Ss[:, nk - NS_TOK:nk], banks[7][:, 0:NS_TOK], 0.125, new_bias_s[:, pair], ALU.mult, ALU.add))
                        if br == 0:
                            step(V.tensor_tensor(Ss[:, 0:PAST].rearrange("p (n k) -> p n k", k=64), Ss[:, 0:PAST].rearrange("p (n k) -> p n k", k=64),
                                                 sel[:, 0, 0:32].rearrange("p (n o) -> p n o", o=1).to_broadcast([P, 32, 64]), ALU.add))
                    step(V.tensor_reduce(sst[:, 0:1], Ss[:, 0:nk], AX.X, ALU.max))
                    step(V.tensor_scalar(sst[:, 1:2], sst[:, 0:1], -1.0, None, ALU.mult), sd_max)
                    dve.wait_ge(sd_sum, job + 1)
                    step(V.reciprocal(sst[:, 3:4], sst[:, 2:3]))
                    if br < 0:
                        step(V.tensor_scalar(Ss[:, 0:nk], Ss[:, 0:nk], sst[:, 3:4], None, ALU.mult), sd_exp)
                        step(V.tensor_copy(sst[:, 4:6], kv_rows))
                    else:
                        step(V.tensor_scalar(sst[:, 4:6], kv_rows, sst[:, 3:4], None, ALU.mult), sd_exp)
                    dve.wait_ge(od_banked, job + 1)
                    if job >= 1:
                        dve.wait_ge(od_out, 16 * job)
                    step(V.tensor_scalar(orow, banks[6][:, 0:64], sst[:, 4:5], None, ALU.mult))
                    step(V.scalar_tensor_tensor(orow, banks[6][:, 64:128], sst[:, 5:6], orow, ALU.mult, ALU.add), od_saved)
                    if br < 0:
                        dve.wait_ge(grp_banked, pair + 1)
                        step(V.tensor_tensor(sel[:, 1], banks[3][:, 0:NBLK], forced, ALU.add))
                        step(V.max(sst[:, 8:16], sel[:, 1]))
                        step(V.match_replace(sel[:, 2], sst[:, 8:16], sel[:, 1], -3e38))
                        step(V.max(sst[:, 8:16], sel[:, 2]))
                        step(V.match_replace(sel[:, 1], sst[:, 8:16], sel[:, 2], -3e38))
                        step(V.tensor_scalar(sel[:, 0], sel[:, 1], -1e37, NEG, ALU.is_gt, ALU.mult), sel_ready)
            dve.wait_ge(odec_in, 16 * 24)
            n = NS_TOK
            od = [odec[0:n, br * D:(br + 1) * D].rearrange("p (h d) -> p h d", d=HD) for br in range(3)]
            og = [g4[0:n, 4, :, br:br + 1].to_broadcast([n, QH, HD]) for br in range(3)]
            o4 = otok[0:n, 4].rearrange("p (h d) -> p h d", d=HD)
            step(V.tensor_tensor(o4, od[0], og[0], ALU.mult))
            step(V.tensor_tensor(od[1], od[1], og[1], ALU.mult))
            step(V.tensor_tensor(od[2], od[2], og[2], ALU.mult))
            step(V.tensor_tensor(o4, o4, od[1], ALU.add))
            step(V.tensor_tensor(o4, o4, od[2], ALU.add), odec_ready)
            for t in range(NTILE):
                t0, n = tok(t)
                for half in range(2):
                    i = 2 * t + half
                    ks = slice(4 * half, 4 * half + 4)
                    dve.wait_ge(of_banked, i + 1)
                    step(V.tensor_tensor(mgB[:, ks, t0:t0 + n], banks[i % 2][:, :].rearrange("p (k n) -> p k n", k=4)[:, :, 0:n],
                                         mgB[:, ks, t0:t0 + n], ALU.mult))
                    step(V.tensor_tensor(hT[:, ks, t0:t0 + n], hT[:, ks, t0:t0 + n], mgB[:, ks, t0:t0 + n], ALU.add), of_ready)

        block_ctx.close()
        end_block()

        dve_step = sem("dve_step")
        act_step = sem("act_step")
        d_in = sem("d_in")
        wout_in = sem("wout_in")
        r_in = sem("r_in")
        o_banked = sem("o_banked")
        res_ready = sem("res_ready")
        var_ready = sem("var_ready")
        rstd_ready = sem("rstd_ready")
        x1_ready = sem("x1_ready")
        x1t_banked = sem("x1t_banked")
        x1t_ready = sem("x1t_ready")
        lg_banked = sem("lg_banked")
        sc_exp = sem("sc_exp")
        lg_saved = sem("lg_saved")
        g_final = sem("g_final")
        gt_banked = sem("gt_banked")
        gt_ready = sem("gt_ready")
        we_in0 = sem("we_in0")
        we_in1 = sem("we_in1")
        e_used = sem("e_used")
        gu_banked = sem("gu_banked")
        sg_ready = sem("sg_ready")
        h_ready = sem("h_ready")
        gb_sel = sem("gb_sel")
        gb_banked = sem("gb_banked")
        gb_saved = sem("gb_saved")
        gu_read = sem("gu_read")
        dn_banked = sem("dn_banked")
        dn_added = sem("dn_added")
        y_banked = sem("y_banked")
        out_ready = sem("out_ready")
        out_done = sem("out_done")
        res2 = sem("res2")
        we_in = [we_in0, we_in1]
        yT = hT
        block_ctx = ExitStack()
        block = block_ctx.enter_context(nc.Block())
        ex = [(io["w_exp_gate"][0], io["w_exp_up"][0], io["w_exp_down"][0])]

        @block.sync
        def _(sp):
            sp.dma_start(wout, io["w_out"][0].rearrange("(k p) n -> p k n", p=P)).then_inc(wout_in, 16)
            sp.dma_start(x1[:, 0:4, :], io["x_prompt"][0].rearrange("(t p) d -> p t d", p=P)).then_inc(d_in, 16)
            sp.dma_start(x1[0:NS_TOK, 4, :], io["x_sample"].rearrange("b t d -> (b t) d")).then_inc(d_in, 16)
            for n, name in enumerate(("ln1_g", "ln1_b", "ln2_g", "ln2_b")):
                sp.dma_start(lnw[:, n], io[name].to_broadcast([P, D])).then_inc(d_in, 16)
            sp.dma_start(wr, io["w_router"][0].rearrange("(k p) n -> p k n", p=P)).then_inc(r_in, 16)
            sp.dma_start(brow, io["b_router"].to_broadcast([P, NE])).then_inc(r_in, 16)
            sp.dma_start(before8, io["before8"].rearrange("p (a b) -> p a b", a=G)).then_inc(r_in, 16)
            sp.wait_ge(gt_ready, 2)

            def load(e, slot, gate, up, down):
                sp.dma_start(wge[slot], gate.rearrange("(k p) n -> p k n", p=P)).then_inc(we_in[slot], 16)
                sp.dma_start(wue[slot], up.rearrange("(k p) n -> p k n", p=P)).then_inc(we_in[slot], 16)
                sp.dma_start(wde[slot], down.rearrange("(k p) n -> p k n", p=P)).then_inc(we_in[slot], 16)

            gate, up, down = io["w_exp_gate"][0], io["w_exp_up"][0], io["w_exp_down"][0]
            for slot in range(2):
                load(slot, slot, gate[slot], up[slot], down[slot])
            for e in range(2, NE):
                sp.wait_ge(e_used, e - 1)
                load(e, e % 2, gate[e], up[e], down[e])
            sp.wait_ge(e_used, NE - 1)
            load(NE, 0, io["w_sh_gate"][0], io["w_sh_up"][0], io["w_sh_down"][0])
            for t in range(NTILE):
                sp.wait_ge(out_ready, t + 1)
                dst = io["out0"][0, t * P:(t + 1) * P] if t < 4 else io["out1"].rearrange("b t d -> (b t) d")
                sp.dma_start(dst, x1[0:tok(t)[1], t]).then_inc(out_done, 16)
            sp.wait_ge(out_done, 16 * NTILE)

        @block.tensor
        def _(pe):
            mm, tr = nc.tensor.matmul, nc.tensor.transpose
            pe.wait_ge(wout_in, 16)
            for t in range(NTILE):
                t0, n = tok(t)
                if t >= 2:
                    pe.wait_ge(res_ready, 2 * (t - 1))
                for half in range(2):
                    for k in range(KD):
                        last = mm(banks[2 * (t % 2) + half][0:n, :], hT[:, k, t0:t0 + n], wout[:, k, half * 512:half * 512 + 512],
                                  start=(k == 0), stop=(k == KD - 1))
                last.then_inc(o_banked, 1)
            for t in range(NTILE):
                t0, n = tok(t)
                pe.wait_ge(x1_ready, t + 1)
                for half in range(2):
                    i = 2 * t + half
                    if i >= 2:
                        pe.wait_ge(x1t_ready, i - 1)
                    for k in range(4):
                        last = tr(banks[4 + i % 2][:, k * P:k * P + n], x1[0:n, t, (4 * half + k) * P:(4 * half + k + 1) * P], ident[0:n, 0:n])
                    last.then_inc(x1t_banked, 1)
            pe.wait_ge(x1t_ready, 2 * NTILE)
            pe.wait_ge(r_in, 48)
            for t in range(NTILE):
                t0, n = tok(t)
                for k in range(KD):
                    last = mm(banks[6][0:n, t * NE:(t + 1) * NE], xT[:, k, t0:t0 + n], wr[:, k], start=(k == 0), stop=(k == KD - 1))
            last.then_inc(lg_banked, 1)
            pe.wait_ge(g_final, 1)
            for t in range(NTILE):
                t0, n = tok(t)
                last = tr((banks[7][0:NE, t0:t0 + n] if t < 4 else banks[6][0:NE, 0:n]), G_[0:n, t], ident[0:n, 0:n])
            last.then_inc(gt_banked, 1)
            pe.wait_ge(gt_ready, 2)
            for e in range(NE + 1):
                slot = e % 2
                pe.wait_ge(we_in[slot], 48 * (e // 2 + 1))
                if e < NE:
                    pe.wait_ge(gb_sel, e + 1)
                    if e >= 1:
                        pe.wait_ge(gb_saved, e)
                    for half in range(2):
                        last = mm(banks[4 + half][:, 0:HALF], ones[0:NE, :], gsel[0:NE, half * HALF:(half + 1) * HALF], start=True, stop=True)
                    last.then_inc(gb_banked, 1)
                for f in range(2):
                    i = 2 * e + f
                    if i >= 1:
                        pe.wait_ge(gu_read, i)
                    for n, wt in enumerate((wge, wue)):
                        for half in range(2):
                            for k in range(KD):
                                last = mm(banks[2 * n + half][:, 0:HALF], wt[slot][:, k, f * P:f * P + P],
                                          xT[:, k, half * HALF:(half + 1) * HALF], start=(k == 0), stop=(k == KD - 1))
                        last.then_inc(gu_banked, 1)
                pe.wait_ge(h_ready, e + 1)
                for m in range(KD):
                    for half in range(2):
                        i = 16 * e + 2 * m + half
                        if i >= 2:
                            pe.wait_ge(dn_added, i - 1)
                        for f in range(2):
                            last = mm(banks[6 + half][:, 0:HALF], wde[slot][:, f, m * P:m * P + P], hid[:, f, half * HALF:(half + 1) * HALF],
                                      start=(f == 0), stop=(f == 1))
                        last.then_inc(dn_banked, 1)
            pe.wait_ge(dn_added, 16 * (NE + 1))
            for t in range(NTILE):
                t0, n = tok(t)
                if t >= 2:
                    pe.wait_ge(res2, t - 1)
                for half in range(2):
                    for k in range(4):
                        last = tr(banks[2 * (t % 2) + half][0:n, k * P:(k + 1) * P], yT[:, 4 * half + k, t0:t0 + n], ident[:, :])
                last.then_inc(y_banked, 1)

        @block.scalar
        def _(sc):
            actv = nc.scalar.activation
            step = Steps(sc, act_step)

            def rstd(t, i):
                n = tok(t)[1]
                sc.wait_ge(var_ready, i + 1)
                step(actv(lnst[0:n, 2:3], lnst[0:n, 1:2], ACT.Ln, bias=eps[0:n, 1:2]))
                actv(lnst[0:n, 3:4], lnst[0:n, 2:3], ACT.Exp, scale=-0.5).then_inc(rstd_ready, 1)

            for t in range(NTILE):
                rstd(t, t)
            for t in range(NTILE):
                t0, n = tok(t)
                for half in range(2):
                    i = 2 * t + half
                    sc.wait_ge(x1t_banked, i + 1)
                    actv(xT[:, 4 * half:4 * half + 4, t0:t0 + n], banks[4 + i % 2][:, :].rearrange("p (k n) -> p k n", k=4)[:, :, 0:n],
                         ACT.Copy).then_inc(x1t_ready, 1)
            sc.wait_ge(lg_saved, 1)
            actv(rt[0], rt[0], ACT.Exp, scale=-1.0).then_inc(sc_exp, 1)
            sc.wait_ge(gt_banked, 1)
            actv(GT[0:NE, 0:NP_TOK], banks[7][0:NE, :], ACT.Copy).then_inc(gt_ready, 1)
            actv(GT[0:NE, NP_TOK:], banks[6][0:NE, 0:NS_TOK], ACT.Copy).then_inc(gt_ready, 1)
            for e in range(NE + 1):
                if e < NE:
                    sc.wait_ge(gb_banked, e + 1)
                    if e >= 1:
                        sc.wait_ge(h_ready, e)
                    for half in range(2):
                        last = actv(grow[:, half * HALF:(half + 1) * HALF], banks[4 + half][:, 0:HALF], ACT.Copy)
                    last.then_inc(gb_saved, 1)
                for f in range(2):
                    i = 2 * e + f
                    sc.wait_ge(gu_banked, 2 * i + 1)
                    if i >= 2:
                        sc.wait_ge(gu_read, i - 1)
                    for half in range(2):
                        last = actv(sg[:, f, half * HALF:(half + 1) * HALF], banks[half][:, 0:HALF], ACT.Silu)
                    last.then_inc(sg_ready, 1)
            for t in range(NTILE):
                rstd(t, NTILE + t)

        @block.vector
        def _(dve):
            step = Steps(dve, dve_step)
            V = nc.vector
            dve.wait_ge(d_in, 16 * 6)

            def norm(t, i, gain, done):
                n = tok(t)[1]
                for half in range(2):
                    step(V.bn_stats(bnst[0:n, half], x1[0:n, t, half * 512:half * 512 + 512]))
                step(V.bn_aggr(lnst[0:n, 0:2], bnst[0:n]), var_ready)
                dve.wait_ge(rstd_ready, i + 1)
                step(V.tensor_scalar(x1[0:n, t], x1[0:n, t], lnst[0:n, 0:1], lnst[0:n, 3:4], ALU.subtract, ALU.mult))
                step(V.tensor_tensor(x1[0:n, t], x1[0:n, t], lnw[0:n, gain], ALU.mult))
                step(V.tensor_tensor(x1[0:n, t], x1[0:n, t], lnw[0:n, gain + 1], ALU.add), done)

            for t in range(NTILE):
                n = tok(t)[1]
                dve.wait_ge(o_banked, t + 1)
                for half in range(2):
                    cs = slice(half * 512, half * 512 + 512)
                    step(V.scalar_tensor_tensor(x1[0:n, t, cs], x1[0:n, t, cs], ALPHA, banks[2 * (t % 2) + half][0:n, :], ALU.mult, ALU.add), res_ready)
                norm(t, t, 0, x1_ready)
            dve.wait_ge(lg_banked, 1)
            dve.wait_ge(r_in, 48)
            score, sel_, tmp, tmp2, pre, pre2 = rt
            step(V.memset(score[:, 4], 0.0))
            step(V.tensor_copy(score[:, 0:4], banks[6][:, 0:4 * NE].rearrange("p (t e) -> p t e", e=NE)))
            step(V.tensor_copy(score[0:NS_TOK, 4], banks[6][0:NS_TOK, 4 * NE:5 * NE]), lg_saved)
            dve.wait_ge(sc_exp, 1)
            step(V.tensor_scalar(score, score, 1.0, None, ALU.add))
            step(V.reciprocal(score, score))
            step(V.tensor_tensor(sel_, score, brow.rearrange("p (o e) -> p o e", o=1).to_broadcast([P, NTILE, NE]), ALU.add))
            for t in range(NTILE):
                for g in range(G):
                    last = V.max(m8[:, t, g], sel_[:, t, g * 8:g * 8 + 8])
                    step(last)
            step(V.tensor_tensor(gs, m8[:, :, :, 0], m8[:, :, :, 1], ALU.add))
            wide = gs.rearrange("p t (o i) -> p t o i", o=1).to_broadcast([P, NTILE, G, G])
            tall = gs.rearrange("p t (j o) -> p t j o", o=1).to_broadcast([P, NTILE, G, G])
            step(V.tensor_tensor(gr[0], wide, tall, ALU.is_gt))
            step(V.tensor_tensor(gr[1], wide, tall, ALU.is_equal))
            step(V.tensor_tensor(gr[1], gr[1], before8.rearrange("p (o j) i -> p o j i", o=1).to_broadcast([P, NTILE, G, G]), ALU.mult))
            step(V.tensor_tensor(gr[0], gr[0], gr[1], ALU.add))
            step(V.tensor_reduce(gs, gr[0], AX.X, ALU.add))
            step(V.tensor_scalar(gs, gs, 3.5, NEG, ALU.is_gt, ALU.mult))
            eight = lambda v: v.rearrange("p t (g j) -> p (t g) j", j=8)
            step(V.tensor_tensor(eight(sel_), eight(sel_), gs.rearrange("p t (g o) -> p (t g) o", o=1).to_broadcast([P, NTILE * G, 8]), ALU.add))
            for t in range(NTILE):
                step(V.max(v8[:, t], sel_[:, t]))
            sixth = v8[:, :, TOP_K - 1:TOP_K].to_broadcast([P, NTILE, NE])
            step(V.tensor_tensor(tmp, sel_, sixth, ALU.is_gt))
            step(V.tensor_reduce(cnt, tmp, AX.X, ALU.add))
            step(V.tensor_scalar(cnt, cnt, -1.0, float(TOP_K), ALU.mult, ALU.add))
            step(V.tensor_tensor(tmp2, sel_, sixth, ALU.is_equal))
            step(V.tensor_copy(pre, tmp2))
            for n in range(6):
                sh = 1 << n
                step(V.tensor_copy(pre2[:, :, 0:sh], pre[:, :, 0:sh]))
                step(V.tensor_tensor(pre2[:, :, sh:], pre[:, :, sh:], pre[:, :, 0:NE - sh], ALU.add))
                pre, pre2 = pre2, pre
            step(V.tensor_tensor(pre, pre, cnt.rearrange("p (t o) -> p t o", o=1).to_broadcast([P, NTILE, NE]), ALU.is_le))
            step(V.tensor_tensor(tmp2, tmp2, pre, ALU.mult))
            step(V.tensor_tensor(tmp, tmp, tmp2, ALU.add))
            step(V.tensor_tensor(G_, score, tmp, ALU.mult))
            step(V.tensor_reduce(cnt, G_, AX.X, ALU.add))
            step(V.reciprocal(cnt, cnt))
            step(V.tensor_scalar(cnt, cnt, ROUTED_SCALE, None, ALU.mult))
            step(V.tensor_tensor(G_, G_, cnt.rearrange("p (t o) -> p t o", o=1).to_broadcast([P, NTILE, NE]), ALU.mult), g_final)
            dve.wait_ge(gt_ready, 2)
            step(V.tensor_scalar(gsel[0:NE], GT[0:NE], ident[0:NE, 0:1], None, ALU.mult), gb_sel)
            for e in range(NE + 1):
                for f in range(2):
                    i = 2 * e + f
                    dve.wait_ge(gu_banked, 2 * i + 2)
                    dve.wait_ge(sg_ready, i + 1)
                    if f == 0 and e >= 1:
                        dve.wait_ge(dn_banked, 16 * e)
                    for half in range(2):
                        hs = slice(half * HALF, half * HALF + HALF)
                        last = V.tensor_tensor(hid[:, f, hs], sg[:, f, hs], banks[2 + half][:, 0:HALF], ALU.mult)
                        if half == 0:
                            step(last)
                    step(last, gu_read)
                if e < NE:
                    dve.wait_ge(gb_saved, e + 1)
                    step(V.tensor_tensor(hid, hid, grow.rearrange("p (o n) -> p o n", o=1).to_broadcast([P, 2, NTOK]), ALU.mult), h_ready)
                else:
                    step(V.tensor_scalar(hid, hid, 1.0, None, ALU.mult), h_ready)
                if e + 1 < NE:
                    dve.wait_ge(gb_banked, e + 1)
                    step(V.tensor_scalar(gsel[0:NE], GT[0:NE], ident[0:NE, e + 1:e + 2], None, ALU.mult), gb_sel)
                for m in range(KD):
                    for half in range(2):
                        i = 16 * e + 2 * m + half
                        hs = slice(half * HALF, half * HALF + HALF)
                        dve.wait_ge(dn_banked, i + 1)
                        if e == 0:
                            step(V.tensor_copy(yT[:, m, hs], banks[6 + half][:, 0:HALF]), dn_added)
                        else:
                            step(V.tensor_tensor(yT[:, m, hs], yT[:, m, hs], banks[6 + half][:, 0:HALF], ALU.add), dn_added)
                step(V.memset(bnst[:, 0, 0:1], 0.0), e_used)
            for t in range(NTILE):
                n = tok(t)[1]
                dve.wait_ge(y_banked, t + 1)
                for half in range(2):
                    cs = slice(half * 512, half * 512 + 512)
                    step(V.scalar_tensor_tensor(x1[0:n, t, cs], x1[0:n, t, cs], ALPHA, banks[2 * (t % 2) + half][0:n, :], ALU.mult, ALU.add),
                         res2 if half else None)
                norm(t, NTILE + t, 2, out_ready)

        block_ctx.close()
        end_block()


INS = ["x_prompt", "x_sample", "cache_cmp_kv", "cache_slc_kv", "cache_win_kv", "state_delta_S", "state_delta_conv",
       "page_table", "w_in", "dn_conv_w", "dn_A_log", "dn_dt_bias", "dn_norm_w", "nsa_cmp_w1", "nsa_cmp_pos", "nsa_cmp_w2",
       "w_out", "ln1_g", "ln1_b", "w_router", "b_router", "w_exp_gate", "w_exp_up", "w_exp_down",
       "w_sh_gate", "w_sh_up", "w_sh_down", "ln2_g", "ln2_b"]
KV = (2, KVH, HD)
OUTS = [(1, NP_TOK, D), (NB, NT, D),
        (1, 1, NP_TOK) + KV, (1, 1, NP_TOK) + KV, (1, 1, WIN) + KV, (1, 1, H, DH, DH), (1, 1, 3, CH),
        (1, NB, NT) + KV, (1, NB, NT) + KV, (1, NB, WIN) + KV, (1, NB, H, DH, DH), (1, NB, 3, CH)]


def kernel(**inputs):
    import concourse.bacc as bacc
    from concourse.bass_utils import run_bass_kernel_spmd

    nc = bacc.Bacc("TRN2", target_bir_lowering=False, num_devices=1)
    arrays, io = {}, {}
    named = {n: np.ascontiguousarray(inputs[n]) for n in INS}
    named.update(shape_constants())
    for name, v in named.items():
        arrays[f"in_{name}"] = v
        io[name] = nc.dram_tensor(f"in_{name}", v.shape, mybir.dt.from_np(v.dtype), kind="ExternalInput").ap()
    for i, shape in enumerate(OUTS):
        io[f"out{i}"] = nc.dram_tensor(f"out_{i}", shape, mybir.dt.float32, kind="ExternalOutput").ap()
    build(nc, io)
    r = run_bass_kernel_spmd(nc, [arrays], core_ids=[0])
    return tuple(r.results[0][f"out_{i}"] for i in range(len(OUTS)))
```

```python
from contextlib import ExitStack

import numpy as np
import concourse.bass as bass
from concourse import mybir

D = 1024
NP_TOK = 512
NB, NT = 8, 4
NS_TOK = NB * NT
NTOK = NP_TOK + NS_TOK
PAST, PAGE, NPOOL = 2048, 128, 160
NPG = PAST // PAGE
H, DH = 8, 128
CH = 3 * H * DH
QH, KVH, G, HD = 16, 2, 8, 64
WIN = 512
NE, DE = 64, 256
ALPHA = 2.0 ** 0.25
NEG = -1e30
P = 128
KD = D // P
NTILE = 5
HALF = NTOK // 2
C = 128
NCH = NP_TOK // C
LEVELS = 7
RAWW = 3 + NP_TOK + NB * 7
SROW = 3 + NP_TOK
NCMP_P = 31
NCMP_S = 127
NBLK = 33
TOP_K = 6
ROUTED_SCALE = 2.5
ARENA = 37400
RING = 6
COL_QKV, COL_Z, COL_AB, COL_NQ, COL_KV, COL_NG, COL_MG = 0, 3072, 4096, 4112, 5136, 5904, 5952
KVW = COL_MG - COL_KV


def shape_constants():
    f = np.float32
    i = np.arange(P)
    c = {}
    c["ident"] = np.eye(P, dtype=f)
    c["tri"] = (i[:, None] <= i[None, :]).astype(f)
    s = np.arange(NS_TOK)
    same = (s[:, None] // NT) == (s[None, :] // NT)
    c["tri_s"] = (same & (s[:, None] <= s[None, :])).astype(f)
    c["same_s"] = same.astype(f)
    c["causal_t"] = np.where(i[:, None] <= i[None, :], 0, NEG).astype(f)
    c["causal_ts"] = np.where(same & (s[:, None] <= s[None, :]), 0, NEG).astype(f)
    lev = []
    for n in range(LEVELS):
        w = 1 << n
        m = (i[:, None] // (2 * w) == i[None, :] // (2 * w)) & (i[:, None] % (2 * w) >= w) & (i[None, :] % (2 * w) < w)
        lev.append(m.T.astype(f))
    c["levels"] = np.stack(lev, 1).reshape(P, LEVELS * P)
    c["rows_s"] = (s[:, None] // NT == np.arange(NB)[None, :]).astype(f)
    slope = (2.0 ** (-8.0 * np.arange(1, QH + 1, dtype=f) / QH)).astype(f)
    m = np.arange(NP_TOK)
    dist = i[:, None] - (m[None, :] - 384)
    c["dist"] = np.where(dist >= 0, dist, 1e32).astype(f)
    tq = np.arange(NP_TOK).reshape(4, P)
    c_end = np.arange(NCMP_S) * 16 + 31
    ok = c_end[None, None, :NCMP_P] <= tq[:, :, None]
    bias = -slope[None, None, :, None] * (tq[:, :, None, None] - c_end[None, None, None, :NCMP_P]).astype(f)
    bias = np.where(ok[:, :, None, :], bias, NEG)
    c["cmp_bias"] = bias.transpose(1, 0, 2, 3).reshape(P, 4 * QH * NCMP_P).astype(f)
    c["cmp_any"] = ok.any(-1).T.astype(f)
    row = np.arange(P)
    rb, rh, rt, rg = row // 64, row // 32 % 2, row // 8 % 4, row % 8
    rs, rq = slope[rh * 8 + rg][:, None], (PAST + rt)[:, None]
    c["cmp_bias_s"] = (-rs * (rq - c_end[None, :]).astype(f)).astype(f)
    key = np.arange(PAST)
    c["slc_bias_s"] = (-rs * (rq - key[None, :]).astype(f)).astype(f)
    wk = PAST - WIN + np.arange(WIN)
    c["win_bias_s"] = np.where(rq - wk[None, :] < WIN, -rs * (rq - wk[None, :]).astype(f), NEG).astype(f)
    nk = np.arange(NS_TOK)
    new = []
    for pair in range(4):
        mine = (nk[None, :] // NT == 2 * pair + rb[:, None]) & (nk[None, :] % NT <= rt[:, None])
        new.append(np.where(mine, -rs * (rt[:, None] - nk[None, :] % NT).astype(f), NEG))
    c["new_bias_s"] = np.stack(new, 1).reshape(P, 4 * NS_TOK).astype(f)
    blk = np.arange(NBLK)
    c["cover"] = ((c_end[:, None] - 31 < blk[None, :] * 64 + 64) & (c_end[:, None] >= blk[None, :] * 64)).astype(f)
    c["forced"] = np.broadcast_to(np.where((blk == 0) | (blk >= NBLK - 2), 1e6, 0.0), (P, NBLK)).astype(f)
    c["group"] = (row[:, None] // 8 == row[None, :] // 8).astype(f)
    c["kv_rows"] = np.stack([rh == 0, rh == 1], 1).astype(f)
    gi = np.arange(8)
    t = np.arange(NTILE)[None, :] * P + i[:, None]
    c["tokens"] = np.stack([t + 1, t * TOP_K], 2).reshape(P, NTILE * 2).astype(f)
    c["slots"] = np.broadcast_to(i, (P, P)).astype(f)
    c["before8"] = np.broadcast_to((gi[None, :] < gi[:, None]).reshape(1, 64), (P, 64)).astype(f)
    return c


SLOPES = [2.0 ** (-(j + 1) / 2.0) for j in range(QH)]


def build(nc, io):
    fp32 = mybir.dt.float32
    ALU = mybir.AluOpType
    ACT = mybir.ActivationFunctionType
    AX = mybir.AxisListType
    ctx = ExitStack()
    with ctx:
        def sb(name, shape, dt=fp32):
            return ctx.enter_context(nc.sbuf_tensor(name, shape, dt))

        def sem(name):
            taken.append(nc.alloc_semaphore(name=f"{name}_{stage[0]}"))
            return taken[-1]

        taken, stage = [], [0]

        def end_block():
            nc.clear_and_free_semaphores(list(taken))
            nc.all_engine_barrier()
            taken.clear()
            stage[0] += 1

        def width(shape):
            n = 1
            for k in shape:
                n *= k
            return n

        def shaped(ap, shape):
            if len(shape) == 2:
                return ap.rearrange("p (a b) -> p a b", a=shape[0])
            if len(shape) == 3:
                return ap.rearrange("p (a b c) -> p a b c", a=shape[0], b=shape[1])
            return ap

        xT = sb("xT", [P, KD, NTOK])
        hT = sb("hT", [P, KD, NTOK])
        kvt = sb("kvt", [P, NTILE, KVW])
        ident = sb("ident", [P, P])
        ones = sb("ones", [P, P])
        tri = sb("tri", [P, P])
        tri_s = sb("tri_s", [NS_TOK, NS_TOK])
        same_s = sb("same_s", [NS_TOK, NS_TOK])
        causal_t = sb("causal_t", [P, P])
        causal_ts = sb("causal_ts", [NS_TOK, NS_TOK])
        rows_s = sb("rows_s", [NS_TOK, NB])
        ab = sb("ab", [P, NTILE, 16])
        eps = sb("eps", [P, 2])
        arena = sb("arena", [P, ARENA])
        banks = [ctx.enter_context(nc.psum_tensor(f"bank{i}", [P, 512], fp32)) for i in range(8)]

        class Carve:
            def __init__(self):
                self.at = 0

            def __call__(self, *shape):
                n = width(shape)
                ap = arena[:, self.at:self.at + n]
                self.at += n
                assert self.at <= ARENA, self.at
                return shaped(ap, shape)

        a = Carve()
        xrow = a(NTILE, D)
        wkv = a(KD, KVW + 16)
        b = Carve()
        b.at = ARENA - RING * D
        wh = [b(KD, P) for _ in range(RING)]
        b.at = 0
        levels = b(LEVELS, P)
        raw = [b(3, RAWW), b(3, RAWW)]
        zm = [b(2, NTOK), b(2, NTOK)]
        convw = b(96)
        conv_rows = [b(3, P), b(3, P)]
        conv_out = [b(3, P), b(3, P)]
        normw = b(1)
        y = b(3, RAWW - 3)
        ey = b(3, RAWW - 3)
        act = b(3, NTOK)
        sq = b(2, NTOK)
        rn = b(2, NTOK)
        gb = b(2, NTILE, P)
        kbT = b(NTOK)
        eg = b(NTOK)
        qgT = b(NTOK)
        dec = b(NTILE, P)
        kbg = b(NTILE, P)
        kdec = b(NTILE, P)
        kdec8 = b(NB, P)
        vb = b(NTILE, P)
        LT = b(NTILE, P)
        AT = b(NTILE, P)
        MT = b(NCH, P)
        T = b(NTILE, P)
        U = b(NTILE, P)
        Y = b(NTILE, P)
        nwT = b(NCH, P)
        nw8 = b(NB * 36)
        vn = b(NTILE, P)
        S = [b(P), b(P)]
        Sb = b(NB, P)
        Sn = b(NB, P)
        oT = b(NTOK)
        sgz = b(2, NTOK)
        cg = b(3, 27)
        assert b.at <= ARENA - RING * D, b.at
        q = Carve()
        qT = q(8, NTOK)
        mgB = q(8, NTOK)
        otok = q(NTILE, D)
        gt = q(NTILE, QH * 3)
        kcT_s = q(NB, NCMP_S)
        vc_s = q(NB, P)
        kcT_p = q(2, 32)
        vc_p = q(P)
        knT = q(2, NS_TOK)
        QD = q(NB, 64)
        small = q(64)
        keep = q.at
        W1 = q(2, 32, P)
        pages = q(8, 256)
        kvT = q(2, 2 * PAST)
        kvT_p = kvT[:, :, 0:NP_TOK]
        posT = q(2, 32)
        pos_rows = q(2, P)
        W2k = q(P)
        W2v = q(P)
        W2kd = q(2, P)
        gk = q(2 * NCMP_S)
        gv = q(2 * NCMP_S)
        cbias = q(2)
        assert q.at <= ARENA
        q.at = keep
        dupK = q(4, 4, P)
        KT = q(4, NP_TOK)
        dist = q(NP_TOK)
        hbias = q(2, NP_TOK)
        sc_p = [q(2, NP_TOK), q(2, NP_TOK)]
        PT = [q(2, 4, P), q(2, 4, P)]
        cmp_bias = q(4, QH, NCMP_P)
        cmp_any = q(4)
        sc_c = q(QH, 32)
        PcT = q(4, P)
        qd_rows = q(D)
        cst = [q(QH), q(QH)]
        ast = [q(8) for _ in range(4)]
        assert q.at <= ARENA
        q.at = keep
        win_raw = q(4, 8, 256)
        flat = [v.rearrange("p k n -> p (k n)") for v in (xT, qT)]
        slc_raw = [[v[:, 0:NPG * 256].rearrange("p (t c) -> p t c", c=256) for v in flat],
                   [win_raw[:, 2 * b2:2 * b2 + 2].rearrange("p a t c -> p (a t) c") for b2 in range(2)]]
        KTs = q(2, PAST)
        Ss = q(PAST + NS_TOK)
        PTs = q(17, P)
        slc_bias_s = q(PAST)
        win_bias_s = q(WIN)
        new_bias_s = q(4, NS_TOK)
        cmp_bias_s = q(NCMP_S)
        cover = q(NBLK)
        forced = q(NBLK)
        group = q(P)
        kv_rows = q(2)
        sel = q(3, NBLK)
        kept = q(4, NBLK)
        sst = q(32)
        orow = q(HD)
        imp = q(NBLK)
        assert q.at <= ARENA, q.at
        odec = slc_raw[1][0][:, 0:12, :].rearrange("p a b -> p (a b)")
        SAMPLE_JOBS = [(pair, br) for pair in range(4) for br in (-1, 1)] + [(pair, 0) for pair in range(4)]

        d = Carve()
        d.at = KD * NTOK
        x1 = d(NTILE, D)
        lnw = d(4, D)
        R = d(NTILE, 3, NE)
        pos = d(NTILE, NE)
        slots = d(P)
        bnst = d(2, 6)
        lnst = d(4)
        keep_d = d.at
        wout = [v[:, 0:KD // 2 * D].rearrange("p (k n) -> p k n", n=D) for v in flat]
        wr = d(KD, NE)
        brow = d(NE)
        tokens = d(NTILE, 2)
        before8 = d(G, G)
        rt = [d(NTILE, NE) for _ in range(6)]
        m8 = d(NTILE, G, 8)
        gs = d(NTILE, G)
        gr = [d(NTILE, G, G) for _ in range(2)]
        v8 = d(NTILE, 8)
        cnt = d(NTILE)
        shgu = d(KD, 2 * DE)
        shd = d(2, D)
        shs = [d(DE) for _ in range(3)]
        assert d.at <= ARENA
        d.at = keep_d
        wgu = [d(KD, 2 * DE), d(KD, 2 * DE)]
        wde = [d(2, D), d(2, D)]
        onehot = [d(NTILE, P), d(NTILE, P)]
        xg = [d(D), d(D)]
        xgT = d(KD, P)
        sg = d(DE)
        hid = d(DE)
        hidT = d(2, P)
        ys = [d(D), d(D)]
        lgate = d(4, 1)
        lempty = d(4, 2)
        assert d.at <= ARENA
        d.at = keep_d
        y6 = [d(TOP_K, D), d(TOP_K, D)]
        assert d.at <= ARENA
        rows_i = sb("rows_i", [P, 4, 2], mybir.dt.int32)
        over_i = sb("over_i", [1, 1], mybir.dt.int32)
        x1_rows = nc.dram_tensor("x1_rows", (NTOK, D), fp32).ap()
        y_rows = nc.dram_tensor("y_rows", (NTOK * TOP_K, D), fp32).ap()

        tk = {n: sb(n, [P, NTILE, H]) for n in ("beta", "gg", "gcum", "bg", "kd", "glast", "hbeta", "tmpa", "tmpb", "tmpc")}
        hb = sb("hb", [P, 2, H])

        page_ids = sb("page_ids", [1, NB * NPG], mybir.dt.int32)
        o_scratch = nc.dram_tensor("o_scratch", (3, NB, 2, NT, G * HD), fp32).ap()

        class Steps:
            def __init__(self, eng, own):
                self.eng, self.own, self.n = eng, own, {}

            def __call__(self, ins, signal=None):
                s = signal if signal is not None else self.own
                k = id(s)
                self.n[k] = self.n.get(k, 0) + 1
                ins.then_inc(s, 1)
                self.eng.wait_ge(s, self.n[k])

        def tok(t):
            return (t * P, P if t < 4 else NS_TOK)

        consts_in = sem("consts_in")
        x_in = sem("x_in")
        wkv_in = sem("wkv_in")
        misc_in = sem("misc_in")
        b_in = sem("b_in")
        dve_step = sem("dve_step")
        act_step = sem("act_step")
        zeroed = sem("zeroed")
        xt_banked = sem("xt_banked")
        xt_ready = sem("xt_ready")
        kv_banked = sem("kv_banked")
        kv_ready = sem("kv_ready")
        kv_out = sem("kv_out")
        g_ready = sem("g_ready")
        gcum_banked = sem("gcum_banked")
        tk_ready = sem("tk_ready")
        cw_banked = sem("cw_banked")
        cw_ready = sem("cw_ready")
        wh_in = [sem(f"wh_in{i}") for i in range(RING)]
        rows_in = [sem("rows_in0"), sem("rows_in1")]
        sb_in = sem("sb_in")
        pr_banked = sem("pr_banked")
        pr_saved = sem("pr_saved")
        conv_done = sem("conv_done")
        zm_done = sem("zm_done")
        cg_ready = sem("cg_ready")
        cg_banked = sem("cg_banked")
        cg_saved = sem("cg_saved")
        ey_ready = sem("ey_ready")
        rn_ready = sem("rn_ready")
        y_ready = sem("y_ready")
        act_ready = sem("act_ready")
        sq_ready = sem("sq_ready")
        ss_banked = sem("ss_banked")
        qk_ready = sem("qk_ready")
        gb_ready = sem("gb_ready")
        bc_banked = sem("bc_banked")
        eg_ready = sem("eg_ready")
        diff_ready = sem("diff_ready")
        dec_ready = sem("dec_ready")
        kb_ready = sem("kb_ready")
        tok_banked = sem("tok_banked")
        tok_ready = sem("tok_ready")
        prod_banked = sem("prod_banked")
        lt_ready = sem("lt_ready")
        u_ready = sem("u_ready")
        t_banked = sem("t_banked")
        t_ready = sem("t_ready")
        mt_ready = sem("mt_ready")
        y_banked = sem("y_banked")
        y_saved = sem("y_saved")
        tu_banked = sem("tu_banked")
        tu_ready = sem("tu_ready")
        w_banked = sem("w_banked")
        w_ready = sem("w_ready")
        vn_banked = sem("vn_banked")
        vn_ready = sem("vn_ready")
        s_banked = sem("s_banked")
        s_ready = sem("s_ready")
        vns_banked = sem("vns_banked")
        vns_ready = sem("vns_ready")
        ss_new_banked = sem("ss_new_banked")
        sn_final = sem("sn_final")
        s_out = sem("s_out")
        sn_out = sem("sn_out")
        o_banked = sem("o_banked")
        o_saved = sem("o_saved")
        osq_ready = sem("osq_ready")
        oss_banked = sem("oss_banked")
        ez_ready = sem("ez_ready")
        h_ready = sem("h_ready")
        conv_sent = [sem("conv_sent0"), sem("conv_sent1")]
        UNIT = (0, 1, 2, 4, 5)
        block_ctx = ExitStack()
        block = block_ctx.enter_context(nc.Block())

        @block.sync
        def _(sp):
            for t, (name, dst) in enumerate((("ident", ident[:, :]), ("tri", tri[:, :]), ("tri_s", tri_s[:, :]),
                                             ("same_s", same_s[:, :]), ("causal_t", causal_t[:, :]),
                                             ("causal_ts", causal_ts[:, :]), ("rows_s", rows_s[:, :]))):
                sp.dma_start(dst, io[name]).then_inc(consts_in, 16)
            sp.dma_start(xrow[:, 0:4, :], io["x_prompt"][0].rearrange("(t p) d -> p t d", p=P)).then_inc(x_in, 16)
            sp.dma_start(xrow[0:NS_TOK, 4, :], io["x_sample"].rearrange("b t d -> (b t) d")).then_inc(x_in, 16)
            w = io["w_in"][0].rearrange("(k p) n -> p k n", p=P)
            sp.dma_start(wkv[:, :, 0:KVW], w[:, :, COL_KV:COL_MG]).then_inc(wkv_in, 16)
            sp.dma_start(wkv[:, :, KVW:KVW + 16], w[:, :, COL_AB:COL_AB + 16]).then_inc(wkv_in, 16)
            sp.dma_start(hb[:, 0, :], io["dn_dt_bias"][0:1, :].to_broadcast([P, H])).then_inc(misc_in, 16)
            sp.dma_start(hb[:, 1, :], io["dn_A_log"][0:1, :].to_broadcast([P, H])).then_inc(misc_in, 16)
            sp.wait_ge(kv_ready, 2 * NTILE)
            for n in range(3):
                cols = slice(n * 256, n * 256 + 256)
                dst = io[("out2", "out3", "out4")[n]][0, 0].rearrange("(t p) s h d -> p t (s h d)", p=P)
                sp.dma_start(dst, kvt[:, 0:4, cols]).then_inc(kv_out, 16)
                rows = kvt[0:NS_TOK, 4, cols]
                if n < 2:
                    dst = io[("out7", "out8")[n]][0].rearrange("b t s h d -> (b t) (s h d)")
                    sp.dma_start(dst, rows).then_inc(kv_out, 16)
                else:
                    for bb in range(NB):
                        sp.dma_start(io["out9"][0, bb, WIN - NT:WIN].rearrange("t s h d -> t (s h d)"),
                                     kvt[bb * NT:bb * NT + NT, 4, cols]).then_inc(kv_out, 16)
            for bb in range(NB):
                sp.dma_start(io["out9"][0, bb, 0:WIN - NT].rearrange("t s h d -> t (s h d)"),
                             io["cache_win_kv"][0, bb, NT:WIN].rearrange("t s h d -> t (s h d)")).then_inc(kv_out, 16)
            sp.wait_ge(xt_ready, 2 * NTILE)
            sp.dma_start(levels, io["levels"].rearrange("p (l i) -> p l i", l=LEVELS)).then_inc(b_in, 16)
            sp.dma_start(normw, io["dn_norm_w"][0].rearrange("(p o) -> p o", o=1)).then_inc(b_in, 16)
            sp.dma_start(y[0:96, 0, 0:P], io["dn_conv_w"][0].rearrange("j (c p) -> (j c) p", p=P)).then_inc(b_in, 16)
            blocks = [COL_QKV, COL_QKV + D, COL_QKV + 2 * D, COL_Z, COL_MG]

            def load_head(h):
                for n, c0 in enumerate(blocks):
                    i = 5 * h + n
                    if i >= RING:
                        done_h, m = divmod(i - RING, 5)
                        sp.wait_ge(pr_banked, 6 * done_h + UNIT[m] + 1)
                    sp.dma_start(wh[i % RING], w[:, :, c0 + h * P:c0 + h * P + P]).then_inc(wh_in[i % RING], 16)
                if h >= 2:
                    sp.wait_ge(pr_banked, 6 * (h - 1))
                sp.dma_start(conv_rows[h % 2][0:24],
                             io["state_delta_conv"][0].rearrange("b r (n c) -> (b r) n c", n=3)[:, :, h * P:h * P + P]
                             ).then_inc(rows_in[h % 2], 16)

            load_head(0)
            load_head(1)
            for h in range(H):
                if h >= 1:
                    sp.wait_ge(sn_final, h)
                sp.dma_start(Sb, io["state_delta_S"][0, :, h].rearrange("b d e -> d b e")).then_inc(sb_in, 16)
                sp.wait_ge(cg_saved, h + 1)
                co = conv_out[h % 2]
                hs = slice(h * P, h * P + P)
                sp.dma_start(io["out6"][0, 0].rearrange("r (n c) -> r n c", n=3)[:, :, hs], co[0:3]).then_inc(conv_sent[h % 2], 16)
                sp.dma_start(io["out11"][0].rearrange("b r (n c) -> (b r) n c", n=3)[:, :, hs], co[3:27]).then_inc(conv_sent[h % 2], 16)
                if h + 2 < H:
                    load_head(h + 2)
                sp.wait_ge(s_ready, (h + 1) * (NCH + 1))
                sp.dma_start(io["out5"][0, 0, h], S[NCH % 2]).then_inc(s_out, 16)
                sp.wait_ge(sn_final, h + 1)
                sp.dma_start(io["out10"][0, :, h].rearrange("b d e -> d b e"), Sn).then_inc(sn_out, 16)
            sp.wait_ge(conv_sent[0], 16 * H)
            sp.wait_ge(conv_sent[1], 16 * H)
            sp.wait_ge(s_out, 16 * H)
            sp.wait_ge(sn_out, 16 * H)
            sp.wait_ge(kv_out, 16 * (5 + 2 * NB))

        @block.tensor
        def _(pe):
            mm, tr = nc.tensor.matmul, nc.tensor.transpose
            pe.wait_ge(consts_in, 16 * 7)
            pe.wait_ge(x_in, 32)
            for t in range(NTILE):
                _, n = tok(t)
                for half in range(2):
                    i = 2 * t + half
                    if i >= 2:
                        pe.wait_ge(xt_ready, i - 1)
                    for k in range(4):
                        last = tr(banks[i % 2][:, k * P:k * P + n], xrow[0:n, t, (4 * half + k) * P:(4 * half + k + 1) * P],
                                  ident[0:n, 0:n])
                    last.then_inc(xt_banked, 1)
            pe.wait_ge(xt_ready, 2 * NTILE)
            pe.wait_ge(wkv_in, 32)
            for t in range(NTILE):
                t0, n = tok(t)
                for half, (c0, c1) in enumerate(((0, 512), (512, KVW + 16))):
                    i = 2 * t + half
                    if i >= 2:
                        pe.wait_ge(kv_ready, i - 1)
                    for k in range(KD):
                        last = mm(banks[2 + i % 2][0:n, 0:c1 - c0], xT[:, k, t0:t0 + n], wkv[:, k, c0:c1],
                                  start=(k == 0), stop=(k == KD - 1))
                    last.then_inc(kv_banked, 1)
            pe.wait_ge(zeroed, 1)
            pe.wait_ge(g_ready, 1)
            gview = tk["gg"]
            mm(banks[4][:, 0:32], tri[:, :], gview[:, 0:4, :], start=True, stop=True)
            mm(banks[4][:, 32:64], ones[:, :], gview[:, 0:4, :], start=True, stop=True)
            mm(banks[4][0:NS_TOK, 64:72], tri_s[:, :], gview[0:NS_TOK, 4, :], start=True, stop=True)
            mm(banks[4][0:NS_TOK, 72:80], same_s[:, :], gview[0:NS_TOK, 4, :], start=True, stop=True).then_inc(gcum_banked, 1)
            pe.wait_ge(b_in, 16 * 3)
            tr(banks[5][:, 0:96], y[0:96, 0, 0:P], ident[0:96, 0:96]).then_inc(cw_banked, 1)

            def part(h, j):
                if h == H:
                    return
                n, quarter = divmod(j, 4)
                half, k0 = quarter // 2, quarter % 2 * 4
                i = 6 * h + UNIT[n]
                blk = 5 * h + n
                if quarter == 0:
                    pe.wait_ge(wh_in[blk % RING], 16 * (blk // RING + 1))
                    if i >= 2:
                        pe.wait_ge(pr_saved, i - 1)
                for k in range(k0, k0 + 4):
                    last = mm(banks[2 * (i % 2) + half][:, 0:HALF], wh[blk % RING][:, k, :],
                              xT[:, k, half * HALF:(half + 1) * HALF], start=(k == 0), stop=(k == KD - 1))
                if quarter == 3:
                    last.then_inc(pr_banked, 1)

            def history(h):
                if h == H:
                    return
                i = 6 * h + 3
                pe.wait_ge(rows_in[h % 2], 16 * (h // 2 + 1))
                if i >= 2:
                    pe.wait_ge(pr_saved, i - 1)
                for n in range(3):
                    last = tr(banks[2 * (i % 2)][:, n * 24:(n + 1) * 24], conv_rows[h % 2][0:24, n], ident[0:24, 0:24])
                last.then_inc(pr_banked, 1)

            def delta(h):
                b4, b5, b6, b7 = banks[4], banks[5], banks[6], banks[7]
                S0 = NP_TOK
                part(h + 1, 0)
                part(h + 1, 1)
                if h >= 1:
                    pe.wait_ge(sn_final, h)
                    pe.wait_ge(rn_ready, 2 * h)
                pe.wait_ge(cg_ready, h + 1)
                for n in range(3):
                    last = tr(b7[0:27, n * P:(n + 1) * P], cg[:, n, :], ident[:, :])
                last.then_inc(cg_banked, 1)
                pe.wait_ge(sq_ready, h + 1)
                mm(b4[:, :], ones[:, :], sq[:, 0, 0:S0], start=True, stop=True)
                mm(b5[:, :], ones[:, :], sq[:, 1, 0:S0], start=True, stop=True)
                mm(b6[:, 0:32], ones[:, :], sq[:, 0, S0:], start=True, stop=True)
                mm(b6[:, 32:64], ones[:, :], sq[:, 1, S0:], start=True, stop=True).then_inc(ss_banked, 1)
                part(h + 1, 2)
                part(h + 1, 3)
                pe.wait_ge(gb_ready, h + 1)
                pe.wait_ge(qk_ready, h + 1)
                for c in range(NCH):
                    mm(b4[:, c * P:(c + 1) * P], gb[:, 0, c], ident[:, :], start=True, stop=True)
                for c in range(NCH):
                    mm(b5[:, c * P:(c + 1) * P], gb[:, 1, c], tri[:, :], start=True, stop=True)
                mm(b6[:, 0:32], gb[0:32, 0, 4], ident[0:32, 0:32], start=True, stop=True)
                mm(b6[:, 32:64], gb[0:32, 1, 4], tri_s[:, :], start=True, stop=True).then_inc(bc_banked, 1)
                part(h + 1, 4)
                part(h + 1, 5)
                pe.wait_ge(cg_saved, h + 1)
                for c in range(NCH):
                    tr(b7[:, c * P:(c + 1) * P], act[:, 1, c * P:(c + 1) * P], ident[:, :])
                pe.wait_ge(kb_ready, h + 1)
                pe.wait_ge(diff_ready, h + 1)
                pe.wait_ge(eg_ready, h + 1)
                for c in range(NCH):
                    tr(b4[:, c * P:(c + 1) * P], act[:, 2, c * P:(c + 1) * P], ident[:, :])
                tr(b6[0:32, 0:P], act[:, 1, S0:], ident[:, :])
                tr(b6[0:32, P:2 * P], act[:, 2, S0:], ident[:, :]).then_inc(tok_banked, 1)
                for c in range(NCH):
                    cs = slice(c * P, (c + 1) * P)
                    mm(b5[:, cs], act[:, 1, cs], kbT[:, cs], start=True, stop=True)
                part(h + 1, 6)
                part(h + 1, 7)
                pe.wait_ge(tok_ready, h + 1)
                for c in range(NCH):
                    cs = slice(c * P, (c + 1) * P)
                    mm(b7[:, cs], act[:, 1, cs], act[:, 0, cs], start=True, stop=True)
                mm(b6[0:32, 256:288], act[:, 1, S0:], kbT[:, S0:], start=True, stop=True)
                mm(b6[0:32, 288:320], act[:, 1, S0:], act[:, 0, S0:], start=True, stop=True).then_inc(prod_banked, 1)
                part(h + 1, 8)
                part(h + 1, 9)
                pe.wait_ge(u_ready, h + 1)
                for c in range(NCH):
                    tr(b4[:, c * P:(c + 1) * P], U[:, c], ident[:, :])
                tr(b6[0:32, 0:32], U[0:32, 4, 0:32], ident[0:32, 0:32]).then_inc(t_banked, 1)
                part(h + 1, 10)
                pe.wait_ge(t_ready, h + 1)
                for lv in range(1, LEVELS):
                    n = h * (LEVELS - 1) + lv
                    pe.wait_ge(mt_ready, n)
                    if lv >= 2:
                        pe.wait_ge(tu_ready, n - 1)
                    for c in range(NCH):
                        last = mm(b4[:, c * P:(c + 1) * P], MT[:, c], T[:, c], start=True, stop=True)
                    if lv == 1:
                        last = mm(b6[0:32, 0:32], vn[0:32, 4, 0:32], T[0:32, 4, 0:32], start=True, stop=True)
                    last.then_inc(y_banked, 1)
                    pe.wait_ge(y_saved, n)
                    for c in range(NCH):
                        last = mm(b5[:, c * P:(c + 1) * P], Y[:, c], U[:, c], start=True, stop=True)
                    if lv == 1:
                        last = mm(b6[0:32, 32:64], Y[0:32, 4, 0:32], U[0:32, 4, 0:32], start=True, stop=True)
                    if lv < LEVELS - 1:
                        for c in range(NCH):
                            last = mm(b7[:, c * P:(c + 1) * P], U[:, c], Y[:, c], start=True, stop=True)
                    last.then_inc(tu_banked, 1)
                    part(h + 1, 10 + lv)
                    if lv == 1:
                        history(h + 1)
                pe.wait_ge(tu_ready, (h + 1) * (LEVELS - 1))
                for c in range(NCH):
                    mm(b4[:, c * P:(c + 1) * P], kbg[:, c], U[:, c], start=True, stop=True)
                mm(b6[:, 0:32], kbg[0:32, 4], U[0:32, 4, 0:32], start=True, stop=True).then_inc(w_banked, 1)
                pe.wait_ge(w_ready, h + 1)
                for c in range(NCH):
                    n = h * NCH + c
                    cs = slice(c * P, (c + 1) * P)
                    pe.wait_ge(s_ready, h * (NCH + 1) + c + 1)
                    mm(b5[:, cs], U[:, c], vb[:, c], start=True, stop=False)
                    mm(b5[:, cs], nwT[:, c], S[c % 2], start=False, stop=True).then_inc(vn_banked, 1)
                    if c < 3:
                        part(h + 1, 17 + c)
                    pe.wait_ge(vn_ready, n + 1)
                    mm(b4[:, cs], kdec[:, c], vn[:, c], start=True, stop=True).then_inc(s_banked, 1)
                    mm(b7[:, cs], S[c % 2], qgT[:, cs], start=True, stop=False)
                    mm(b7[:, cs], vn[:, c], AT[:, c], start=False, stop=True).then_inc(o_banked, 1)
                pe.wait_ge(sb_in, 16 * (h + 1))
                mm(b6[0:32, 128:256], U[0:32, 4, 0:32], vb[0:32, 4], start=True, stop=False)
                for bb in range(NB):
                    last = mm(b6[0:32, 128:256], nw8[:, bb * 32:bb * 32 + 32], Sb[:, bb], start=False, stop=(bb == NB - 1))
                last.then_inc(vns_banked, 1)
                pe.wait_ge(vns_ready, h + 1)
                mm(b6[:, 0:32], vn[0:32, 4], AT[0:32, 4, 0:32], start=True, stop=False)
                for bb in range(NB):
                    last = mm(b6[:, bb * NT:bb * NT + NT], Sb[:, bb], qgT[:, S0 + bb * NT:S0 + bb * NT + NT],
                              start=False, stop=(bb == NB - 1))
                last.then_inc(o_banked, 1)
                pe.wait_ge(s_ready, (h + 1) * (NCH + 1))
                for bb in range(NB):
                    last = mm((b4, b5)[bb // 4][:, (bb % 4) * P:(bb % 4 + 1) * P], kdec8[0:32, bb], vn[0:32, 4],
                              start=True, stop=True)
                last.then_inc(ss_new_banked, 1)
                pe.wait_ge(osq_ready, h + 1)
                mm(b7[:, :], ones[:, :], sq[:, 0, 0:S0], start=True, stop=True)
                mm(b6[:, 0:32], ones[:, :], sq[:, 0, S0:], start=True, stop=True).then_inc(oss_banked, 1)

            for j in range(12):
                part(0, j)
            history(0)
            for j in range(12, 20):
                part(0, j)
            for h in range(H):
                delta(h)

        @block.scalar
        def _(sc):
            actv = nc.scalar.activation
            step = Steps(sc, act_step)
            for t in range(NTILE):
                t0, n = tok(t)
                for half in range(2):
                    i = 2 * t + half
                    sc.wait_ge(xt_banked, i + 1)
                    actv(xT[:, 4 * half:4 * half + 4, t0:t0 + n],
                         banks[i % 2][:, :].rearrange("p (k n) -> p k n", k=4)[:, :, 0:n], ACT.Copy).then_inc(xt_ready, 1)
            sc.wait_ge(zeroed, 2)
            for t in range(NTILE):
                _, n = tok(t)
                sc.wait_ge(kv_banked, 2 * t + 1)
                actv(kvt[0:n, t, 0:512], banks[2][0:n, :], ACT.Copy).then_inc(kv_ready, 1)
                sc.wait_ge(kv_banked, 2 * t + 2)
                actv(ab[0:n, t, :], banks[3][0:n, 304:320], ACT.Copy)
                actv(kvt[0:n, t, 512:KVW], banks[3][0:n, 0:304], ACT.Copy).then_inc(kv_ready, 1)
            sc.wait_ge(misc_in, 32)
            sc.wait_ge(y_ready, 1)
            step(actv(tk["tmpb"][:, :, :], tk["tmpa"][:, :, :], ACT.Abs))
            step(actv(tk["tmpb"][:, :, :], tk["tmpb"][:, :, :], ACT.Exp, scale=-1.0))
            actv(tk["beta"][:, :, :], ab[:, :, 8:16], ACT.Exp, scale=-1.0)
            actv(hb[:, 1, :], hb[:, 1, :], ACT.Exp)
            actv(tk["tmpb"][:, :, :], tk["tmpb"][:, :, :], ACT.Ln, bias=1.0).then_inc(ey_ready, 1)
            sc.wait_ge(y_ready, 2)
            actv(tk["kd"][:, :, :], tk["kd"][:, :, :], ACT.Exp)
            actv(tk["bg"][:, :, :], tk["gcum"][:, :, :], ACT.Exp).then_inc(ey_ready, 1)
            sc.wait_ge(cw_banked, 1)
            actv(convw[:, :], banks[5][:, 0:96], ACT.Copy).then_inc(cw_ready, 1)

            def save(h, unit):
                if h == H:
                    return
                i = 6 * h + unit
                if h >= 2 and unit == 0:
                    sc.wait_ge(conv_done, h - 1)
                    sc.wait_ge(cg_ready, h - 1)
                if h >= 2 and unit == 4:
                    sc.wait_ge(zm_done, h - 1)
                b0, b1 = banks[2 * (i % 2)], banks[2 * (i % 2) + 1]
                m = NP_TOK - HALF
                sc.wait_ge(pr_banked, i + 1)
                if unit < 3:
                    r = raw[h % 2]
                    actv(r[:, unit, 3:3 + HALF], b0[:, 0:HALF], ACT.Copy)
                    actv(r[:, unit, 3 + HALF:SROW], b1[:, 0:m], ACT.Copy)
                    actv(r[:, unit, SROW:].rearrange("p (b s) -> p b s", s=7)[:, :, 3:7],
                         b1[:, m:HALF].rearrange("p (b s) -> p b s", s=4), ACT.Copy).then_inc(pr_saved, 1)
                elif unit == 3:
                    for n in range(3):
                        last = actv(raw[h % 2][:, n, SROW:].rearrange("p (b s) -> p b s", s=7)[:, :, 0:3],
                                    b0[:, n * 24:(n + 1) * 24].rearrange("p (b s) -> p b s", s=3), ACT.Copy)
                    last.then_inc(pr_saved, 1)
                else:
                    actv(zm[h % 2][:, unit - 4, 0:HALF], b0[:, 0:HALF], ACT.Copy)
                    actv(zm[h % 2][:, unit - 4, HALF:], b1[:, 0:HALF], ACT.Copy).then_inc(pr_saved, 1)

            def conv_tanh(h):
                if h < H:
                    sc.wait_ge(conv_done, h + 1)
                    actv(ey, y, ACT.Tanh, scale=0.5).then_inc(ey_ready, 1)

            def squares(h):
                if h < H:
                    sc.wait_ge(act_ready, h + 1)
                    actv(sq, act[:, 0:2, :], ACT.Square, scale=0.5).then_inc(sq_ready, 1)

            def delta(h):
                b4, b5, b6, b7 = banks[4], banks[5], banks[6], banks[7]
                S0 = NP_TOK
                sc.wait_ge(cg_banked, h + 1)
                if h >= 2:
                    sc.wait_ge(conv_sent[h % 2], 32 * (h // 2))
                actv(conv_out[h % 2][0:27],
                     b7[0:27, 0:384].rearrange("r (n c) -> r n c", n=3), ACT.Copy).then_inc(cg_saved, 1)
                sc.wait_ge(ss_banked, h + 1)
                if h >= 1:
                    sc.wait_ge(h_ready, h)
                actv(rn[:, 0, 0:S0], b4[:, :], ACT.Ln, bias=eps[:, 0:1])
                actv(rn[:, 1, 0:S0], b5[:, :], ACT.Ln, bias=eps[:, 0:1])
                step(actv(rn[:, :, S0:], b6[:, 0:64].rearrange("p (a b) -> p a b", a=2), ACT.Ln, bias=eps[:, 0:1]))
                actv(rn, rn, ACT.Exp, scale=-0.5).then_inc(rn_ready, 1)
                save(h + 1, 0)
                sc.wait_ge(bc_banked, h + 1)
                actv(eg[:, 0:S0], b5[:, :], ACT.Exp)
                actv(eg[:, S0:], b6[:, 32:64], ACT.Exp).then_inc(eg_ready, 1)
                sc.wait_ge(diff_ready, h + 1)
                actv(dec[:, 0:4], dec[:, 0:4], ACT.Exp)
                actv(dec[0:32, 4, 0:32], dec[0:32, 4, 0:32], ACT.Exp).then_inc(dec_ready, 1)
                save(h + 1, 1)
                sc.wait_ge(t_banked, h + 1)
                actv(T[:, 0:4], b4[:, :].rearrange("p (c i) -> p c i", c=4), ACT.Copy)
                actv(T[0:32, 4, 0:32], b6[0:32, 0:32], ACT.Copy).then_inc(t_ready, 1)
                for lv in range(1, LEVELS):
                    sc.wait_ge(y_banked, h * (LEVELS - 1) + lv)
                    last = actv(Y[:, 0:4], b4[:, :].rearrange("p (c i) -> p c i", c=4), ACT.Copy)
                    if lv == 1:
                        last = actv(Y[0:32, 4, 0:32], b6[0:32, 0:32], ACT.Copy)
                    last.then_inc(y_saved, 1)
                    if lv == 2:
                        save(h + 1, 2)
                        save(h + 1, 3)
                    if lv == 6:
                        save(h + 1, 4)
                        conv_tanh(h + 1)
                sc.wait_ge(w_banked, h + 1)
                actv(nwT, b4[:, :].rearrange("p (c i) -> p c i", c=4), ACT.Copy, scale=-1.0)
                actv(nw8.rearrange("p (b s) -> p b s", s=36)[:, :, 0:NT],
                     b6[:, 0:32].rearrange("p (b s) -> p b s", s=NT), ACT.Copy, scale=-1.0).then_inc(w_ready, 1)
                for c in range(NCH):
                    n = h * NCH + c
                    sc.wait_ge(vn_banked, n + 1)
                    actv(vn[:, c], b5[:, c * P:(c + 1) * P], ACT.Copy).then_inc(vn_ready, 1)
                save(h + 1, 5)
                sc.wait_ge(pr_saved, 6 * (h + 1))
                actv(sgz, zm[h % 2], ACT.Tanh, scale=0.5).then_inc(ez_ready, 1)
                sc.wait_ge(vns_banked, h + 1)
                actv(vn[0:32, 4], b6[0:32, 128:256], ACT.Copy).then_inc(vns_ready, 1)
                sc.wait_ge(o_banked, (h + 1) * (NCH + 1))
                actv(oT[:, 0:S0], b7[:, :], ACT.Copy)
                step(actv(oT[:, S0:], b6[:, 0:32], ACT.Copy), o_saved)
                actv(sq[:, 0, :], oT, ACT.Square).then_inc(osq_ready, 1)
                sc.wait_ge(oss_banked, h + 1)
                actv(rn[:, 1, 0:S0], b7[:, :], ACT.Ln, scale=1.0 / DH, bias=eps[:, 0:1])
                step(actv(rn[:, 1, S0:], b6[:, 0:32], ACT.Ln, scale=1.0 / DH, bias=eps[:, 0:1]))
                actv(rn[:, 1], rn[:, 1], ACT.Exp, scale=-0.5).then_inc(rn_ready, 1)

            for unit in range(6):
                save(0, unit)
            conv_tanh(0)
            squares(0)
            for h in range(H):
                delta(h)
                squares(h + 1)

        @block.gpsimd
        def _(pool):
            nc.gpsimd.memset(eps[:, 0:1], 1e-6)
            nc.gpsimd.memset(eps[:, 1:2], 1e-5)
            nc.gpsimd.memset(ones[:, :], 1.0).then_inc(zeroed, 1)
            nc.gpsimd.memset(ab[:, 4, :], 0.0).then_inc(zeroed, 1)
            pool.wait_ge(tk_ready, 1)
            pool.wait_ge(kv_ready, 2 * NTILE)
            for r in raw:
                for n in range(3):
                    nc.gpsimd.memset(r[:, n, 0:3], 0.0)
            nc.gpsimd.memset(nw8, 0.0).then_inc(zeroed, 1)
            for h in range(H):
                if h >= 1:
                    pool.wait_ge(bc_banked, h)
                for n, src in enumerate((tk["beta"], tk["gg"])):
                    last = nc.gpsimd.tensor_copy(gb[:, n], src[:, :, h:h + 1].to_broadcast([P, NTILE, P]))
                last.then_inc(gb_ready, 1)
                pool.wait_ge(pr_saved, 6 * h + 4)
                if h >= 1:
                    pool.wait_ge(cg_banked, h)
                nc.gpsimd.tensor_copy(cg[:, :, 0:3], raw[h % 2][:, :, NP_TOK:NP_TOK + 3])
                for n in range(3):
                    last = nc.gpsimd.tensor_copy(cg[:, n, 3:27].rearrange("p (b s) -> p b s", s=3),
                                                 raw[h % 2][:, n, SROW:].rearrange("p (b s) -> p b s", s=7)[:, :, 4:7])
                last.then_inc(cg_ready, 1)
                pool.wait_ge(lt_ready, h + 1)
                for lv in range(1, LEVELS):
                    n = h * (LEVELS - 1) + lv
                    if n >= 2:
                        pool.wait_ge(y_banked, n - 1)
                    last = nc.gpsimd.tensor_tensor(MT, LT[:, 0:4], levels[:, lv:lv + 1, :].to_broadcast([P, 4, P]), ALU.mult)
                    if lv == 1:
                        last = nc.gpsimd.tensor_tensor(vn[0:32, 4, 0:32], LT[0:32, 4, 0:32], levels[0:32, lv, 0:32], ALU.mult)
                    last.then_inc(mt_ready, 1)

        @block.vector
        def _(dve):
            step = Steps(dve, dve_step)
            V = nc.vector
            beta, gg, gcum, bg, kd, glast, hbeta = (tk[n] for n in ("beta", "gg", "gcum", "bg", "kd", "glast", "hbeta"))
            dve.wait_ge(zeroed, 2)
            step(V.memset(gcum[:, 4, :], 0.0))
            step(V.memset(glast[:, 4, :], 0.0))
            dve.wait_ge(kv_ready, 2 * NTILE)
            dve.wait_ge(misc_in, 32)
            step(V.tensor_tensor(tk["tmpa"][:, :, :], ab[:, :, 0:8], hb[:, 0:1, :].to_broadcast([P, NTILE, H]), ALU.add), y_ready)
            dve.wait_ge(ey_ready, 1)
            step(V.tensor_scalar(tk["tmpc"][:, :, :], tk["tmpa"][:, :, :], 0.0, None, ALU.max))
            step(V.tensor_tensor(tk["tmpc"][:, :, :], tk["tmpc"][:, :, :], tk["tmpb"][:, :, :], ALU.add))
            step(V.scalar_tensor_tensor(gg[:, :, :], tk["tmpc"][:, :, :], -1.0, hb[:, 1:2, :].to_broadcast([P, NTILE, H]),
                                        ALU.mult, ALU.mult), g_ready)
            step(V.tensor_scalar(beta[:, :, :], beta[:, :, :], 1.0, None, ALU.add))
            step(V.reciprocal(beta[:, :, :], beta[:, :, :]))
            step(V.tensor_scalar(hbeta[:, :, :], beta[:, :, :], 0.5, None, ALU.mult))
            dve.wait_ge(gcum_banked, 1)
            step(V.tensor_copy(gcum[:, 0:4, :], banks[4][:, 0:32].rearrange("p (c h) -> p c h", c=4)))
            step(V.tensor_copy(glast[:, 0:4, :], banks[4][:, 32:64].rearrange("p (c h) -> p c h", c=4)))
            step(V.tensor_copy(gcum[0:32, 4, :], banks[4][0:32, 64:72]))
            step(V.tensor_copy(glast[0:32, 4, :], banks[4][0:32, 72:80]))
            step(V.tensor_tensor(kd[:, :, :], glast[:, :, :], gcum[:, :, :], ALU.subtract), y_ready)
            dve.wait_ge(ey_ready, 2)
            step(V.tensor_tensor(bg[:, :, :], bg[:, :, :], beta[:, :, :], ALU.mult), tk_ready)
            dve.wait_ge(zeroed, 3)
            dve.wait_ge(cw_ready, 1)
            dve.wait_ge(b_in, 16 * 3)
            step(V.tensor_scalar(normw, normw, 0.25, None, ALU.mult))

            def conv(h, i):
                if h == H:
                    return
                dve.wait_ge(pr_saved, 6 * h + 4)
                r = raw[h % 2]
                n = RAWW - 3
                w = [convw[:, j * 24 + i * 8 + h:j * 24 + i * 8 + h + 1] for j in range(4)]
                step(V.tensor_scalar(y[:, i], r[:, i, 0:n], w[0], None, ALU.mult))
                for j in range(1, 3):
                    step(V.scalar_tensor_tensor(y[:, i], r[:, i, j:j + n], w[j], y[:, i], ALU.mult, ALU.add))
                ins = V.scalar_tensor_tensor(y[:, i], r[:, i, 3:3 + n], w[3], y[:, i], ALU.mult, ALU.add)
                step(ins, conv_done if i == 2 else None)

            def conv_act(h, i):
                if h == H:
                    return
                dve.wait_ge(ey_ready, 2 + h + 1)
                V.scalar_tensor_tensor(act[:, i, 0:NP_TOK], ey[:, i, 0:NP_TOK], 1.0, y[:, i, 0:NP_TOK], ALU.add, ALU.mult)
                ev, yv = (v[:, i, SROW:SROW + 49].rearrange("p (b s) -> p b s", s=7)[:, :, 0:4] for v in (ey, y))
                step(V.scalar_tensor_tensor(act[:, i, NP_TOK:NP_TOK + 28].rearrange("p (b s) -> p b s", s=4), ev, 1.0, yv,
                                            ALU.add, ALU.mult))
                if i == 2:
                    end = slice(SROW + 49, SROW + 53)
                    step(V.scalar_tensor_tensor(act[:, :, NP_TOK + 28:], ey[:, :, end], 1.0, y[:, :, end], ALU.add, ALU.mult), act_ready)

            def delta(h):
                b4, b5, b6, b7 = banks[4], banks[5], banks[6], banks[7]
                S0 = NP_TOK
                chunks = lambda ap: ap.rearrange("p (c i) -> p c i", c=4)
                dve.wait_ge(rn_ready, 2 * h + 1)
                step(V.scalar_tensor_tensor(act[:, 0], act[:, 0], 0.5 * float(DH) ** -0.5, rn[:, 0], ALU.mult, ALU.mult))
                step(V.scalar_tensor_tensor(act[:, 1], act[:, 1], 0.5, rn[:, 1], ALU.mult, ALU.mult), qk_ready)
                dve.wait_ge(bc_banked, h + 1)
                step(V.tensor_tensor(kbT[:, 0:S0], act[:, 1, 0:S0], b4[:, :], ALU.mult))
                dve.wait_ge(eg_ready, h + 1)
                step(V.tensor_tensor(kbT[:, S0:], act[:, 1, S0:], b6[:, 0:32], ALU.mult), kb_ready)
                step(V.tensor_tensor(dec[:, 0:4], chunks(b5[:, :]), gcum[:, 0:4, h:h + 1].to_broadcast([P, 4, P]), ALU.subtract))
                step(V.scalar_tensor_tensor(dec[:, 0:4], dec[:, 0:4], 0.0, causal_t[:, :].rearrange("p (o i) -> p o i", o=1).to_broadcast([P, 4, P]),
                                            ALU.min, ALU.add))
                step(V.tensor_scalar(dec[0:32, 4, 0:32], b6[0:32, 32:64], gcum[0:32, 4, h:h + 1], 0.0, ALU.subtract, ALU.min))
                step(V.tensor_tensor(dec[0:32, 4, 0:32], dec[0:32, 4, 0:32], causal_ts[:, :], ALU.add), diff_ready)
                step(V.tensor_tensor(qgT, act[:, 0], eg, ALU.mult))
                dve.wait_ge(tok_banked, h + 1)
                if h >= 1:
                    dve.wait_ge(ss_new_banked, h)
                for dst, src, ssrc, s in ((kbg, b7[:, :], b6[0:32, 0:P], bg), (kdec, b7[:, :], b6[0:32, 0:P], kd),
                                          (vb, b4[:, :], b6[0:32, P:2 * P], hbeta)):
                    step(V.tensor_tensor(dst[:, 0:4], chunks(src), s[:, 0:4, h:h + 1].to_broadcast([P, 4, P]), ALU.mult))
                    last = V.tensor_scalar(dst[0:32, 4], ssrc, s[0:32, 4, h:h + 1], None, ALU.mult)
                    step(last, tok_ready if s is hbeta else None)
                step(V.tensor_tensor(kdec8[0:32], kdec[0:32, 4:5, :].to_broadcast([32, NB, P]),
                                     rows_s[:, :].rearrange("p (b o) -> p b o", o=1).to_broadcast([32, NB, P]), ALU.mult))
                dve.wait_ge(prod_banked, h + 1)
                dve.wait_ge(dec_ready, h + 1)
                step(V.tensor_tensor(LT[:, 0:4], chunks(b5[:, :]), dec[:, 0:4], ALU.mult))
                step(V.tensor_tensor(LT[0:32, 4, 0:32], b6[0:32, 256:288], dec[0:32, 4, 0:32], ALU.mult), lt_ready)
                step(V.tensor_tensor(AT[:, 0:4], chunks(b7[:, :]), dec[:, 0:4], ALU.mult))
                step(V.tensor_tensor(AT[0:32, 4, 0:32], b6[0:32, 288:320], dec[0:32, 4, 0:32], ALU.mult))
                step(V.scalar_tensor_tensor(U[:, 0:4], LT[:, 0:4], -1.0, levels[:, 0:1, :].to_broadcast([P, 4, P]), ALU.mult, ALU.mult))
                step(V.scalar_tensor_tensor(U[0:32, 4, 0:32], LT[0:32, 4, 0:32], -1.0, levels[0:32, 0, 0:32], ALU.mult, ALU.mult))
                step(V.tensor_tensor(U[:, 0:4], U[:, 0:4], ident[:, :].rearrange("p (o i) -> p o i", o=1).to_broadcast([P, 4, P]), ALU.add))
                step(V.tensor_tensor(U[0:32, 4, 0:32], U[0:32, 4, 0:32], ident[0:32, 0:32], ALU.add), u_ready)
                dve.wait_ge(t_ready, h + 1)
                for lv in range(1, LEVELS):
                    dve.wait_ge(tu_banked, h * (LEVELS - 1) + lv)
                    if lv == 1:
                        step(V.tensor_tensor(U[0:32, 4, 0:32], U[0:32, 4, 0:32], b6[0:32, 32:64], ALU.subtract))
                    if lv < LEVELS - 1:
                        step(V.tensor_tensor(T[:, 0:4], T[:, 0:4], chunks(b7[:, :]), ALU.subtract))
                    step(V.tensor_tensor(U[:, 0:4], U[:, 0:4], chunks(b5[:, :]), ALU.subtract), tu_ready)
                    if 3 <= lv <= 5:
                        conv(h + 1, lv - 3)
                if h >= 1:
                    dve.wait_ge(s_out, 16 * h)
                step(V.memset(S[0], 0.0), s_ready)
                for c in range(NCH):
                    dve.wait_ge(s_banked, h * NCH + c + 1)
                    last = (V.scalar_tensor_tensor(S[(c + 1) % 2], S[c % 2], eg[:, (c + 1) * P - 1:(c + 1) * P],
                                                     b4[:, c * P:(c + 1) * P], ALU.mult, ALU.add))
                    step(last, s_ready)
                    if c < 3:
                        conv_act(h + 1, c)
                if h >= 1:
                    dve.wait_ge(sn_out, 16 * h)
                dve.wait_ge(ss_new_banked, h + 1)
                egl = eg[:, S0:].rearrange("p (b s) -> p b s", s=NT)[:, :, NT - 1:NT].to_broadcast([P, NB, P])
                step(V.tensor_tensor(Sn, Sb, egl, ALU.mult))
                step(V.tensor_tensor(Sn[:, 0:4], Sn[:, 0:4], chunks(b4[:, :]), ALU.add))
                step(V.tensor_tensor(Sn[:, 4:8], Sn[:, 4:8], chunks(b5[:, :]), ALU.add), sn_final)
                dve.wait_ge(rn_ready, 2 * h + 2)
                step(V.scalar_tensor_tensor(oT, oT, normw, rn[:, 1], ALU.mult, ALU.mult))
                dve.wait_ge(ez_ready, h + 1)
                step(V.scalar_tensor_tensor(sgz[:, 0], sgz[:, 0], 1.0, zm[h % 2][:, 0], ALU.add, ALU.mult), zm_done)
                step(V.scalar_tensor_tensor(sgz[:, 0], sgz[:, 1], 1.0, sgz[:, 0], ALU.add, ALU.mult))
                step(V.tensor_tensor(hT[:, h], oT, sgz[:, 0], ALU.mult), h_ready)

            for i in range(3):
                conv(0, i)
            for i in range(3):
                conv_act(0, i)
            for h in range(H):
                delta(h)

        block_ctx.close()
        end_block()

        dve_step = sem("dve_step")
        act_step = sem("act_step")
        wh_in = [sem(f"wh_in{i}") for i in range(RING)]
        ids_in = sem("ids_in")
        w1_in = sem("w1_in")
        c2_in = sem("c2_in")
        att_in = sem("att_in")
        dec_in = sem("dec_in")
        pool_step = sem("pool_step")
        prj_banked = sem("prj_banked")
        prj_saved = sem("prj_saved")
        q_zeroed = sem("q_zeroed")
        kvp_banked = sem("kvp_banked")
        kvp_saved = sem("kvp_saved")
        posr_banked = sem("posr_banked")
        posr_saved = sem("posr_saved")
        pg_banked = sem("pg_banked")
        pg_saved = [sem("pg_saved_even"), sem("pg_saved_odd")]
        hid_banked = sem("hid_banked")
        gelu_done = sem("gelu_done")
        cmpo_banked = sem("cmpo_banked")
        cmpo_saved = sem("cmpo_saved")
        gt_tanh = sem("gt_tanh")
        gt_ready = sem("gt_ready")
        dup_ready = sem("dup_ready")
        kt_banked = sem("kt_banked")
        kt_saved = sem("kt_saved")
        cs_banked = sem("cs_banked")
        cs_max = sem("cs_max")
        cs_exp = sem("cs_exp")
        cs_ready = sem("cs_ready")
        pct_banked = sem("pct_banked")
        pct_saved = sem("pct_saved")
        co_banked = sem("co_banked")
        co_saved = sem("co_saved")
        hb_ready = sem("hb_ready")
        at_banked = sem("at_banked")
        at_max = sem("at_max")
        at_exp = sem("at_exp")
        at_tr_banked = sem("at_tr_banked")
        at_pt_saved = sem("at_pt_saved")
        at_pt_saved_v = sem("at_pt_saved_v")
        at_o_banked = sem("at_o_banked")
        at_done = sem("at_done")
        qr_banked = sem("qr_banked")
        qr_saved = sem("qr_saved")
        qd_banked = sem("qd_banked")
        qd_ready = sem("qd_ready")
        slc_in = [sem("slc_in0"), sem("slc_in1")]
        win_in = [sem(f"win_in{n}") for n in range(4)]
        wout_in = sem("wout_in")
        ks_banked = sem("ks_banked")
        ks_saved = sem("ks_saved")
        kn_saved = sem("kn_saved")
        sd_banked = sem("sd_banked")
        sd_max = sem("sd_max")
        sd_exp = sem("sd_exp")
        sd_sum = sem("sd_sum")
        ptd_banked = sem("ptd_banked")
        ptd_saved = sem("ptd_saved")
        od_banked = sem("od_banked")
        od_saved = sem("od_saved")
        imp_banked = sem("imp_banked")
        imp_saved = sem("imp_saved")
        grp_banked = sem("grp_banked")
        sel_ready = sem("sel_ready")
        od_out = sem("od_out")
        odec_in = sem("odec_in")
        odec_ready = sem("odec_ready")
        of_banked = sem("of_banked")
        of_ready = sem("of_ready")
        page_in = [sem(f"page_in{i}") for i in range(8)]
        block_ctx = ExitStack()
        block = block_ctx.enter_context(nc.Block())

        @block.sync
        def _(sp):
            w = io["w_in"][0].rearrange("(k p) n -> p k n", p=P)
            for n in range(16):
                if n >= RING:
                    sp.wait_ge(prj_banked, n - RING + 1)
                c0 = COL_NQ + n * P if n < 8 else COL_MG + D + (n - 8) * P
                sp.dma_start(wh[n % RING], w[:, :, c0:c0 + P]).then_inc(wh_in[n % RING], 16)
            w1 = io["nsa_cmp_w1"][0].rearrange("s (r d) e -> d s r e", d=HD)
            for s in range(2):
                for kv in range(2):
                    half = slice(kv * 64, kv * 64 + 64)
                    sp.dma_start(W1[half, s, :, half], w1[:, s]).then_inc(w1_in, 16)
            sp.dma_start(page_ids[0:1, :], io["page_table"].rearrange("(o b) p -> o (b p)", o=1)).then_inc(ids_in, 16)
            sp.wait_ge(prj_banked, 16)
            pos = io["nsa_cmp_pos"][0].rearrange("s r d -> r s d")
            w2 = io["nsa_cmp_w2"][0]
            for kv in range(2):
                half = slice(kv * 64, kv * 64 + 64)
                sp.dma_start(pos_rows[0:32, :, half], pos).then_inc(c2_in, 16)
                sp.wait_ge(q_zeroed, 1)
                sp.dma_start(W2k[half, half], w2[0]).then_inc(c2_in, 16)
                sp.dma_start(W2v[half, half], w2[1]).then_inc(c2_in, 16)
                for dup in range(2):
                    sp.dma_start(W2kd[half, kv, dup * 64:dup * 64 + 64], w2[0]).then_inc(c2_in, 16)
            sp.wait_ge(ids_in, 16)
            cmp_pool = io["cache_cmp_kv"][0].rearrange("n p s h d -> n p (s h d)")
            slc_pool = io["cache_slc_kv"][0].rearrange("n p s h d -> n p (s h d)")
            for j in range(8):
                page = sp.value_load(page_ids[0:1, j:j + 1], min_val=0, max_val=NPOOL - 1)
                sp.dma_start(pages[:, j, :], cmp_pool[bass.ds(page, 1)]).then_inc(page_in[j], 16)
            with sp.Fori(1, NB * NPG // 8) as it:
                for j in range(8):
                    page = sp.value_load(page_ids[0:1, bass.ds(it * 8 + j, 1)], min_val=0, max_val=NPOOL - 1)
                    sp.wait_ge(pg_banked, it * 4 + (j // 2 - 3))
                    sp.dma_start(pages[:, j, :], cmp_pool[bass.ds(page, 1)]).then_inc(page_in[j], 16)

            def selected_pages(pair, b2):
                with sp.Fori(0, NPG) as i:
                    page = sp.value_load(page_ids[0:1, bass.ds(i + NPG * (2 * pair + b2), 1)], min_val=0, max_val=NPOOL - 1)
                    sp.dma_start(slc_raw[pair % 2][b2][:, bass.ds(i, 1), :], slc_pool[bass.ds(page, 1)].rearrange("o p c -> p o c")).then_inc(slc_in[pair % 2], 16)

            selected_pages(0, 0)
            sp.wait_ge(cmpo_saved, 2 + 8)
            sp.dma_start(dist, io["dist"]).then_inc(att_in, 16)
            sp.dma_start(cmp_bias, io["cmp_bias"].rearrange("p (t h c) -> p t h c", t=4, h=QH)).then_inc(att_in, 16)
            sp.dma_start(cmp_any, io["cmp_any"]).then_inc(att_in, 16)
            sp.wait_ge(at_done, 64)
            sp.wait_ge(qd_ready, 1)
            for dst, name in ((slc_bias_s, "slc_bias_s"), (win_bias_s, "win_bias_s"), (cmp_bias_s, "cmp_bias_s"),
                              (cover[0:NCMP_S], "cover"), (forced, "forced"), (group, "group"), (kv_rows, "kv_rows")):
                sp.dma_start(dst, io[name]).then_inc(dec_in, 16)
            sp.dma_start(new_bias_s, io["new_bias_s"].rearrange("p (a k) -> p a k", a=4)).then_inc(dec_in, 16)
            win_pool = io["cache_win_kv"][0].rearrange("b (t p) s h d -> b p t (s h d)", p=P)
            for pair in range(4):
                for b2 in range(2):
                    sp.dma_start(win_raw[:, pair, 4 * b2:4 * b2 + 4, :], win_pool[2 * pair + b2]).then_inc(win_in[pair], 16)
            sp.wait_ge(qr_banked, 1)
            selected_pages(0, 1)
            for job, (pair, br) in enumerate(SAMPLE_JOBS):
                sp.wait_ge(od_saved, job + 1)
                sp.dma_start(o_scratch[br + 1, 2 * pair:2 * pair + 2].rearrange("b h t (g d) -> (b h t g) d", g=G), orow).then_inc(od_out, 16)
                if (pair, br) == (3, 1):
                    selected_pages(1, 0)
                    selected_pages(1, 1)
                if br == 0 and pair < 2:
                    selected_pages(pair + 2, 0)
                    selected_pages(pair + 2, 1)
                if (pair, br) == (2, 0):
                    for n in range(2):
                        sp.dma_start(wout[n], io["w_out"][0].rearrange("(n k p) e -> n p k e", n=2, p=P)[n]).then_inc(wout_in, 16)
            sp.wait_ge(od_out, 16 * 12)
            sp.wait_ge(wout_in, 32)
            for br in range(3):
                for bb in range(NB):
                    sp.dma_start(odec[bb * NT:bb * NT + NT, br * D:(br + 1) * D].rearrange("t (h x) -> t h x", h=2),
                                 o_scratch[br, bb].rearrange("h t x -> t h x")).then_inc(odec_in, 16)

        @block.tensor
        def _(pe):
            mm, tr = nc.tensor.matmul, nc.tensor.transpose
            for n in range(16):
                blk = n
                pe.wait_ge(wh_in[blk % RING], 16 * (blk // RING + 1))
                if n >= 2:
                    pe.wait_ge(prj_saved, n - 1)
                for half in range(2):
                    for k in range(KD):
                        last = mm(banks[2 * (n % 2) + half][:, 0:HALF], wh[blk % RING][:, k, :],
                                  xT[:, k, half * HALF:(half + 1) * HALF], start=(k == 0), stop=(k == KD - 1))
                last.then_inc(prj_banked, 1)
            pe.wait_ge(prj_saved, 16)
            for g in range(2):
                for s in range(2):
                    for j in range(2):
                        last = tr(banks[g][:, s * 256 + j * P:s * 256 + j * P + P], kvt[:, 2 * g + j, s * P:s * P + P], ident[:, :])
                last.then_inc(kvp_banked, 1)
            pe.wait_ge(c2_in, 16 * 10)
            for s in range(2):
                last = tr(banks[2][:, s * 32:s * 32 + 32], pos_rows[0:32, s, :], ident[0:32, 0:32])
            last.then_inc(posr_banked, 1)
            pe.wait_ge(posr_saved, 1)
            pe.wait_ge(w1_in, 16 * 4)
            for s in range(2):
                for rp in range(32):
                    last = mm(banks[3][:, s:s + 1], W1[:, s, rp, :], posT[:, s, rp:rp + 1], start=(rp == 0), stop=(rp == 31))
            last.then_inc(posr_banked, 1)

            def compress(src, width):
                for s in range(2):
                    for rp in range(32):
                        last = mm(banks[4 + s][:, 0:width], W1[:, s, rp, :], src(s, rp // 16, rp % 16), start=(rp == 0), stop=(rp == 31))
                last.then_inc(hid_banked, 1)

            pe.wait_ge(kvp_saved, 2)
            compress(lambda s, a, b: kvT_p[:, s].rearrange("p (n q) -> p n q", q=16)[:, a:a + NCMP_P, b], NCMP_P)
            pe.wait_ge(gelu_done, 1)
            for kv in range(2):
                mm(banks[6][:, kv * 32:kv * 32 + NCMP_P], W2kd[:, kv], gk[:, 0:NCMP_P], start=True, stop=True)
            mm(banks[7][:, 0:P], gv[:, 0:P], W2v, start=True, stop=True).then_inc(cmpo_banked, 1)
            for pair in range(4):
                for g in range(16):
                    i = 16 * pair + g
                    for j in range(2):
                        n = 2 * i + j
                        pe.wait_ge(page_in[n % 8], 16 * (n // 8 + 1))
                    if i >= 2:
                        pe.wait_ge(pg_saved[i % 2], i // 2)
                    if i == 0:
                        pe.wait_ge(kvp_saved, 2)
                    for s in range(2):
                        for j in range(2):
                            last = tr(banks[i % 2][:, s * 256 + j * P:s * 256 + j * P + P],
                                      pages[:, (2 * i + j) % 8, s * P:s * P + P], ident[:, :])
                    last.then_inc(pg_banked, 1)
                pe.wait_ge(pg_saved[0], 8 * (pair + 1))
                pe.wait_ge(pg_saved[1], 8 * (pair + 1))
                pe.wait_ge(gelu_done, pair + 1)
                compress(lambda s, a, b: kvT[:, s].rearrange("p (c n q) -> p c n q", c=2, q=16)[:, :, a:a + NCMP_S, b], 2 * NCMP_S)
                pe.wait_ge(gelu_done, pair + 2)
                pe.wait_ge(cmpo_saved, 2 * pair + 2)
                mm(banks[6][:, 0:2 * NCMP_S], W2k, gk, start=True, stop=True)
                for b2 in range(2):
                    last = mm(banks[7][0:NCMP_S, b2 * P:(b2 + 1) * P], gv[:, b2 * NCMP_S:(b2 + 1) * NCMP_S], W2v, start=True, stop=True)
                last.then_inc(cmpo_banked, 1)

            pe.wait_ge(dup_ready, 1)
            for n in range(4):
                if n >= 2:
                    pe.wait_ge(kt_saved, n - 1)
                for t in range(4):
                    last = tr(banks[n % 2][:, t * P:t * P + P], dupK[:, n, t], ident[:, :])
                last.then_inc(kt_banked, 1)
            pe.wait_ge(kt_saved, 4)
            for t in range(4):
                if t >= 1:
                    pe.wait_ge(co_saved, t)
                for hd in range(QH):
                    half = slice(hd % 2 * 64, hd % 2 * 64 + 64)
                    last = mm(banks[4 * (hd % 2)][:, hd // 2 * 32:hd // 2 * 32 + NCMP_P], qT[half, hd // 2, t * P:t * P + P],
                              kcT_p[half, hd // 8, 0:NCMP_P], start=True, stop=True)
                last.then_inc(cs_banked, 1)
                pe.wait_ge(cs_ready, t + 1)
                for j in range(4):
                    last = tr(banks[1][:, j * P:j * P + P], sc_c[:, 4 * j:4 * j + 4, :].rearrange("p a b -> p (a b)"), ident[:, :])
                last.then_inc(pct_banked, 1)
                pe.wait_ge(pct_saved, t + 1)
                for hd in range(QH):
                    rows = slice(hd % 4 * 32, hd % 4 * 32 + 32)
                    kv = hd // 8
                    last = mm(banks[(2, 3, 5, 6)[hd % 4]][:, hd // 4 * 64:hd // 4 * 64 + 64], PcT[rows, hd // 4], vc_p[rows, kv * 64:kv * 64 + 64],
                              start=True, stop=True)
                last.then_inc(co_banked, 1)
            pe.wait_ge(co_saved, 4)

            def scores(i):
                hd, t = divmod(i, 4)
                if i >= 2:
                    pe.wait_ge(at_max, 2 * (i - 1))
                half = slice(hd % 2 * 64, hd % 2 * 64 + 64)
                for br in range(2):
                    last = mm(banks[2 * (i % 2) + br][:, 0:(t + 1) * P], qT[half, hd // 2, t * P:t * P + P],
                              KT[half, 2 * br + hd // 8, 0:(t + 1) * P], start=True, stop=True)
                last.then_inc(at_banked, 1)

            def values(i):
                hd, t = divmod(i, 4)
                pe.wait_ge(at_pt_saved, i + 1)
                pe.wait_ge(at_pt_saved_v, i + 1)
                if i >= 2:
                    pe.wait_ge(at_done, i - 1)
                for br in range(2):
                    c0 = (br + 1) * 256 + P + hd // 8 * 64
                    for k in range(t + 1):
                        last = mm(banks[6 + i % 2][:, br * 64:br * 64 + 64], PT[i % 2][:, br, k], kvt[:, k, c0:c0 + 64],
                                  start=(k == 0), stop=(k == t))
                last.then_inc(at_o_banked, 1)

            scores(0)
            for i in range(64):
                if i + 1 < 64:
                    scores(i + 1)
                if i >= 1:
                    values(i - 1)
                pe.wait_ge(at_exp, i + 1)
                for br in range(2):
                    for k in range(i % 4 + 1):
                        last = tr(banks[4 + br][:, k * P:k * P + P], sc_p[i % 2][:, br, k * P:k * P + P], ident[:, :])
                last.then_inc(at_tr_banked, 1)
            values(63)

            pe.wait_ge(at_done, 64)
            for m in range(8):
                last = tr(banks[m // 4][0:NS_TOK, m % 4 * P:m % 4 * P + P], qT[:, m, NP_TOK:], ident[:, :])
            last.then_inc(qr_banked, 1)
            pe.wait_ge(qr_saved, 1)
            for g in range(G):
                last = tr(banks[2][:, g * NS_TOK:(g + 1) * NS_TOK], dupK[0:NS_TOK, g // 4, g % 4], ident[0:NS_TOK, 0:NS_TOK])
            for br in range(2):
                last = tr(banks[3][:, br * NS_TOK:(br + 1) * NS_TOK], kvt[0:NS_TOK, 4, (br + 1) * 256:(br + 1) * 256 + P],
                          ident[0:NS_TOK, 0:NS_TOK])
            last.then_inc(qd_banked, 1)
            pe.wait_ge(qd_ready, 1)
            pe.wait_ge(kn_saved, 1)
            pe.wait_ge(dec_in, 16 * 8)
            ktg = 0
            ptd = 0
            for job, (pair, br) in enumerate(SAMPLE_JOBS):
                if br < 0:
                    if job >= 1:
                        pe.wait_ge(od_saved, job)
                    for b2 in range(2):
                        half = slice(64 * b2, 64 * b2 + 64)
                        last = mm(banks[0][half, 0:NCMP_S], QD[:, 2 * pair + b2], kcT_s[:, 2 * pair + b2], start=True, stop=True)
                    last.then_inc(sd_banked, 1)
                    pe.wait_ge(sd_exp, job + 1)
                    tr(banks[1][0:NCMP_S, 0:P], Ss[:, 0:NCMP_S], ident[:, :]).then_inc(ptd_banked, 1)
                    ptd += 1
                    pe.wait_ge(ptd_saved, ptd)
                    for b2 in range(2):
                        half = slice(64 * b2, 64 * b2 + 64)
                        last = mm(banks[6][half, 0:P], PTs[0:NCMP_S, 0, half], vc_s[0:NCMP_S, 2 * pair + b2], start=True, stop=True)
                    last.then_inc(od_banked, 1)
                    mm(banks[2][:, 0:NBLK], PTs[0:NCMP_S, 0], cover[0:NCMP_S], start=True, stop=True).then_inc(imp_banked, 1)
                    pe.wait_ge(imp_saved, pair + 1)
                    mm(banks[3][:, 0:NBLK], group, imp, start=True, stop=True).then_inc(grp_banked, 1)
                    continue
                ntile = (16, 4)[br]
                nk = ntile * P
                if br == 0:
                    pe.wait_ge(slc_in[pair % 2], 512 * (pair // 2 + 1))
                else:
                    pe.wait_ge(win_in[pair], 32)
                rows = slc_raw[pair % 2] if br == 0 else [win_raw[:, pair, 0:4], win_raw[:, pair, 4:8]]
                for g in range(2 * ntile // 4):
                    if ktg >= 2:
                        pe.wait_ge(ks_saved, ktg - 1)
                    b2, t0 = divmod(4 * g, ntile)
                    for j in range(4):
                        last = tr(banks[4 + ktg % 2][:, j * P:j * P + P], rows[b2][:, t0 + j, 0:P], ident[:, :])
                    last.then_inc(ks_banked, 1)
                    ktg += 1
                pe.wait_ge(od_saved, job)
                pe.wait_ge(ks_saved, ktg)
                pe.wait_ge(sel_ready, pair + 1 if br == 1 else 4)
                for c in range(ntile // 4 + 1):
                    for b2 in range(2):
                        half = slice(64 * b2, 64 * b2 + 64)
                        bb = 2 * pair + b2
                        if c < ntile // 4:
                            last = mm(banks[c % 4][half, :], QD[:, bb], KTs[:, b2, c * 512:c * 512 + 512], start=True, stop=True)
                        else:
                            last = mm(banks[7][half, 0:NS_TOK], QD[:, bb], knT[:, br], start=True, stop=True)
                last.then_inc(sd_banked, 1)
                pe.wait_ge(sd_exp, job + 1)
                for g in range(ntile // 4):
                    if g >= 2:
                        pe.wait_ge(ptd_saved, ptd - 1)
                    for j in range(4):
                        last = tr(banks[4 + g % 2][:, j * P:j * P + P], Ss[:, (4 * g + j) * P:(4 * g + j + 1) * P], ident[:, :])
                    if g == ntile // 4 - 1:
                        last = tr(banks[7][0:NS_TOK, 0:P], Ss[:, nk:nk + NS_TOK], ident[:, :])
                    last.then_inc(ptd_banked, 1)
                    ptd += 1
                pe.wait_ge(ptd_saved, ptd)
                for b2 in range(2):
                    half = slice(64 * b2, 64 * b2 + 64)
                    for j in range(ntile):
                        mm(banks[6][half, 0:P], PTs[:, j, half], rows[b2][:, j, P:256], start=(j == 0), stop=False)
                    last = mm(banks[6][half, 0:P], PTs[0:NS_TOK, 16, half], kvt[0:NS_TOK, 4, (br + 1) * 256 + P:(br + 2) * 256],
                              start=False, stop=True)
                last.then_inc(od_banked, 1)
            pe.wait_ge(odec_ready, 1)
            for t in range(NTILE):
                _, n = tok(t)
                for half in range(2):
                    i = 2 * t + half
                    if i >= 2:
                        pe.wait_ge(of_ready, i - 1)
                    for k in range(4):
                        last = tr(banks[i % 2][:, k * P:k * P + n], otok[0:n, t, (4 * half + k) * P:(4 * half + k + 1) * P],
                                  ident[0:n, 0:n])
                    last.then_inc(of_banked, 1)

        @block.scalar
        def _(sc):
            actv = nc.scalar.activation
            step = Steps(sc, act_step)
            for n in range(16):
                sc.wait_ge(prj_banked, n + 1)
                dst = qT[:, n] if n < 8 else mgB[:, n - 8]
                for half in range(2):
                    last = actv(dst[:, half * HALF:(half + 1) * HALF], banks[2 * (n % 2) + half][:, 0:HALF], ACT.Copy)
                last.then_inc(prj_saved, 1)
            sc.wait_ge(prj_saved, 16)
            actv(mgB, mgB, ACT.Tanh, scale=0.5)
            actv(gt[:, 0:4], kvt[:, 0:4, 768:816], ACT.Tanh, scale=0.5)
            actv(gt[0:NS_TOK, 4], kvt[0:NS_TOK, 4, 768:816], ACT.Tanh, scale=0.5).then_inc(gt_tanh, 1)
            for g in range(2):
                sc.wait_ge(kvp_banked, g + 1)
                actv(kvT_p[:, :, g * 256:(g + 1) * 256], banks[g][:, :].rearrange("p (s n) -> p s n", s=2), ACT.Copy).then_inc(kvp_saved, 1)
            sc.wait_ge(posr_banked, 1)
            step(actv(posT, banks[2][:, 0:64].rearrange("p (s n) -> p s n", s=2), ACT.Copy), posr_saved)
            sc.wait_ge(posr_banked, 2)
            step(actv(cbias, banks[3][:, 0:2], ACT.Copy), posr_saved)
            sc.wait_ge(q_zeroed, 2)
            sc.wait_ge(hid_banked, 1)
            actv(gk[:, 0:NCMP_P], banks[4][:, 0:NCMP_P], ACT.Gelu_apprx_tanh, bias=cbias[:, 0:1])
            for j in range(4):
                last = actv(gv[:, 32 * j:32 * j + NCMP_P], banks[5][:, 0:NCMP_P], ACT.Gelu_apprx_tanh, bias=cbias[:, 1:2])
            last.then_inc(gelu_done, 1)
            sc.wait_ge(cmpo_banked, 1)
            actv(kcT_p[:, :, 0:NCMP_P], banks[6][:, 0:64].rearrange("p (k n) -> p k n", k=2)[:, :, 0:NCMP_P], ACT.Copy).then_inc(cmpo_saved, 1)
            actv(vc_p, banks[7][:, 0:P], ACT.Copy).then_inc(cmpo_saved, 1)
            for pair in range(4):
                for g in range(0, 16, 2):
                    i = 16 * pair + g
                    sc.wait_ge(pg_banked, i + 1)
                    if g == 0:
                        sc.wait_ge(hid_banked, pair + 1)
                    c0 = g * 256
                    actv(kvT[:, :, c0:c0 + 256], banks[i % 2][:, :].rearrange("p (s n) -> p s n", s=2), ACT.Copy).then_inc(pg_saved[0], 1)
                sc.wait_ge(hid_banked, pair + 2)
                actv(gk, banks[4][:, 0:2 * NCMP_S], ACT.Gelu_apprx_tanh, bias=cbias[:, 0:1])
                actv(gv, banks[5][:, 0:2 * NCMP_S], ACT.Gelu_apprx_tanh, bias=cbias[:, 1:2]).then_inc(gelu_done, 1)
                sc.wait_ge(cmpo_banked, pair + 2)
                actv(kcT_s[:, 2 * pair:2 * pair + 2], banks[6][:, 0:2 * NCMP_S].rearrange("p (b n) -> p b n", b=2), ACT.Copy).then_inc(cmpo_saved, 1)
                actv(vc_s[0:NCMP_S, 2 * pair:2 * pair + 2], banks[7][0:NCMP_S, 0:2 * P].rearrange("p (b n) -> p b n", b=2), ACT.Copy).then_inc(cmpo_saved, 1)
            for n in range(4):
                sc.wait_ge(kt_banked, n + 1)
                actv(KT[:, n], banks[n % 2][:, :], ACT.Copy).then_inc(kt_saved, 1)
            for t in range(4):
                sc.wait_ge(cs_max, t + 1)
                actv(sc_c[:, :, 0:NCMP_P], sc_c[:, :, 0:NCMP_P], ACT.Exp).then_inc(cs_exp, 1)
                sc.wait_ge(pct_banked, t + 1)
                actv(PcT, banks[1][:, :].rearrange("p (j n) -> p j n", j=4), ACT.Copy).then_inc(pct_saved, 1)
                sc.wait_ge(co_banked, t + 1)
                for j in range(4):
                    last = actv(otok[:, t].rearrange("p (a j d) -> p j a d", j=4, d=HD)[:, j],
                                banks[(2, 3, 5, 6)[j]][:, 0:256].rearrange("p (a d) -> p a d", d=HD), ACT.Copy)
                last.then_inc(co_saved, 1)

            def exps(i):
                n = (i % 4 + 1) * P
                sc.wait_ge(at_max, 2 * (i + 1))
                for br in range(2):
                    last = actv(sc_p[i % 2][:, br, 0:n], sc_p[i % 2][:, br, 0:n], ACT.Exp, scale=-1.0, bias=ast[i % 4][:, br:br + 1],
                                accum_out=ast[i % 4][:, 4 + br:5 + br])
                last.then_inc(at_exp, 1)

            exps(0)
            for i in range(64):
                sc.wait_ge(at_tr_banked, i + 1)
                if i >= 2:
                    sc.wait_ge(at_o_banked, i - 1)
                n = i % 4 + 1
                actv(PT[i % 2][:, 0, 0:n], banks[4][:, 0:n * P].rearrange("p (k n) -> p k n", n=P), ACT.Copy).then_inc(at_pt_saved, 1)
                if i + 1 < 64:
                    exps(i + 1)

            sc.wait_ge(qr_banked, 1)
            for half in range(2):
                src = banks[half][0:NS_TOK, :].rearrange("p (g d) -> p g d", g=G)
                last = actv(dupK[0:NS_TOK, 0:2].rearrange("p a b c -> p (a b) c")[:, :, half * 64:half * 64 + 64], src, ACT.Copy)
            last.then_inc(qr_saved, 1)
            sc.wait_ge(qd_banked, 1)
            actv(knT, banks[3][:, 0:2 * NS_TOK].rearrange("p (b n) -> p b n", b=2), ACT.Copy).then_inc(kn_saved, 1)
            sc.wait_ge(dec_in, 16 * 8)
            ktg = 0
            ptd = 0
            for job, (pair, br) in enumerate(SAMPLE_JOBS):
                nk = (NCMP_S, PAST + NS_TOK, WIN + NS_TOK)[br + 1]
                if br >= 0:
                    ntile = (16, 4)[br]
                    for g in range(2 * ntile // 4):
                        sc.wait_ge(ks_banked, ktg + 1)
                        b2, c0 = divmod(4 * g, ntile)
                        actv(KTs[:, b2, c0 * P:c0 * P + 512], banks[4 + ktg % 2][:, :], ACT.Copy).then_inc(ks_saved, 1)
                        ktg += 1
                sc.wait_ge(sd_max, job + 1)
                actv(Ss[:, 0:nk], Ss[:, 0:nk], ACT.Exp, bias=sst[:, 1:2], accum_out=sst[:, 2:3]).then_inc(sd_sum, 1)
                if br < 0:
                    ptd += 1
                    sc.wait_ge(ptd_banked, ptd)
                    actv(PTs[0:NCMP_S, 0], banks[1][0:NCMP_S, 0:P], ACT.Copy).then_inc(ptd_saved, 1)
                    sc.wait_ge(imp_banked, pair + 1)
                    actv(imp, banks[2][:, 0:NBLK], ACT.Copy).then_inc(imp_saved, 1)
                else:
                    for g in range(ntile // 4):
                        ptd += 1
                        sc.wait_ge(ptd_banked, ptd)
                        last = actv(PTs[:, 4 * g:4 * g + 4], banks[4 + g % 2][:, :].rearrange("p (k n) -> p k n", n=P), ACT.Copy)
                        if g == ntile // 4 - 1:
                            last = actv(PTs[0:NS_TOK, 16], banks[7][0:NS_TOK, 0:P], ACT.Copy)
                        last.then_inc(ptd_saved, 1)

        @block.gpsimd
        def _(pool):
            step = Steps(pool, pool_step)
            for kv in range(2):
                step(nc.gpsimd.memset(W1[kv * 64:kv * 64 + 64, :, :, 64 - kv * 64:128 - kv * 64], 0.0))
            pool.wait_ge(prj_banked, 16)
            for kv in range(2):
                step(nc.gpsimd.memset(W2kd[kv * 64:kv * 64 + 64, 1 - kv], 0.0))
                for wt in (W2k, W2v):
                    step(nc.gpsimd.memset(wt[kv * 64:kv * 64 + 64, 64 - kv * 64:128 - kv * 64], 0.0))
            step(nc.gpsimd.memset(QD, 0.0), q_zeroed)
            step(nc.gpsimd.memset(gv[:, 0:P], 0.0), q_zeroed)
            pool.wait_ge(cmpo_saved, 2 + 8)
            for br in range(2):
                for kv in range(2):
                    c0 = (br + 1) * 256 + kv * 64
                    for half in range(2):
                        step(nc.gpsimd.tensor_copy(dupK[:, 2 * br + kv, :, half * 64:half * 64 + 64], kvt[:, 0:4, c0:c0 + 64]))
            step(nc.gpsimd.memset(sc_c, 0.0), dup_ready)
            pool.wait_ge(att_in, 16 * 3)
            for hd in range(QH):
                if hd >= 2:
                    pool.wait_ge(at_max, 8 * (hd - 1))
                step(nc.gpsimd.tensor_scalar(hbias[:, hd % 2], dist, -8.0 * SLOPES[hd], None, ALU.mult), hb_ready)

        @block.vector
        def _(dve):
            step = Steps(dve, dve_step)
            V = nc.vector
            dve.wait_ge(gt_tanh, 1)
            step(V.tensor_scalar(mgB, mgB, 1.0, 0.5, ALU.add, ALU.mult))
            step(V.tensor_scalar(gt[:, 0:4], gt[:, 0:4], 1.0, 0.5, ALU.add, ALU.mult))
            step(V.tensor_scalar(gt[0:NS_TOK, 4], gt[0:NS_TOK, 4], 1.0, 0.5, ALU.add, ALU.mult), gt_ready)
            for pair in range(4):
                for g in range(1, 16, 2):
                    i = 16 * pair + g
                    dve.wait_ge(pg_banked, i + 1)
                    dve.wait_ge(hid_banked, pair + 1)
                    V.tensor_copy(kvT[:, :, g * 256:g * 256 + 256], banks[i % 2][:, :].rearrange("p (s n) -> p s n", s=2)).then_inc(pg_saved[1], 1)
            dve.wait_ge(dup_ready, 1)
            dve.wait_ge(att_in, 16 * 3)
            g4 = gt.rearrange("p t (h b) -> p t h b", b=3)
            for t in range(4):
                live = sc_c[:, :, 0:NCMP_P]
                wide = lambda v: v.rearrange("p (h o) -> p h o", o=1).to_broadcast([P, QH, NCMP_P])
                dve.wait_ge(cs_banked, t + 1)
                if t >= 1:
                    dve.wait_ge(pct_banked, t)
                for odd in range(2):
                    step(V.scalar_tensor_tensor(live.rearrange("p (h o) c -> p o h c", o=2)[:, odd],
                                                banks[4 * odd][:, 0:256].rearrange("p (h c) -> p h c", c=32)[:, :, 0:NCMP_P], 0.125,
                                                cmp_bias[:, t].rearrange("p (h o) c -> p o h c", o=2)[:, odd], ALU.mult, ALU.add))
                step(V.tensor_reduce(cst[0], live, AX.X, ALU.max))
                step(V.tensor_tensor(live, live, wide(cst[0]), ALU.subtract), cs_max)
                dve.wait_ge(cs_exp, t + 1)
                step(V.tensor_reduce(cst[0], live, AX.X, ALU.add))
                step(V.reciprocal(cst[0], cst[0]))
                step(V.tensor_scalar(cst[0], cst[0], cmp_any[:, t:t + 1], None, ALU.mult))
                step(V.tensor_tensor(cst[0], cst[0], g4[:, t, :, 0], ALU.mult))
                step(V.tensor_tensor(live, live, wide(cst[0]), ALU.mult), cs_ready)
            dve.wait_ge(co_saved, 4)

            def maxima(i):
                hd, t = divmod(i, 4)
                n = (t + 1) * P
                dve.wait_ge(at_banked, i + 1)
                dve.wait_ge(hb_ready, hd + 1)
                if i >= 2:
                    dve.wait_ge(at_tr_banked, i - 1)
                for br in range(2):
                    V.tensor_tensor_reduce(out=sc_p[i % 2][:, br, 0:n], in0=banks[2 * (i % 2) + br][:, 0:n],
                                           in1=hbias[:, hd % 2, NP_TOK - n:], scale=-0.125, scalar=3e38, op0=ALU.add, op1=ALU.min,
                                           accum_out=ast[i % 4][:, br:br + 1]).then_inc(at_max, 1)

            def combine(i):
                hd, t = divmod(i, 4)
                a = ast[i % 4]
                dst = otok[:, t, hd * 64:hd * 64 + 64]
                dve.wait_ge(at_o_banked, i + 1)
                step(V.reciprocal(a[:, 6:8], a[:, 4:6]))
                step(V.tensor_tensor(a[:, 6:8], a[:, 6:8], g4[:, t, hd, 1:3], ALU.mult))
                step(V.scalar_tensor_tensor(dst, banks[6 + i % 2][:, 0:64], a[:, 6:7], dst, ALU.mult, ALU.add))
                step(V.scalar_tensor_tensor(dst, banks[6 + i % 2][:, 64:128], a[:, 7:8], dst, ALU.mult, ALU.add), at_done)

            maxima(0)
            for i in range(64):
                if i + 1 < 64:
                    maxima(i + 1)
                dve.wait_ge(at_tr_banked, i + 1)
                if i >= 2:
                    dve.wait_ge(at_o_banked, i - 1)
                n = i % 4 + 1
                V.tensor_copy(PT[i % 2][:, 1, 0:n], banks[5][:, 0:n * P].rearrange("p (k n) -> p k n", n=P)).then_inc(at_pt_saved_v, 1)
                if i >= 1:
                    combine(i - 1)
            combine(63)

            dve.wait_ge(qd_banked, 1)
            dve.wait_ge(q_zeroed, 2)
            for kv in range(2):
                half = slice(kv * 64, kv * 64 + 64)
                last = V.tensor_copy(QD[half, :, kv * 32:kv * 32 + 32].rearrange("p b (t g) -> p b t g", g=G),
                                     banks[2][half, 0:256].rearrange("p (g b t) -> p b t g", g=G, t=NT))
            step(last, qd_ready)
            dve.wait_ge(dec_in, 16 * 8)
            for job, (pair, br) in enumerate(SAMPLE_JOBS):
                nk = (NCMP_S, PAST + NS_TOK, WIN + NS_TOK)[br + 1]
                dve.wait_ge(sd_banked, job + 1)
                if br < 0:
                    step(V.scalar_tensor_tensor(Ss[:, 0:NCMP_S], banks[0][:, 0:NCMP_S], 0.125, cmp_bias_s, ALU.mult, ALU.add))
                else:
                    bias = (slc_bias_s, win_bias_s)[br]
                    for c in range((4, 1)[br]):
                        cs = slice(c * 512, c * 512 + 512)
                        step(V.scalar_tensor_tensor(Ss[:, cs], banks[c][:, :], 0.125, bias[:, cs], ALU.mult, ALU.add))
                    step(V.scalar_tensor_tensor(Ss[:, nk - NS_TOK:nk], banks[7][:, 0:NS_TOK], 0.125, new_bias_s[:, pair], ALU.mult, ALU.add))
                    if br == 0:
                        step(V.tensor_tensor(Ss[:, 0:PAST].rearrange("p (n k) -> p n k", k=64), Ss[:, 0:PAST].rearrange("p (n k) -> p n k", k=64),
                                             kept[:, pair, 0:32].rearrange("p (n o) -> p n o", o=1).to_broadcast([P, 32, 64]), ALU.add))
                step(V.tensor_reduce(sst[:, 0:1], Ss[:, 0:nk], AX.X, ALU.max))
                step(V.tensor_scalar(sst[:, 1:2], sst[:, 0:1], -1.0, None, ALU.mult), sd_max)
                dve.wait_ge(sd_sum, job + 1)
                step(V.reciprocal(sst[:, 3:4], sst[:, 2:3]))
                if br < 0:
                    step(V.tensor_scalar(Ss[:, 0:nk], Ss[:, 0:nk], sst[:, 3:4], None, ALU.mult), sd_exp)
                    step(V.tensor_copy(sst[:, 4:6], kv_rows))
                else:
                    step(V.tensor_scalar(sst[:, 4:6], kv_rows, sst[:, 3:4], None, ALU.mult), sd_exp)
                dve.wait_ge(od_banked, job + 1)
                if job >= 1:
                    dve.wait_ge(od_out, 16 * job)
                step(V.tensor_scalar(orow, banks[6][:, 0:64], sst[:, 4:5], None, ALU.mult))
                step(V.scalar_tensor_tensor(orow, banks[6][:, 64:128], sst[:, 5:6], orow, ALU.mult, ALU.add), od_saved)
                if br < 0:
                    dve.wait_ge(grp_banked, pair + 1)
                    step(V.tensor_tensor(sel[:, 1], banks[3][:, 0:NBLK], forced, ALU.add))
                    step(V.max(sst[:, 8:16], sel[:, 1]))
                    step(V.match_replace(sel[:, 2], sst[:, 8:16], sel[:, 1], -3e38))
                    step(V.max(sst[:, 8:16], sel[:, 2]))
                    step(V.match_replace(sel[:, 1], sst[:, 8:16], sel[:, 2], -3e38))
                    step(V.tensor_scalar(kept[:, pair], sel[:, 1], -1e37, NEG, ALU.is_gt, ALU.mult), sel_ready)
            dve.wait_ge(odec_in, 16 * 24)
            n = NS_TOK
            od = [odec[0:n, br * D:(br + 1) * D].rearrange("p (h d) -> p h d", d=HD) for br in range(3)]
            og = [g4[0:n, 4, :, br:br + 1].to_broadcast([n, QH, HD]) for br in range(3)]
            o4 = otok[0:n, 4].rearrange("p (h d) -> p h d", d=HD)
            step(V.tensor_tensor(o4, od[0], og[0], ALU.mult))
            step(V.tensor_tensor(od[1], od[1], og[1], ALU.mult))
            step(V.tensor_tensor(od[2], od[2], og[2], ALU.mult))
            step(V.tensor_tensor(o4, o4, od[1], ALU.add))
            step(V.tensor_tensor(o4, o4, od[2], ALU.add), odec_ready)
            for t in range(NTILE):
                t0, n = tok(t)
                for half in range(2):
                    i = 2 * t + half
                    ks = slice(4 * half, 4 * half + 4)
                    dve.wait_ge(of_banked, i + 1)
                    step(V.tensor_tensor(mgB[:, ks, t0:t0 + n], banks[i % 2][:, :].rearrange("p (k n) -> p k n", k=4)[:, :, 0:n],
                                         mgB[:, ks, t0:t0 + n], ALU.mult))
                    step(V.tensor_tensor(hT[:, ks, t0:t0 + n], hT[:, ks, t0:t0 + n], mgB[:, ks, t0:t0 + n], ALU.add), of_ready)

        block_ctx.close()
        end_block()

        dve_step = sem("dve_step")
        act_step = sem("act_step")
        pool_step = sem("pool_step")
        d_in = sem("d_in")
        r_in = sem("r_in")
        sh_in = sem("sh_in")
        o_banked = sem("o_banked")
        res_ready = sem("res_ready")
        var_ready = sem("var_ready")
        rstd_ready = sem("rstd_ready")
        x1_ready = sem("x1_ready")
        x1_out = sem("x1_out")
        x1t_banked = sem("x1t_banked")
        x1t_ready = sem("x1t_ready")
        lg_banked = sem("lg_banked")
        sc_exp = sem("sc_exp")
        lg_saved = sem("lg_saved")
        mask_ready = sem("mask_ready")
        pos_banked = sem("pos_banked")
        s_gu_banked = sem("s_gu_banked")
        s_sg_ready = sem("s_sg_ready")
        s_h_ready = sem("s_h_ready")
        s_ht_banked = sem("s_ht_banked")
        s_ht_saved = sem("s_ht_saved")
        s_y_banked = sem("s_y_banked")
        s_y_added = sem("s_y_added")
        block_ctx = ExitStack()
        block = block_ctx.enter_context(nc.Block())

        @block.sync
        def _(sp):
            sp.dma_start(x1[:, 0:4, :], io["x_prompt"][0].rearrange("(t p) d -> p t d", p=P)).then_inc(d_in, 16)
            sp.dma_start(x1[0:NS_TOK, 4, :], io["x_sample"].rearrange("b t d -> (b t) d")).then_inc(d_in, 16)
            for n, name in enumerate(("ln1_g", "ln1_b", "ln2_g", "ln2_b")):
                sp.dma_start(lnw[:, n], io[name].to_broadcast([P, D])).then_inc(d_in, 16)
            sp.dma_start(wr, io["w_router"][0].rearrange("(k p) n -> p k n", p=P)).then_inc(r_in, 16)
            sp.dma_start(brow, io["b_router"].to_broadcast([P, NE])).then_inc(r_in, 16)
            sp.dma_start(before8, io["before8"].rearrange("p (a b) -> p a b", a=G)).then_inc(r_in, 16)
            sp.dma_start(tokens, io["tokens"].rearrange("p (t c) -> p t c", c=2)).then_inc(r_in, 16)
            sp.dma_start(slots, io["slots"]).then_inc(r_in, 16)
            sp.dma_start(shgu[:, :, 0:DE], io["w_sh_gate"][0].rearrange("(k p) n -> p k n", p=P)).then_inc(sh_in, 16)
            sp.dma_start(shgu[:, :, DE:], io["w_sh_up"][0].rearrange("(k p) n -> p k n", p=P)).then_inc(sh_in, 16)
            sp.dma_start(shd, io["w_sh_down"][0].rearrange("(k p) n -> p k n", p=P)).then_inc(sh_in, 16)
            for t in range(NTILE):
                t0, n = tok(t)
                sp.wait_ge(x1_ready, t + 1)
                sp.dma_start(x1_rows[t0:t0 + n], x1[0:n, t]).then_inc(x1_out, 16)
            sp.wait_ge(x1_out, 16 * NTILE)

        @block.tensor
        def _(pe):
            mm, tr = nc.tensor.matmul, nc.tensor.transpose
            for t in range(NTILE):
                t0, n = tok(t)
                if t >= 2:
                    pe.wait_ge(res_ready, 2 * (t - 1))
                for half in range(2):
                    for k in range(KD):
                        last = mm(banks[2 * (t % 2) + half][0:n, :], hT[:, k, t0:t0 + n], wout[k // 4][:, k % 4, half * 512:half * 512 + 512],
                                  start=(k == 0), stop=(k == KD - 1))
                last.then_inc(o_banked, 1)
            for t in range(NTILE):
                t0, n = tok(t)
                pe.wait_ge(x1_ready, t + 1)
                for half in range(2):
                    i = 2 * t + half
                    if i >= 2:
                        pe.wait_ge(x1t_ready, i - 1)
                    for k in range(4):
                        last = tr(banks[4 + i % 2][:, k * P:k * P + n], x1[0:n, t, (4 * half + k) * P:(4 * half + k + 1) * P], ident[0:n, 0:n])
                    last.then_inc(x1t_banked, 1)
            pe.wait_ge(x1t_ready, 2 * NTILE)
            pe.wait_ge(r_in, 80)
            for t in range(NTILE):
                t0, n = tok(t)
                for k in range(KD):
                    last = mm(banks[6][0:n, t * NE:(t + 1) * NE], xT[:, k, t0:t0 + n], wr[:, k], start=(k == 0), stop=(k == KD - 1))
            last.then_inc(lg_banked, 1)
            pe.wait_ge(sh_in, 48)
            for t in range(NTILE):
                t0, n = tok(t)
                if t >= 1:
                    pe.wait_ge(s_h_ready, t)
                for k in range(KD):
                    last = mm(banks[0][0:n, :], xT[:, k, t0:t0 + n], shgu[:, k], start=(k == 0), stop=(k == KD - 1))
                last.then_inc(s_gu_banked, 1)
                pe.wait_ge(s_h_ready, t + 1)
                for f in range(2):
                    last = tr(banks[1][:, f * P:f * P + n], shs[1][0:n, f * P:f * P + P], ident[0:n, 0:n])
                last.then_inc(s_ht_banked, 1)
                pe.wait_ge(s_ht_saved, t + 1)
                if t >= 1:
                    pe.wait_ge(s_y_added, 2 * t)
                for half in range(2):
                    for f in range(2):
                        last = mm(banks[2 + half][0:n, :], shs[2][:, f * P:f * P + n], shd[:, f, half * 512:half * 512 + 512],
                                  start=(f == 0), stop=(f == 1))
                last.then_inc(s_y_banked, 1)
            pe.wait_ge(mask_ready, 1)
            mask = rt[1]
            for t in range(NTILE):
                for u in range(t + 1):
                    last = mm(banks[7][:, t * NE:(t + 1) * NE], (tri if u == t else ones)[:, :], mask[:, u], start=(u == 0), stop=(u == t))
            for u in range(NTILE):
                last = mm(banks[7][:, 320:384], ones[:, :], mask[:, u], start=(u == 0), stop=(u == 4))
            last.then_inc(pos_banked, 1)

        @block.scalar
        def _(sc):
            actv = nc.scalar.activation
            step = Steps(sc, act_step)
            for t in range(NTILE):
                n = tok(t)[1]
                sc.wait_ge(var_ready, t + 1)
                step(actv(lnst[0:n, 2:3], lnst[0:n, 1:2], ACT.Ln, bias=eps[0:n, 1:2]))
                actv(lnst[0:n, 3:4], lnst[0:n, 2:3], ACT.Exp, scale=-0.5).then_inc(rstd_ready, 1)
            for t in range(NTILE):
                t0, n = tok(t)
                for half in range(2):
                    i = 2 * t + half
                    sc.wait_ge(x1t_banked, i + 1)
                    actv(xT[:, 4 * half:4 * half + 4, t0:t0 + n], banks[4 + i % 2][:, :].rearrange("p (k n) -> p k n", k=4)[:, :, 0:n],
                         ACT.Copy).then_inc(x1t_ready, 1)
            sc.wait_ge(lg_saved, 1)
            actv(rt[0], rt[0], ACT.Exp, scale=-1.0).then_inc(sc_exp, 1)
            for t in range(NTILE):
                n = tok(t)[1]
                sc.wait_ge(s_gu_banked, t + 1)
                actv(shs[0][0:n], banks[0][0:n, 0:DE], ACT.Silu).then_inc(s_sg_ready, 1)
                sc.wait_ge(s_ht_banked, t + 1)
                actv(shs[2].rearrange("p (f n) -> p f n", f=2)[:, :, 0:n], banks[1][:, 0:2 * P].rearrange("p (f n) -> p f n", f=2)[:, :, 0:n],
                     ACT.Copy).then_inc(s_ht_saved, 1)

        @block.vector
        def _(dve):
            step = Steps(dve, dve_step)
            V = nc.vector
            dve.wait_ge(d_in, 16 * 6)

            def norm(t, i, gain, done):
                n = tok(t)[1]
                for half in range(2):
                    step(V.bn_stats(bnst[0:n, half], x1[0:n, t, half * 512:half * 512 + 512]))
                step(V.bn_aggr(lnst[0:n, 0:2], bnst[0:n]), var_ready)
                dve.wait_ge(rstd_ready, i + 1)
                step(V.tensor_scalar(x1[0:n, t], x1[0:n, t], lnst[0:n, 0:1], lnst[0:n, 3:4], ALU.subtract, ALU.mult))
                step(V.tensor_tensor(x1[0:n, t], x1[0:n, t], lnw[0:n, gain], ALU.mult))
                step(V.tensor_tensor(x1[0:n, t], x1[0:n, t], lnw[0:n, gain + 1], ALU.add), done)

            for t in range(NTILE):
                n = tok(t)[1]
                dve.wait_ge(o_banked, t + 1)
                for half in range(2):
                    cs = slice(half * 512, half * 512 + 512)
                    step(V.scalar_tensor_tensor(x1[0:n, t, cs], x1[0:n, t, cs], ALPHA, banks[2 * (t % 2) + half][0:n, :], ALU.mult, ALU.add), res_ready)
                norm(t, t, 0, x1_ready)
            dve.wait_ge(lg_banked, 1)
            dve.wait_ge(r_in, 80)
            score, sel_, tmp, tmp2, pre, pre2 = rt
            mask = sel_
            step(V.memset(score[:, 4], 0.0))
            step(V.tensor_copy(score[:, 0:4], banks[6][:, 0:4 * NE].rearrange("p (t e) -> p t e", e=NE)))
            step(V.tensor_copy(score[0:NS_TOK, 4], banks[6][0:NS_TOK, 4 * NE:5 * NE]), lg_saved)
            dve.wait_ge(x1_out, 16 * NTILE)
            for t in range(NTILE):
                n = tok(t)[1]
                dve.wait_ge(s_gu_banked, t + 1)
                dve.wait_ge(s_sg_ready, t + 1)
                step(V.tensor_tensor(shs[1][0:n], shs[0][0:n], banks[0][0:n, DE:], ALU.mult), s_h_ready)
                dve.wait_ge(s_y_banked, t + 1)
                for half in range(2):
                    cs = slice(half * 512, half * 512 + 512)
                    step(V.scalar_tensor_tensor(x1[0:n, t, cs], x1[0:n, t, cs], ALPHA, banks[2 + half][0:n, :], ALU.mult, ALU.add), s_y_added)
            dve.wait_ge(sc_exp, 1)
            step(V.tensor_scalar(score, score, 1.0, None, ALU.add))
            step(V.reciprocal(score, score))
            step(V.tensor_tensor(sel_, score, brow.rearrange("p (o e) -> p o e", o=1).to_broadcast([P, NTILE, NE]), ALU.add))
            for t in range(NTILE):
                for g in range(G):
                    last = V.max(m8[:, t, g], sel_[:, t, g * 8:g * 8 + 8])
                    step(last)
            step(V.tensor_tensor(gs, m8[:, :, :, 0], m8[:, :, :, 1], ALU.add))
            wide = gs.rearrange("p t (o i) -> p t o i", o=1).to_broadcast([P, NTILE, G, G])
            tall = gs.rearrange("p t (j o) -> p t j o", o=1).to_broadcast([P, NTILE, G, G])
            step(V.tensor_tensor(gr[0], wide, tall, ALU.is_gt))
            step(V.tensor_tensor(gr[1], wide, tall, ALU.is_equal))
            step(V.tensor_tensor(gr[1], gr[1], before8.rearrange("p (o j) i -> p o j i", o=1).to_broadcast([P, NTILE, G, G]), ALU.mult))
            step(V.tensor_tensor(gr[0], gr[0], gr[1], ALU.add))
            step(V.tensor_reduce(gs, gr[0], AX.X, ALU.add))
            step(V.tensor_scalar(gs, gs, 3.5, NEG, ALU.is_gt, ALU.mult))
            eight = lambda v: v.rearrange("p t (g j) -> p (t g) j", j=8)
            step(V.tensor_tensor(eight(sel_), eight(sel_), gs.rearrange("p t (g o) -> p (t g) o", o=1).to_broadcast([P, NTILE * G, 8]), ALU.add))
            for t in range(NTILE):
                step(V.max(v8[:, t], sel_[:, t]))
            sixth = v8[:, :, TOP_K - 1:TOP_K].to_broadcast([P, NTILE, NE])
            step(V.tensor_tensor(tmp, sel_, sixth, ALU.is_gt))
            step(V.tensor_reduce(cnt, tmp, AX.X, ALU.add))
            step(V.tensor_scalar(cnt, cnt, -1.0, float(TOP_K), ALU.mult, ALU.add))
            step(V.tensor_tensor(tmp2, sel_, sixth, ALU.is_equal))
            step(V.tensor_copy(pre, tmp2))
            for n in range(6):
                sh = 1 << n
                step(V.tensor_copy(pre2[:, :, 0:sh], pre[:, :, 0:sh]))
                step(V.tensor_tensor(pre2[:, :, sh:], pre[:, :, sh:], pre[:, :, 0:NE - sh], ALU.add))
                pre, pre2 = pre2, pre
            step(V.tensor_tensor(pre, pre, cnt.rearrange("p (t o) -> p t o", o=1).to_broadcast([P, NTILE, NE]), ALU.is_le))
            step(V.tensor_tensor(tmp2, tmp2, pre, ALU.mult))
            step(V.tensor_tensor(tmp, tmp, tmp2, ALU.add))
            G_ = R[:, :, 2]
            step(V.tensor_tensor(G_, score, tmp, ALU.mult))
            step(V.tensor_reduce(cnt, G_, AX.X, ALU.add))
            step(V.reciprocal(cnt, cnt))
            step(V.tensor_scalar(cnt, cnt, ROUTED_SCALE, None, ALU.mult))
            step(V.tensor_tensor(G_, G_, cnt.rearrange("p (t o) -> p t o", o=1).to_broadcast([P, NTILE, NE]), ALU.mult))
            for p0 in (32, 64):
                step(V.memset(tmp[p0:2 * p0, 4], 0.0))
            step(V.tensor_copy(mask, tmp), mask_ready)
            step(V.tensor_copy(pre, mask))
            for n in range(6):
                sh = 1 << n
                step(V.tensor_copy(pre2[:, :, 0:sh], pre[:, :, 0:sh]))
                step(V.tensor_tensor(pre2[:, :, sh:], pre[:, :, sh:], pre[:, :, 0:NE - sh], ALU.add))
                pre, pre2 = pre2, pre
            step(V.tensor_copy(R[:, :, 0], tokens[:, :, 0:1].to_broadcast([P, NTILE, NE])))
            step(V.tensor_tensor(R[:, :, 1], pre, tokens[:, :, 1:2].to_broadcast([P, NTILE, NE]), ALU.add))
            dve.wait_ge(pos_banked, 1)
            step(V.tensor_tensor(pos, banks[7][:, 0:NTILE * NE].rearrange("p (t e) -> p t e", e=NE), mask, ALU.mult))
            step(V.tensor_scalar(pos, pos, -1.0, None, ALU.add))
            step(V.tensor_reduce(cnt[:, 0:1], banks[7][:, 320:384], AX.X, ALU.max))
            step(V.tensor_scalar(over_i[0:1, 0:1], cnt[0:1, 0:1], float(P), None, ALU.is_gt))

        block_ctx.close()
        end_block()

        we_in = [sem("we_in0"), sem("we_in1")]
        wd_in = [sem("wd_in0"), sem("wd_in1")]
        xg_in = [sem("xg_in0"), sem("xg_in1")]
        y_out = [sem("y_out0"), sem("y_out1")]
        xg_zeroed = sem("xg_zeroed")
        pool_turns = sem("pool_turns")
        onehot_ready = sem("onehot_ready")
        list_banked = sem("list_banked")
        empty_ready = sem("empty_ready")
        list_ready = sem("list_ready")
        xt_banked = sem("xt_banked")
        xt_saved_a = sem("xt_saved_a")
        xt_saved_v = sem("xt_saved_v")
        gu_banked = sem("gu_banked")
        sg_ready = sem("sg_ready")
        h_ready = sem("h_ready")
        ht_banked = sem("ht_banked")
        ht_saved = sem("ht_saved")
        y_banked = sem("y_banked")
        ys_a = sem("ys_a")
        ys_v = sem("ys_v")
        block_ctx = ExitStack()
        block = block_ctx.enter_context(nc.Block())
        LAST = NE - 4

        def reached(eng, s, value):
            if not isinstance(value, int) or value > 0:
                eng.wait_ge(s, value)

        def all_experts(eng, expert):
            for u in range(4):
                expert(u, u // 2, u, False)
            with eng.Fori(1, NE // 4 - 1) as it:
                for u in range(4):
                    expert(4 * it + u, 2 * it + u // 2, u, False)
            for u in range(4):
                expert(LAST + u, (LAST + u) // 2, u, True)

        @block.sync
        def _(sp):
            def load(e, u):
                one = bass.ds(e, 1)
                for n, name in enumerate(("w_exp_gate", "w_exp_up")):
                    sp.dma_start(wgu[u][:, :, n * DE:(n + 1) * DE], io[name][0, one].rearrange("o (k p) n -> p (o k) n", p=P)).then_inc(we_in[u], 16)

            def load_down(e, u):
                sp.dma_start(wde[u], io["w_exp_down"][0, bass.ds(e, 1)].rearrange("o (k p) n -> p (o k) n", p=P)).then_inc(wd_in[u], 16)

            for u in range(2):
                load(u, u)
                load_down(u, u)
            with sp.Fori(0, NE // 2 - 1) as it:
                for u in range(2):
                    sp.wait_ge(gu_banked, 2 * it + (u + 1))
                    load(2 * it + (u + 2), u)
                    sp.wait_ge(y_banked, 2 * it + (u + 1))
                    load_down(2 * it + (u + 2), u)

        @block.gpsimd
        def _(pool):
            def gather(e, u):
                pool.wait_ge(list_ready, e + 1)
                pool.sem_inc(pool_turns, 1)
                nc.gpsimd.indirect_dma_start(out=xg[u % 2], out_offset=None, in_=x1_rows,
                                             in_offset=bass.IndirectOffsetOnAxis(ap=rows_i[:, u, 0:1], axis=0),
                                             bounds_check=NTOK - 1, oob_is_err=False).then_inc(xg_in[u % 2], 16)

            def scatter(e, u):
                pool.wait_ge(ys_a, e + 1)
                pool.wait_ge(ys_v, e + 1)
                pool.sem_inc(pool_turns, 1)
                nc.gpsimd.indirect_dma_start(out=y_rows, out_offset=bass.IndirectOffsetOnAxis(ap=rows_i[:, u, 1:2], axis=0),
                                             in_=ys[u % 2], in_offset=None,
                                             bounds_check=NTOK * TOP_K - 1, oob_is_err=False).then_inc(y_out[u % 2], 16)

            for u in range(2):
                nc.gpsimd.memset(xg[u], 0.0).then_inc(xg_zeroed, 1)
            pool.wait_ge(xg_zeroed, 2)
            gather(0, 0)
            gather(1, 1)

            def expert(e, half, u, last):
                if not last or u < 2:
                    gather(e + 2, (u + 2) % 4)
                scatter(e, u)

            all_experts(pool, expert)
            pool.wait_ge(y_out[0], 16 * NE // 2)
            pool.wait_ge(y_out[1], 16 * NE // 2)

        @block.tensor
        def _(pe):
            mm, tr = nc.tensor.matmul, nc.tensor.transpose

            def make_list(e, u):
                pe.wait_ge(onehot_ready, e + 1)
                reached(pe, list_ready, e)
                for t in range(NTILE):
                    last = mm(banks[7][:, 0:3], onehot[u % 2][:, t], R[:, t, :, bass.ds(e, 1)].rearrange("p c o -> p (c o)"),
                              start=(t == 0), stop=(t == NTILE - 1))
                last.then_inc(list_banked, 1)

            def turn(e, u):
                pe.wait_ge(xg_in[u % 2], (e // 2 + 1) * 16 if isinstance(e, int) else (e - u % 2) * 8 + 16)
                for k in range(KD):
                    last = tr(banks[k // 4][:, k % 4 * P:(k % 4 + 1) * P], xg[u % 2][:, k * P:(k + 1) * P], ident[:, :])
                last.then_inc(xt_banked, 1)

            def expert(e, half, u, last):
                pe.wait_ge(we_in[u % 2], half * 32 + 32)
                pe.wait_ge(xt_saved_a, e + 1)
                pe.wait_ge(xt_saved_v, e + 1)
                reached(pe, h_ready, e)
                for k in range(KD):
                    ins = mm(banks[2][:, :], xgT[:, k], wgu[u % 2][:, k], start=(k == 0), stop=(k == KD - 1))
                ins.then_inc(gu_banked, 1)
                if not last or u < 3:
                    turn(e + 1, (u + 1) % 4)
                pe.wait_ge(h_ready, e + 1)
                reached(pe, ht_saved, e)
                for f in range(2):
                    ins = tr(banks[3][:, f * P:(f + 1) * P], hid[:, f * P:(f + 1) * P], ident[:, :])
                ins.then_inc(ht_banked, 1)
                if not last or u < 2:
                    make_list(e + 2, u)
                pe.wait_ge(wd_in[u % 2], half * 16 + 16)
                pe.wait_ge(ht_saved, e + 1)
                reached(pe, ys_a, e)
                reached(pe, ys_v, e)
                for n in range(2):
                    for f in range(2):
                        ins = mm(banks[4 + n][:, :], hidT[:, f], wde[u % 2][:, f, n * 512:n * 512 + 512], start=(f == 0), stop=(f == 1))
                ins.then_inc(y_banked, 1)

            make_list(0, 0)
            make_list(1, 1)
            turn(0, 0)
            all_experts(pe, expert)

        @block.scalar
        def _(sc):
            actv = nc.scalar.activation

            def save_rows(e):
                sc.wait_ge(xt_banked, e + 1)
                actv(xgT[:, 0:4], banks[0][:, :].rearrange("p (k n) -> p k n", k=4), ACT.Copy).then_inc(xt_saved_a, 1)

            def expert(e, half, u, last):
                sc.wait_ge(gu_banked, e + 1)
                reached(sc, h_ready, e)
                actv(sg, banks[2][:, 0:DE], ACT.Silu).then_inc(sg_ready, 1)
                if not last or u < 3:
                    save_rows(e + 1)
                sc.wait_ge(ht_banked, e + 1)
                reached(sc, y_banked, e)
                actv(hidT, banks[3][:, 0:2 * P].rearrange("p (f n) -> p f n", f=2), ACT.Copy).then_inc(ht_saved, 1)
                sc.wait_ge(y_banked, e + 1)
                reached(sc, y_out[u % 2], half * 16)
                actv(ys[u % 2][:, 0:512], banks[4][:, :], ACT.Copy).then_inc(ys_a, 1)

            save_rows(0)
            all_experts(sc, expert)

        @block.vector
        def _(dve):
            V = nc.vector

            def match(e, u):
                reached(dve, list_banked, e - 1)
                V.tensor_tensor(onehot[u % 2], slots.rearrange("p (o s) -> p o s", o=1).to_broadcast([P, NTILE, P]),
                                pos[:, :, bass.ds(e, 1)].to_broadcast([P, NTILE, P]), ALU.is_equal).then_inc(onehot_ready, 1)

            def keep_list(e, u):
                dve.wait_ge(list_banked, e + 1)
                V.tensor_scalar(lempty[:, u], banks[7][:, 0:2], 0.0, 1e5, ALU.is_equal, ALU.mult).then_inc(empty_ready, 1)
                V.tensor_copy(lgate[:, u], banks[7][:, 2:3])
                dve.wait_ge(empty_ready, e + 1)
                V.scalar_tensor_tensor(rows_i[:, u], banks[7][:, 0:2], -1.0, lempty[:, u], ALU.add, ALU.add).then_inc(list_ready, 1)

            def save_rows(e):
                dve.wait_ge(xt_banked, e + 1)
                V.tensor_copy(xgT[:, 4:8], banks[1][:, :].rearrange("p (k n) -> p k n", k=4)).then_inc(xt_saved_v, 1)

            def expert(e, half, u, last):
                if not last or u < 2:
                    match(e + 2, u)
                dve.wait_ge(sg_ready, e + 1)
                reached(dve, ht_banked, e)
                V.scalar_tensor_tensor(hid, sg, lgate[:, u], banks[2][:, DE:], ALU.mult, ALU.mult).then_inc(h_ready, 1)
                if not last or u < 3:
                    save_rows(e + 1)
                if not last or u < 2:
                    reached(dve, y_out[u % 2], half * 16)
                    keep_list(e + 2, (u + 2) % 4)
                dve.wait_ge(y_banked, e + 1)
                reached(dve, y_out[u % 2], half * 16)
                V.tensor_copy(ys[u % 2][:, 512:], banks[5][:, :]).then_inc(ys_v, 1)

            match(0, 0)
            keep_list(0, 0)
            match(1, 1)
            keep_list(1, 1)
            save_rows(0)
            all_experts(dve, expert)

        block_ctx.close()
        end_block()

        w_in = sem("w_in")
        xg_in = sem("xg_in")
        y_out = sem("y_out")
        pool_turns = sem("pool_turns")
        sp_turns = sem("sp_turns")
        dve_turns = sem("dve_turns")
        pos_moved = sem("pos_moved")
        onehot_ready = sem("onehot_ready")
        list_banked = sem("list_banked")
        empty_ready = sem("empty_ready")
        list_ready = sem("list_ready")
        xt_banked = sem("xt_banked")
        xt_saved = sem("xt_saved")
        gu_banked = sem("gu_banked")
        sg_ready = sem("sg_ready")
        h_ready = sem("h_ready")
        ht_banked = sem("ht_banked")
        ht_saved = sem("ht_saved")
        y_banked = sem("y_banked")
        ys_ready = sem("ys_ready")
        block_ctx = ExitStack()
        block = block_ctx.enter_context(nc.Block())
        PASSES = (NTOK + P - 1) // P - 1

        def for_each_expert(eng, expert, before=None):
            flag = eng.value_load(over_i[0:1, 0:1])
            with eng.If(flag > 0):
                with eng.Fori(0, PASSES) as r:
                    if before is not None:
                        before(r)
                    with eng.Fori(0, NE) as e:
                        expert(e, r * NE + e + 1)

        @block.sync
        def _(sp):
            def expert(e, n):
                one = bass.ds(e, 1)
                sp.dma_start(wgu[0][:, :, 0:DE], io["w_exp_gate"][0, one].rearrange("o (k p) n -> p (o k) n", p=P)).then_inc(w_in, 16)
                sp.dma_start(wgu[0][:, :, DE:], io["w_exp_up"][0, one].rearrange("o (k p) n -> p (o k) n", p=P)).then_inc(w_in, 16)
                sp.dma_start(wde[0], io["w_exp_down"][0, one].rearrange("o (k p) n -> p (o k) n", p=P)).then_inc(w_in, 16)
                sp.wait_ge(y_banked, n)
                sp.sem_inc(sp_turns, 1)

            for_each_expert(sp, expert)

        @block.gpsimd
        def _(pool):
            def expert(e, n):
                pool.wait_ge(list_ready, n)
                pool.sem_inc(pool_turns, 1)
                nc.gpsimd.indirect_dma_start(out=xg[0], out_offset=None, in_=x1_rows,
                                             in_offset=bass.IndirectOffsetOnAxis(ap=rows_i[:, 0, 0:1], axis=0),
                                             bounds_check=NTOK - 1, oob_is_err=False).then_inc(xg_in, 16)
                pool.wait_ge(ys_ready, n)
                pool.sem_inc(pool_turns, 1)
                nc.gpsimd.indirect_dma_start(out=y_rows, out_offset=bass.IndirectOffsetOnAxis(ap=rows_i[:, 0, 1:2], axis=0),
                                             in_=ys[0], in_offset=None,
                                             bounds_check=NTOK * TOP_K - 1, oob_is_err=False).then_inc(y_out, 16)
                pool.wait_ge(y_out, n * 16)
                pool.sem_inc(pool_turns, 1)

            for_each_expert(pool, expert)

        @block.tensor
        def _(pe):
            mm, tr = nc.tensor.matmul, nc.tensor.transpose

            def expert(e, n):
                pe.wait_ge(onehot_ready, n)
                for t in range(NTILE):
                    last = mm(banks[7][:, 0:3], onehot[0][:, t], R[:, t, :, bass.ds(e, 1)].rearrange("p c o -> p (c o)"),
                              start=(t == 0), stop=(t == NTILE - 1))
                last.then_inc(list_banked, 1)
                pe.wait_ge(xg_in, n * 16)
                for k in range(KD):
                    last = tr(banks[k // 4][:, k % 4 * P:(k % 4 + 1) * P], xg[0][:, k * P:(k + 1) * P], ident[:, :])
                last.then_inc(xt_banked, 1)
                pe.wait_ge(w_in, n * 48)
                pe.wait_ge(xt_saved, n)
                for k in range(KD):
                    last = mm(banks[2][:, :], xgT[:, k], wgu[0][:, k], start=(k == 0), stop=(k == KD - 1))
                last.then_inc(gu_banked, 1)
                pe.wait_ge(h_ready, n)
                for f in range(2):
                    last = tr(banks[3][:, f * P:(f + 1) * P], hid[:, f * P:(f + 1) * P], ident[:, :])
                last.then_inc(ht_banked, 1)
                pe.wait_ge(ht_saved, n)
                for half in range(2):
                    for f in range(2):
                        last = mm(banks[4 + half][:, :], hidT[:, f], wde[0][:, f, half * 512:half * 512 + 512], start=(f == 0), stop=(f == 1))
                last.then_inc(y_banked, 1)

            for_each_expert(pe, expert)

        @block.scalar
        def _(sc):
            actv = nc.scalar.activation

            def expert(e, n):
                sc.wait_ge(xt_banked, n)
                actv(xgT[:, 0:4], banks[0][:, :].rearrange("p (k n) -> p k n", k=4), ACT.Copy)
                actv(xgT[:, 4:8], banks[1][:, :].rearrange("p (k n) -> p k n", k=4), ACT.Copy).then_inc(xt_saved, 1)
                sc.wait_ge(gu_banked, n)
                actv(sg, banks[2][:, 0:DE], ACT.Silu).then_inc(sg_ready, 1)
                sc.wait_ge(ht_banked, n)
                actv(hidT, banks[3][:, 0:2 * P].rearrange("p (f n) -> p f n", f=2), ACT.Copy).then_inc(ht_saved, 1)

            for_each_expert(sc, expert)

        @block.vector
        def _(dve):
            V = nc.vector

            def next_slots(r):
                V.tensor_scalar(pos, pos, float(-P), None, ALU.add).then_inc(pos_moved, 1)
                dve.wait_ge(pos_moved, r + 1)
                dve.sem_inc(dve_turns, 1)

            def expert(e, n):
                V.tensor_tensor(onehot[0], slots.rearrange("p (o s) -> p o s", o=1).to_broadcast([P, NTILE, P]),
                                pos[:, :, bass.ds(e, 1)].to_broadcast([P, NTILE, P]), ALU.is_equal).then_inc(onehot_ready, 1)
                dve.wait_ge(list_banked, n)
                V.tensor_scalar(lempty[:, 0], banks[7][:, 0:2], 0.0, 1e5, ALU.is_equal, ALU.mult).then_inc(empty_ready, 1)
                V.tensor_copy(lgate[:, 0], banks[7][:, 2:3])
                dve.wait_ge(empty_ready, n)
                V.scalar_tensor_tensor(rows_i[:, 0], banks[7][:, 0:2], -1.0, lempty[:, 0], ALU.add, ALU.add).then_inc(list_ready, 1)
                dve.wait_ge(sg_ready, n)
                dve.wait_ge(list_ready, n)
                V.scalar_tensor_tensor(hid, sg, lgate[:, 0], banks[2][:, DE:], ALU.mult, ALU.mult).then_inc(h_ready, 1)
                dve.wait_ge(y_banked, n)
                V.tensor_copy(ys[0][:, 0:512], banks[4][:, :])
                V.tensor_copy(ys[0][:, 512:], banks[5][:, :]).then_inc(ys_ready, 1)
                dve.wait_ge(y_out, n * 16)
                dve.sem_inc(dve_turns, 1)

            for_each_expert(dve, expert, next_slots)

        block_ctx.close()
        end_block()

        dve_step = sem("dve_step")
        act_step = sem("act_step")
        var_ready = sem("var_ready")
        rstd_ready = sem("rstd_ready")
        out_ready = sem("out_ready")
        out_done = sem("out_done")
        y_in = [sem("y_in0"), sem("y_in1")]
        block_ctx = ExitStack()
        block = block_ctx.enter_context(nc.Block())
        y_view = y_rows.rearrange("(t k) d -> t k d", k=TOP_K)

        @block.sync
        def _(sp):
            def store(t):
                sp.wait_ge(out_ready, t + 1)
                dst = io["out0"][0, t * P:(t + 1) * P] if t < 4 else io["out1"].rearrange("b t d -> (b t) d")
                sp.dma_start(dst, x1[0:tok(t)[1], t]).then_inc(out_done, 16)

            for t in range(NTILE):
                t0, n = tok(t)
                if t >= 2:
                    store(t - 2)
                sp.dma_start(y6[t % 2][0:n], y_view[t0:t0 + n]).then_inc(y_in[t % 2], 16)
            store(3)
            store(4)
            sp.wait_ge(out_done, 16 * NTILE)

        @block.scalar
        def _(sc):
            actv = nc.scalar.activation
            step = Steps(sc, act_step)
            for t in range(NTILE):
                n = tok(t)[1]
                sc.wait_ge(var_ready, t + 1)
                step(actv(lnst[0:n, 2:3], lnst[0:n, 1:2], ACT.Ln, bias=eps[0:n, 1:2]))
                actv(lnst[0:n, 3:4], lnst[0:n, 2:3], ACT.Exp, scale=-0.5).then_inc(rstd_ready, 1)

        @block.vector
        def _(dve):
            step = Steps(dve, dve_step)
            V = nc.vector

            def norm(t, i, gain, done):
                n = tok(t)[1]
                for half in range(2):
                    step(V.bn_stats(bnst[0:n, half], x1[0:n, t, half * 512:half * 512 + 512]))
                step(V.bn_aggr(lnst[0:n, 0:2], bnst[0:n]), var_ready)
                dve.wait_ge(rstd_ready, i + 1)
                step(V.tensor_scalar(x1[0:n, t], x1[0:n, t], lnst[0:n, 0:1], lnst[0:n, 3:4], ALU.subtract, ALU.mult))
                step(V.tensor_tensor(x1[0:n, t], x1[0:n, t], lnw[0:n, gain], ALU.mult))
                step(V.tensor_tensor(x1[0:n, t], x1[0:n, t], lnw[0:n, gain + 1], ALU.add), done)

            for t in range(NTILE):
                n = tok(t)[1]
                y = y6[t % 2]
                dve.wait_ge(y_in[t % 2], 16 * (t // 2 + 1))
                step(V.tensor_tensor(y[0:n, 0:3], y[0:n, 0:3], y[0:n, 3:6], ALU.add))
                for k in range(3):
                    step(V.tensor_tensor(x1[0:n, t], x1[0:n, t], y[0:n, k], ALU.add))
                norm(t, t, 2, out_ready)

        block_ctx.close()


INS = ["x_prompt", "x_sample", "cache_cmp_kv", "cache_slc_kv", "cache_win_kv", "state_delta_S", "state_delta_conv",
       "page_table", "w_in", "dn_conv_w", "dn_A_log", "dn_dt_bias", "dn_norm_w", "nsa_cmp_w1", "nsa_cmp_pos", "nsa_cmp_w2",
       "w_out", "ln1_g", "ln1_b", "w_router", "b_router", "w_exp_gate", "w_exp_up", "w_exp_down",
       "w_sh_gate", "w_sh_up", "w_sh_down", "ln2_g", "ln2_b"]
KV = (2, KVH, HD)
OUTS = [(1, NP_TOK, D), (NB, NT, D),
        (1, 1, NP_TOK) + KV, (1, 1, NP_TOK) + KV, (1, 1, WIN) + KV, (1, 1, H, DH, DH), (1, 1, 3, CH),
        (1, NB, NT) + KV, (1, NB, NT) + KV, (1, NB, WIN) + KV, (1, NB, H, DH, DH), (1, NB, 3, CH)]


def kernel(**inputs):
    import concourse.bacc as bacc
    from concourse.bass_utils import run_bass_kernel_spmd

    nc = bacc.Bacc("TRN2", target_bir_lowering=False, num_devices=1)
    arrays, io = {}, {}
    named = {n: np.ascontiguousarray(inputs[n]) for n in INS}
    named.update(shape_constants())
    for name, v in named.items():
        arrays[f"in_{name}"] = v
        io[name] = nc.dram_tensor(f"in_{name}", v.shape, mybir.dt.from_np(v.dtype), kind="ExternalInput").ap()
    for i, shape in enumerate(OUTS):
        io[f"out{i}"] = nc.dram_tensor(f"out_{i}", shape, mybir.dt.float32, kind="ExternalOutput").ap()
    build(nc, io)
    r = run_bass_kernel_spmd(nc, [arrays], core_ids=[0])
    return tuple(r.results[0][f"out_{i}"] for i in range(len(OUTS)))
```
